# Optimizing a Trainium2 kernel written in Bass

```python
import jax
import jax.numpy as jnp
from jax import lax
import numpy as np
import jax, jax.numpy as jnp

D_MODEL = 1024
BATCH = 1
SEQ = 512
DEPTH = 2

GRID_W = 64
CTX_LEN = 256
N_MOD = 9
D_FF = 2816
RMS_EPS = 1e-6
A_HEADS = 8
A_KV_HEADS = 2
A_HEAD_DIM = 64
WINDOW = 128
BLOCK = WINDOW
ROPE_BASE = 10000.0
B_HEADS = 4
B_DK = 64
B_DV = 128
B_GATE_RANK = 16
B_GATE_NORM = 16.0
B_CHUNK = 64
POOL_WINDOWS = (2, 4, 8, 16)
POOL_GROUP = D_MODEL // len(POOL_WINDOWS)
A_Q = A_HEADS * A_HEAD_DIM
A_KV = A_KV_HEADS * A_HEAD_DIM
B_QK = B_HEADS * B_DK
B_V = B_HEADS * B_DV
PROJ_SIZES = (A_Q, A_KV, A_KV, B_QK, B_QK, B_V, B_V, 2 * B_GATE_RANK)
PROJ_DIM = A_Q + 2 * A_KV + 2 * B_QK + 2 * B_V + 2 * B_GATE_RANK
MIX_OUT = A_Q + B_V


def rmsnorm(x, g):
    x32 = x.astype(jnp.float32)
    y = x32 * lax.rsqrt(jnp.mean(x32 * x32, axis=-1, keepdims=True) + RMS_EPS)
    return y.astype(x.dtype) * g

def adaln(cond, w, b):
    mm = jax.nn.silu(cond) @ w + b
    mm = mm.reshape(mm.shape[:-1] + (N_MOD, mm.shape[-1] // N_MOD))
    return [mm[..., i, None, :] for i in range(N_MOD)]

def modulate(z, g, shift, scale):
    return rmsnorm(z, g) * (1.0 + scale) + shift

def swiglu(h, wi, wo):
    a, u = jnp.split(h @ wi, 2, axis=-1)
    return (jax.nn.silu(a) * u) @ wo

def _rotate(x, pos):
    n = x.shape[-1] // 2
    freqs = ROPE_BASE ** (-jnp.arange(n, dtype=jnp.float32) / n)
    ang = pos[:, None] * freqs
    cos = jnp.cos(ang)[:, None, :].astype(x.dtype)
    sin = jnp.sin(ang)[:, None, :].astype(x.dtype)
    x1, x2 = x[..., :n], x[..., n:]
    return jnp.concatenate([x1 * cos - x2 * sin, x2 * cos + x1 * sin], axis=-1)

def axial_rope(x, rows, cols):
    half = x.shape[-1] // 2
    return jnp.concatenate([_rotate(x[..., :half], rows), _rotate(x[..., half:], cols)], axis=-1)

def window_attention(q, k, v, kc, vc, sink):
    B, T, Hq, d = q.shape
    G = k.shape[2]
    R = Hq // G
    nb = T // BLOCK
    L = kc.shape[1]
    scale = d ** -0.5
    qb = q.reshape(B, nb, BLOCK, G, R, d)

    def band(a):
        ap = jnp.pad(a, ((0, 0), (BLOCK, BLOCK), (0, 0), (0, 0))).reshape(B, nb + 2, BLOCK, G, d)
        return jnp.concatenate([ap[:, :nb], ap[:, 1:nb + 1], ap[:, 2:]], axis=2)

    kb, vb = band(k), band(v)
    s_band = jnp.einsum('bnigrd,bnjgd->bgrnij', qb, kb).astype(jnp.float32) * scale
    s_ctx = jnp.einsum('bnigrd,blgd->bgrnil', qb, kc).astype(jnp.float32) * scale
    qpos = jnp.arange(nb)[:, None, None] * BLOCK + jnp.arange(BLOCK)[None, :, None]
    kpos = jnp.arange(nb)[:, None, None] * BLOCK - BLOCK + jnp.arange(3 * BLOCK)[None, None, :]
    valid = (kpos >= 0) & (kpos < T) & (jnp.abs(kpos - qpos) <= WINDOW)
    s_band = jnp.where(valid, s_band, -jnp.inf)
    sink_l = jnp.broadcast_to(sink.astype(jnp.float32).reshape(1, G, R, 1, 1, 1), s_band.shape[:-1] + (1,))
    p = jax.nn.softmax(jnp.concatenate([s_band, s_ctx, sink_l], axis=-1), axis=-1)
    nk = 3 * BLOCK
    o = (jnp.einsum('bgrnij,bnjgd->bnigrd', p[..., :nk].astype(vb.dtype), vb)
         + jnp.einsum('bgrnil,blgd->bnigrd', p[..., nk:nk + L].astype(vc.dtype), vc))
    return o.reshape(B, T, Hq * d)

def context_attention(qc, kc, vc, sink):
    B, L, Hq, d = qc.shape
    G = kc.shape[2]
    R = Hq // G
    s = jnp.einsum('blgrd,bmgd->bgrlm', qc.reshape(B, L, G, R, d), kc).astype(jnp.float32) * d ** -0.5
    sink_l = jnp.broadcast_to(sink.astype(jnp.float32).reshape(1, G, R, 1, 1), s.shape[:-1] + (1,))
    p = jax.nn.softmax(jnp.concatenate([s, sink_l], axis=-1), axis=-1)
    o = jnp.einsum('bgrlm,bmgd->blgrd', p[..., :L].astype(vc.dtype), vc)
    return o.reshape(B, L, Hq * d)

def gla_chunked(q, k, v, log_a, s0):
    B, T, H, dk = q.shape
    C = B_CHUNK
    n = T // C
    f32 = jnp.float32

    def chunks(a):
        return a.astype(f32).reshape(B, n, C, H, a.shape[-1])

    qc_ = chunks(q) * dk ** -0.5
    kc_ = chunks(k)
    vc_ = chunks(v)
    g = jnp.cumsum(chunks(log_a), axis=2)
    g_last = g[:, :, -1:]
    q_t = qc_ * jnp.exp(g)
    k_t = kc_ * jnp.exp(-g)
    k_end = kc_ * jnp.exp(g_last - g)
    lower = jnp.tril(jnp.ones((C, C), dtype=bool))
    att = jnp.where(lower, jnp.einsum('bnihd,bnjhd->bnhij', q_t, k_t), 0.0)
    o = jnp.einsum('bnhij,bnjhv->bnihv', att, vc_)
    d_state = jnp.einsum('bnjhd,bnjhv->bnhdv', k_end, vc_)
    decay = jnp.exp(g_last[:, :, 0])

    def step(S, inp):
        dec, ds = inp
        return dec[..., None] * S + ds, S

    s_final, s_prev = lax.scan(step, s0, (jnp.moveaxis(decay, 1, 0), jnp.moveaxis(d_state, 1, 0)))
    s_prev = jnp.moveaxis(s_prev, 0, 1)
    o = o + jnp.einsum('bnihd,bnhdv->bnihv', q_t, s_prev)
    return o.reshape(B, T, H, v.shape[-1]).astype(q.dtype), s_final

def bidir_gla(q, k, v, la_f, la_b, qc, kc, vc, lac_f, lac_b):
    flip = lambda a: a[:, ::-1]
    B = q.shape[0]
    zeros = jnp.zeros((B, B_HEADS, B_DK, B_DV), jnp.float32)
    oc_f, sc_f = gla_chunked(qc, kc, vc, lac_f, zeros)
    oc_b, sc_b = gla_chunked(flip(qc), flip(kc), flip(vc), flip(lac_b), zeros)
    o_f, _ = gla_chunked(q, k, v, la_f, sc_f)
    o_b, _ = gla_chunked(flip(q), flip(k), flip(v), flip(la_b), sc_b)
    return o_f + flip(o_b), oc_f + flip(oc_b)

def gla_output(o, r, gla_g):
    B, T = o.shape[:2]
    return rmsnorm(o, gla_g).reshape(B, T, B_V) * jax.nn.silu(r)

def mixer_ab(h, hc, rows, cols, need_ctx_out, w_in, w_a2_f, b_a_f, w_a2_b, b_a_b, sink, gla_g, w_out):
    split_points = [int(s) for s in np.cumsum(PROJ_SIZES)[:-1]]

    def project(z):
        Bz, Tz = z.shape[:2]
        qa, ka, va, qb, kb, vb, rb, zg = jnp.split(z @ w_in, split_points, axis=-1)
        la_f = jax.nn.log_sigmoid((zg[..., :B_GATE_RANK] @ w_a2_f + b_a_f).astype(jnp.float32)) / B_GATE_NORM
        la_b = jax.nn.log_sigmoid((zg[..., B_GATE_RANK:] @ w_a2_b + b_a_b).astype(jnp.float32)) / B_GATE_NORM
        return (qa.reshape(Bz, Tz, A_HEADS, A_HEAD_DIM),
                ka.reshape(Bz, Tz, A_KV_HEADS, A_HEAD_DIM),
                va.reshape(Bz, Tz, A_KV_HEADS, A_HEAD_DIM),
                qb.reshape(Bz, Tz, B_HEADS, B_DK),
                kb.reshape(Bz, Tz, B_HEADS, B_DK),
                vb.reshape(Bz, Tz, B_HEADS, B_DV),
                rb,
                la_f.reshape(Bz, Tz, B_HEADS, B_DK),
                la_b.reshape(Bz, Tz, B_HEADS, B_DK))

    qa, ka, va, qb, kb, vb, rb, la_f, la_b = project(h)
    cqa, cka, cva, cqb, ckb, cvb, crb, cla_f, cla_b = project(hc)
    o_a = window_attention(axial_rope(qa, rows, cols), axial_rope(ka, rows, cols), va, cka, cva, sink)
    o_b, oc_b = bidir_gla(qb, kb, vb, la_f, la_b, cqb, ckb, cvb, cla_f, cla_b)
    y = jnp.concatenate([o_a, gla_output(o_b, rb, gla_g)], axis=-1) @ w_out
    yc = None
    if need_ctx_out:
        oc_a = context_attention(cqa, cka, cva, sink)
        yc = jnp.concatenate([oc_a, gla_output(oc_b, crb, gla_g)], axis=-1) @ w_out
    return y, yc

def pool_mixer(h, w_pool, pool_scale):
    B, T, D = h.shape
    ng = len(POOL_WINDOWS)
    hg = h.astype(jnp.float32).reshape(B, T, ng, POOL_GROUP)
    prefix = jnp.pad(jnp.cumsum(hg, axis=1), ((0, 0), (1, 0), (0, 0), (0, 0)))
    t = jnp.arange(T)
    means = []
    for gi, w in enumerate(POOL_WINDOWS):
        lo = jnp.maximum(t - w // 2, 0)
        hi = jnp.minimum(t + (w - w // 2), T)
        total = prefix[:, hi, gi] - prefix[:, lo, gi]
        means.append(total / (hi - lo).astype(jnp.float32)[:, None])
    pooled = (jnp.stack(means, axis=2) - hg).astype(h.dtype)
    y = jnp.einsum('btgc,gce->btge', pooled, w_pool)
    return y.reshape(B, T, D) * pool_scale

def first_inputs(seed: int = 0) -> dict:
    key = jax.random.key(seed)
    ks = jax.random.split(key, 24)
    D = D_MODEL
    ne = (DEPTH + 1) // 2
    no = DEPTH // 2

    def nrm(k, shape, scale=1.0):
        return jax.random.normal(k, shape, jnp.float32) * scale

    return {
        "x": nrm(ks[0], (BATCH, SEQ, D)),
        "c": nrm(ks[1], (BATCH, D)),
        "ctx": nrm(ks[2], (BATCH, CTX_LEN, D)),
        "c_ctx": nrm(ks[3], (D,)),
        "w_mod": nrm(ks[4], (DEPTH, D, N_MOD * D), 0.5 * D ** -0.5),
        "b_mod": nrm(ks[5], (DEPTH, N_MOD * D), 0.01),
        "norm_g": 1.0 + nrm(ks[6], (DEPTH, 3, D), 0.05),
        "ffn1_wi": nrm(ks[7], (DEPTH, D, 2 * D_FF), D ** -0.5),
        "ffn1_wo": nrm(ks[8], (DEPTH, D_FF, D), D_FF ** -0.5),
        "ffn2_wi": nrm(ks[9], (DEPTH, D, 2 * D_FF), D ** -0.5),
        "ffn2_wo": nrm(ks[10], (DEPTH, D_FF, D), D_FF ** -0.5),
        "w_in": nrm(ks[11], (ne, D, PROJ_DIM), D ** -0.5),
        "w_a2_f": nrm(ks[12], (ne, B_GATE_RANK, B_QK), B_GATE_RANK ** -0.5),
        "b_a_f": nrm(ks[13], (ne, B_QK), 0.1),
        "w_a2_b": nrm(ks[14], (ne, B_GATE_RANK, B_QK), B_GATE_RANK ** -0.5),
        "b_a_b": nrm(ks[15], (ne, B_QK), 0.1),
        "sink": nrm(ks[16], (ne, A_HEADS), 1.0),
        "gla_g": 1.0 + nrm(ks[17], (ne, B_DV), 0.05),
        "w_out": nrm(ks[18], (ne, MIX_OUT, D), MIX_OUT ** -0.5),
        "w_pool": nrm(ks[19], (no, len(POOL_WINDOWS), POOL_GROUP, POOL_GROUP), POOL_GROUP ** -0.5),
        "pool_scale": 1.0 + nrm(ks[20], (no, D), 0.1),
        "final_g": 1.0 + nrm(ks[21], (D,), 0.05),
    }

def first_block(x, c, ctx, c_ctx, w_mod, b_mod, norm_g, ffn1_wi, ffn1_wo, ffn2_wi, ffn2_wo,
              w_in, w_a2_f, b_a_f, w_a2_b, b_a_b, sink, gla_g, w_out, w_pool, pool_scale, final_g):
    T = x.shape[1]
    ROWS = T // GRID_W
    rows = jnp.repeat(jnp.arange(ROWS, dtype=jnp.float32), GRID_W)
    cols = jnp.tile(jnp.arange(GRID_W, dtype=jnp.float32), ROWS)

    for l in range(DEPTH):
        even = l % 2 == 0
        ctx_out = any(j % 2 == 0 for j in range(l + 1, DEPTH))
        ctx_in = even or ctx_out
        m = adaln(c, w_mod[l], b_mod[l])
        mc = adaln(c_ctx, w_mod[l], b_mod[l]) if ctx_in else None

        x = x + 0.5 * m[2] * swiglu(modulate(x, norm_g[l, 0], m[0], m[1]), ffn1_wi[l], ffn1_wo[l])
        if ctx_in:
            ctx = ctx + 0.5 * mc[2] * swiglu(modulate(ctx, norm_g[l, 0], mc[0], mc[1]), ffn1_wi[l], ffn1_wo[l])

        h = modulate(x, norm_g[l, 1], m[3], m[4])
        if even:
            e = l // 2
            hc = modulate(ctx, norm_g[l, 1], mc[3], mc[4])
            y, yc = mixer_ab(h, hc, rows, cols, ctx_out, w_in[e], w_a2_f[e], b_a_f[e], w_a2_b[e], b_a_b[e],
                             sink[e], gla_g[e], w_out[e])
        else:
            o = l // 2
            y = pool_mixer(h, w_pool[o], pool_scale[o])
            yc = pool_mixer(modulate(ctx, norm_g[l, 1], mc[3], mc[4]), w_pool[o], pool_scale[o]) if ctx_out else None
        x = x + m[5] * y
        if ctx_out:
            ctx = ctx + mc[5] * yc

        x = x + 0.5 * m[8] * swiglu(modulate(x, norm_g[l, 2], m[6], m[7]), ffn2_wi[l], ffn2_wo[l])
        if ctx_out:
            ctx = ctx + 0.5 * mc[8] * swiglu(modulate(ctx, norm_g[l, 2], mc[6], mc[7]), ffn2_wi[l], ffn2_wo[l])

    return rmsnorm(x, final_g)


DEPTH_2 = 1

M_HEADS = 4
M_V_DIM = 128
M_QK_DIM = 64
M_CHUNK = 64
WINDOWS = (128, 512, 2048)
DILATIONS = (1, 4, 16)
ROT_DIM = A_HEAD_DIM // 4
ROPE_THETA = 500000.0
MIX_WIDTH = M_HEADS * M_V_DIM + A_HEADS * A_HEAD_DIM
IN_SPLITS = (M_HEADS * M_QK_DIM, M_HEADS * M_QK_DIM, M_HEADS * M_V_DIM, M_HEADS * M_V_DIM,
             4 * M_HEADS, A_HEADS * A_HEAD_DIM, A_HEADS * A_HEAD_DIM, A_HEADS * A_HEAD_DIM)
IN_COLS = sum(IN_SPLITS)
HALF_STEP = 0.5
EPS = 1e-6
NEG_INF = -1e30


def rms_norm(x, g):
    xf = x.astype(jnp.float32)
    y = xf * lax.rsqrt(jnp.mean(xf * xf, axis=-1, keepdims=True) + EPS)
    return (y * g.astype(jnp.float32)).astype(x.dtype)

def modulate_2(h, shift, scale):
    return h * (1.0 + scale) + shift

def swiglu_2(h, w_gu, w_down):
    g, u = jnp.split(h @ w_gu, 2, axis=-1)
    return (jax.nn.silu(g) * u) @ w_down

def partial_rope(t, pos):
    half = ROT_DIM // 2
    inv_freq = ROPE_THETA ** (-2.0 * jnp.arange(half, dtype=jnp.float32) / ROT_DIM)
    ang = pos.astype(jnp.float32)[:, None] * inv_freq[None, :]
    cos, sin = jnp.cos(ang), jnp.sin(ang)
    t1, t2 = t[..., :half], t[..., half:ROT_DIM]
    return jnp.concatenate([t1 * cos - t2 * sin, t2 * cos + t1 * sin, t[..., ROT_DIM:]], axis=-1)

def mlstm_scan(q, k, v, log_i, log_f):
    B, H, S, Dk = q.shape
    Dv = v.shape[-1]
    lc = min(M_CHUNK, S)
    nc = S // lc

    def chunks(t):
        return jnp.moveaxis(t.reshape((B, H, nc, lc) + t.shape[3:]), 2, 0)

    xs = (chunks(q), chunks(k), chunks(v), chunks(log_i), chunks(log_f))
    tril = jnp.tril(jnp.ones((lc, lc), dtype=bool))

    def step(carry, inp):
        C, n, m = carry
        q_c, k_c, v_c, li, lf = inp
        b = jnp.cumsum(lf, axis=-1)
        a_inter = b + m[..., None]
        d = jnp.where(tril, b[..., :, None] - b[..., None, :] + li[..., None, :], NEG_INF)
        m_t = jnp.maximum(a_inter, jnp.max(d, axis=-1))
        w_inter = jnp.exp(a_inter - m_t)
        s = jnp.exp(d - m_t[..., None]) * jnp.einsum('bhtd,bhsd->bhts', q_c, k_c)
        num = (w_inter[..., None] * jnp.einsum('bhvd,bhtd->bhtv', C, q_c)
               + jnp.einsum('bhts,bhsv->bhtv', s, v_c))
        den = w_inter * jnp.einsum('bhd,bhtd->bht', n, q_c) + jnp.sum(s, axis=-1)
        h = num / jnp.maximum(jnp.abs(den), jnp.exp(-m_t))[..., None]
        b_end = b[..., -1]
        g = b_end[..., None] - b + li
        m_new = jnp.maximum(b_end + m, jnp.max(g, axis=-1))
        decay = jnp.exp(b_end + m - m_new)
        wg = jnp.exp(g - m_new[..., None])
        C_new = decay[..., None, None] * C + jnp.einsum('bhs,bhsv,bhsd->bhvd', wg, v_c, k_c)
        n_new = decay[..., None] * n + jnp.einsum('bhs,bhsd->bhd', wg, k_c)
        return (C_new, n_new, m_new), h

    init = (jnp.zeros((B, H, Dv, Dk), jnp.float32), jnp.zeros((B, H, Dk), jnp.float32),
            jnp.full((B, H), NEG_INF, jnp.float32))
    _, hs = lax.scan(step, init, xs)
    return jnp.moveaxis(hs, 0, 2).reshape(B, H, S, Dv)

def bidirectional_mlstm(q, k, v, li_f, lf_f, li_b, lf_b):
    h_fwd = mlstm_scan(q, k, v, li_f, lf_f)
    flip = lambda t: jnp.flip(t, axis=2)
    h_bwd = flip(mlstm_scan(flip(q), flip(k), flip(v), flip(li_b), flip(lf_b)))
    return h_fwd + h_bwd

def dilated_band_attention(q, k, v, dilation, n_side):
    B, H, S, Dh = q.shape
    L = S // dilation

    def to_sub(t):
        return t.reshape(B, H, L, dilation, Dh).transpose(0, 1, 3, 2, 4)

    blk = n_side
    nb = -(-L // blk)
    lp = nb * blk
    qs = jnp.pad(to_sub(q), ((0, 0),) * 3 + ((0, lp - L), (0, 0)))
    kpad = ((0, 0),) * 3 + ((n_side, lp - L + n_side), (0, 0))
    ks = jnp.pad(to_sub(k), kpad)
    vs = jnp.pad(to_sub(v), kpad)
    qb = qs.reshape(B, H, dilation, nb, blk, Dh)

    def windows(t):
        tb = t.reshape(B, H, dilation, nb + 2, blk, Dh)
        return jnp.concatenate([tb[:, :, :, :-2], tb[:, :, :, 1:-1], tb[:, :, :, 2:]], axis=4)

    kw, vw = windows(ks), windows(vs)
    s = jnp.einsum('bhrnqe,bhrnke->bhrnqk', qb, kw)
    qi = jnp.arange(blk)[:, None]
    kk = jnp.arange(3 * blk)[None, :]
    band = jnp.abs(kk - n_side - qi) <= n_side
    key_idx = jnp.arange(nb)[:, None] * blk + kk - n_side
    in_range = (key_idx >= 0) & (key_idx < L)
    mask = band[None, :, :] & in_range[:, None, :]
    s = jnp.where(mask, s, NEG_INF)
    m = jnp.max(s, axis=-1, keepdims=True)
    p = jnp.exp(s - m)
    den = jnp.sum(p, axis=-1)
    o = jnp.einsum('bhrnqk,bhrnke->bhrnqe', p, vw) / den[..., None]
    lse = m[..., 0] + jnp.log(den)
    o = o.reshape(B, H, dilation, lp, Dh)[:, :, :, :L].transpose(0, 1, 3, 2, 4).reshape(B, H, S, Dh)
    lse = lse.reshape(B, H, dilation, lp)[..., :L].transpose(0, 1, 3, 2).reshape(B, H, S)
    return o, lse

def dilated_attention(q, k, v):
    outs, lses = [], []
    for w, d in zip(WINDOWS, DILATIONS):
        o, l = dilated_band_attention(q, k, v, d, w // (2 * d))
        outs.append(o)
        lses.append(l)
    wts = jax.nn.softmax(jnp.stack(lses), axis=0)
    return jnp.sum(wts[..., None] * jnp.stack(outs), axis=0)

def hybrid_mixer(h, w_in, gate_bias, g_q, g_k, g_mh, w_out):
    B, S, _ = h.shape
    proj = (h @ w_in).astype(jnp.float32)
    idx, acc = [], 0
    for n_cols in IN_SPLITS[:-1]:
        acc += n_cols
        idx.append(acc)
    mq, mk, mv, mo, mg, aq, ak, av = jnp.split(proj, idx, axis=-1)

    def heads(t, n):
        return t.reshape(B, S, n, -1).transpose(0, 2, 1, 3)

    gates = mg.reshape(B, S, 4, M_HEADS).transpose(2, 0, 3, 1) + gate_bias.astype(jnp.float32)[:, None, :, None]
    hm = bidirectional_mlstm(heads(mq, M_HEADS), heads(mk, M_HEADS) * (M_QK_DIM ** -0.5), heads(mv, M_HEADS),
                             gates[0], jax.nn.log_sigmoid(gates[1]), gates[2], jax.nn.log_sigmoid(gates[3]))
    hm = rms_norm(hm.transpose(0, 2, 1, 3), g_mh.reshape(M_HEADS, M_V_DIM))
    hm = (hm * jax.nn.sigmoid(mo.reshape(B, S, M_HEADS, M_V_DIM))).reshape(B, S, M_HEADS * M_V_DIM)

    pos = jnp.arange(S)
    qa = partial_rope(rms_norm(heads(aq, A_HEADS), g_q), pos) * (A_HEAD_DIM ** -0.5)
    ka = partial_rope(rms_norm(heads(ak, A_HEADS), g_k), pos)
    ha = dilated_attention(qa, ka, heads(av, A_HEADS))
    ha = ha.transpose(0, 2, 1, 3).reshape(B, S, A_HEADS * A_HEAD_DIM)

    return jnp.concatenate([hm, ha], axis=-1).astype(h.dtype) @ w_out

def second_inputs(seed: int = 0) -> dict:
    key = jax.random.key(seed)
    ks = jax.random.split(key, 20)
    f32 = jnp.float32

    def nrm(k, shape, scale):
        return jax.random.normal(k, shape, f32) * scale

    gate_bias = (nrm(ks[9], (DEPTH_2, 4, M_HEADS), 0.1)
                 + jnp.array([0.0, 1.0, 0.0, 1.0], f32)[None, :, None]
                 * jnp.linspace(3.0, 6.0, M_HEADS, dtype=f32)[None, None, :])
    return {
        'x': nrm(ks[0], (BATCH, SEQ, D_MODEL), 1.0),
        'c': nrm(ks[1], (BATCH, D_MODEL), 1.0),
        'w_ada': nrm(ks[2], (DEPTH_2, D_MODEL, N_MOD * D_MODEL), 0.5 * D_MODEL ** -0.5),
        'b_ada': nrm(ks[3], (DEPTH_2, N_MOD * D_MODEL), 0.02),
        'g_ffn1': 1.0 + nrm(ks[4], (DEPTH_2, D_MODEL), 0.02),
        'w_gu1': nrm(ks[5], (DEPTH_2, D_MODEL, 2 * D_FF), D_MODEL ** -0.5),
        'w_down1': nrm(ks[6], (DEPTH_2, D_FF, D_MODEL), D_FF ** -0.5),
        'g_mix': 1.0 + nrm(ks[7], (DEPTH_2, D_MODEL), 0.02),
        'w_in': nrm(ks[8], (DEPTH_2, D_MODEL, IN_COLS), D_MODEL ** -0.5),
        'gate_bias': gate_bias,
        'g_q': 1.0 + nrm(ks[10], (DEPTH_2, A_HEAD_DIM), 0.02),
        'g_k': 1.0 + nrm(ks[11], (DEPTH_2, A_HEAD_DIM), 0.02),
        'g_mh': 1.0 + nrm(ks[12], (DEPTH_2, M_HEADS * M_V_DIM), 0.02),
        'w_out': nrm(ks[13], (DEPTH_2, MIX_WIDTH, D_MODEL), MIX_WIDTH ** -0.5),
        'g_ffn2': 1.0 + nrm(ks[14], (DEPTH_2, D_MODEL), 0.02),
        'w_gu2': nrm(ks[15], (DEPTH_2, D_MODEL, 2 * D_FF), D_MODEL ** -0.5),
        'w_down2': nrm(ks[16], (DEPTH_2, D_FF, D_MODEL), D_FF ** -0.5),
        'g_final': 1.0 + nrm(ks[17], (DEPTH_2, D_MODEL), 0.02),
    }

def second_block(x, c, w_ada, b_ada, g_ffn1, w_gu1, w_down1, g_mix, w_in, gate_bias, g_q, g_k, g_mh,
              w_out, g_ffn2, w_gu2, w_down2, g_final):
    B, S, D = x.shape
    cs = jax.nn.silu(c)
    for l in range(DEPTH_2):
        mod = (cs @ w_ada[l] + b_ada[l]).reshape(B, N_MOD, D)[:, :, None, :]
        sh1, sc1, gt1, sh2, sc2, gt2, sh3, sc3, gt3 = [mod[:, i] for i in range(N_MOD)]
        h = modulate_2(rms_norm(x, g_ffn1[l]), sh1, sc1)
        x = x + HALF_STEP * gt1 * swiglu_2(h, w_gu1[l], w_down1[l])
        h = modulate_2(rms_norm(x, g_mix[l]), sh2, sc2)
        x = x + gt2 * hybrid_mixer(h, w_in[l], gate_bias[l], g_q[l], g_k[l], g_mh[l], w_out[l])
        h = modulate_2(rms_norm(x, g_ffn2[l]), sh3, sc3)
        x = x + HALF_STEP * gt3 * swiglu_2(h, w_gu2[l], w_down2[l])
        x = rms_norm(x, g_final[l])
    return x


def setup_inputs(seed=0):
    out = dict(first_inputs(seed))
    for name, value in second_inputs(seed + 1).items():
        if name != "x":
            out[name + "_2"] = value
    return out


def reference(
    x, c, ctx, c_ctx, w_mod, b_mod, norm_g, ffn1_wi, ffn1_wo, ffn2_wi, ffn2_wo, w_in, w_a2_f,
    b_a_f, w_a2_b, b_a_b, sink, gla_g, w_out, w_pool, pool_scale, final_g, c_2, w_ada_2,
    b_ada_2, g_ffn1_2, w_gu1_2, w_down1_2, g_mix_2, w_in_2, gate_bias_2, g_q_2, g_k_2, g_mh_2,
    w_out_2, g_ffn2_2, w_gu2_2, w_down2_2, g_final_2,
):
    x = first_block(
        x, c, ctx, c_ctx, w_mod, b_mod, norm_g, ffn1_wi, ffn1_wo, ffn2_wi, ffn2_wo, w_in,
        w_a2_f, b_a_f, w_a2_b, b_a_b, sink, gla_g, w_out, w_pool, pool_scale, final_g,
    )
    return second_block(
        x, c_2, w_ada_2, b_ada_2, g_ffn1_2, w_gu1_2, w_down1_2, g_mix_2, w_in_2, gate_bias_2,
        g_q_2, g_k_2, g_mh_2, w_out_2, g_ffn2_2, w_gu2_2, w_down2_2, g_final_2,
    )


_drawn_inputs = setup_inputs


def setup_inputs(seed=0):
    import zlib

    import numpy as np

    out = dict(_drawn_inputs(seed))
    spreads = {}
    factors = {'b_mod': 3.782,
     'w_a2_f': 4.567,
     'b_a_f': 8.0,
     'w_a2_b': 3.524,
     'b_a_b': 8.0,
     'sink': 8.0,
     'gla_g': 7.691,
     'b_ada_2': 2.859,
     'g_ffn1_2': 8.0,
     'g_mix_2': 8.0,
     'g_q_2': 8.0,
     'g_k_2': 8.0,
     'g_mh_2': 64.0,
     'g_ffn2_2': 23.354,
     'g_final_2': 8.437}
    for name, (base, spread) in spreads.items():
        noise = np.random.default_rng([zlib.crc32(name.encode()), seed]).standard_normal(out[name].shape)
        drawn = base * np.exp(spread * noise) if base else spread * noise
        out[name] = jnp.asarray(drawn.astype(out[name].dtype))
    for name, factor in factors.items():
        out[name] = (out[name] * factor).astype(out[name].dtype)
    return out
```

```python
from contextlib import ExitStack

import numpy as np

import concourse.bass as bass
from concourse import mybir

F32 = mybir.dt.float32
F32R = mybir.dt.float32r
BF16 = mybir.dt.bfloat16
I32 = mybir.dt.int32
ALU = mybir.AluOpType
ACT = mybir.ActivationFunctionType
AXX = mybir.AxisListType.X

D = 1024
T = 512
TC = 256
FF = 2816
NF = FF // 128
NRAW = 8
EPS = 1e-6
BIG = 1e30

VEC = [("b_mod", 144), ("norm_g", 48), ("pool_scale", 8), ("final_g", 8), ("gla_g", 1),
       ("c", 8), ("c_ctx", 8), ("b_a_f", 2), ("b_a_b", 2), ("c_2", 8), ("b_ada_2", 72),
       ("g_ffn1_2", 8), ("g_mix_2", 8), ("g_ffn2_2", 8), ("g_final_2", 8), ("g_mh_2", 4),
       ("g_q_2", 1), ("g_k_2", 1), ("gate_bias_2", 4), ("sink", 1)]
VOFF = {}
_o = 0
for _n, _c in VEC:
    VOFF[_n] = _o
    _o += _c
NV = _o

AQ, AK, AV, GQ, GK, GV, GR, GZ = 0, 4, 5, 6, 8, 10, 14, 18
NIN1 = 19
MQ, MK, MV, MO, MG, DQ, DK, DV = 0, 2, 4, 8, 12, 13, 17, 21
NIN2 = 25


class Queue:

    def __init__(self, sem):
        self.sem, self.n, self.items = sem, 0, []

    def put(self, fn, *after):
        self.items.append([fn, after, None])

    def do(self, fn, *after):
        self.items.append([fn, after, (self.sem, 1)])
        self.n += 1
        return (self.sem, self.n)

    def tt(self, o, x, y, op, *after):
        return self.do(lambda e: e.tensor_tensor(o, x, y, op), *after)

    def stt(self, o, x, s, y, op0, op1, *after, acc=None):
        return self.do(lambda e: e.scalar_tensor_tensor(o, x, s, y, op0, op1, accum_out=acc) if acc is not None
                       else e.scalar_tensor_tensor(o, x, s, y, op0, op1), *after)

    def ts(self, o, x, s1, s2, op0, op1, *after):
        return self.do(lambda e: e.tensor_scalar(o, x, s1, s2, op0, op1) if op1 is not None
                       else e.tensor_scalar(o, x, s1, s2, op0), *after)

    def cp(self, o, x, *after):
        return self.do(lambda e: e.tensor_copy(o, x), *after)

    def recip(self, o, x, *after):
        return self.do(lambda e: e.reciprocal(o, x), *after)

    def maxr(self, o, x, *after, negate=False):
        return self.do(lambda e: e.tensor_reduce(o, x, AXX, ALU.max, negate=negate), *after)

    def scan(self, o, m, x, init, op0, op1, *after):
        return self.do(lambda e: e.tensor_tensor_scan(o, m, x, init, op0, op1), *after)

    def fill(self, o, v, *after):
        return self.do(lambda e: e.memset(o, v), *after)

    def fn(self, o, x, f, *after, bias=0.0, scale=1.0, acc=None):
        return self.do(lambda e: e.activation(o, x, f, bias=bias, scale=scale, accum_out=acc) if acc is not None
                       else e.activation(o, x, f, bias=bias, scale=scale), *after)

    def mm(self, o, l, r, start, stop, *after, share=False):
        self.put(lambda e: e.matmul(o, l, r, start=start, stop=stop, skip_group_check=share), *after)

    def tr(self, o, x, ident, *after):
        self.put(lambda e: e.transpose(o, x, ident), *after)

    def tok(self):
        last = next((i for i in reversed(self.items) if i[0] is not None), None)
        if last is None:
            return None
        if last[2] is None:
            last[2] = (self.sem, 1)
            self.n += 1
        return (self.sem, self.n)

    def wait(self, *after):
        self.items.append([None, after, None])

    def dma(self, out, in_, chan, *after):
        self.items.append([lambda e: e.dma_start(out, in_), after, (chan.sem, 16)])
        chan.n += 16
        return (chan.sem, chan.n)

    def emit(self, eng):
        seen = {}

        def wait(a):
            if a is None:
                return
            if callable(a):
                a = a()
            if isinstance(a, list):
                for b in a:
                    wait(b)
                return
            if a is None:
                return
            sem, v = a
            if seen.get(id(sem), 0) < v:
                eng.wait_ge(sem, v)
                seen[id(sem)] = v

        for fn, after, sig in self.items:
            for a in after:
                wait(a)
            if fn is not None:
                ins = fn(eng)
                if sig is not None:
                    ins.then_inc(*sig)


class Chan:

    def __init__(self, sem):
        self.sem, self.n = sem, 0

    def tok(self):
        return (self.sem, self.n)


class Load:

    def __init__(self, view, ready):
        self.view, self.ready, self.free = view, ready, None


class Unit:

    def __init__(self, hi, lo, ready):
        self.hi, self.lo, self.ready, self.free = hi, lo, ready, None


class Job:

    def __init__(self, srcs, run, raw=False):
        self.srcs, self.run, self.raw, self.tiles = srcs, run, raw, None


class Program:
    def __init__(self, nc, ctx, a, stages):
        self.nc, self.ctx, self.a, self.stages = nc, ctx, a, stages
        sem = lambda n: ctx.enter_context(nc.semaphore(n))
        self.pe, self.act, self.dve, self.pool = (Queue(sem(f"s_{n}")) for n in ("pe", "act", "dve", "pool"))
        self.sp = Queue(None)
        self.free_sems = [sem(f"s_m{i}") for i in range(60)]
        self.rawc = [Chan(sem(f"s_raw{i}")) for i in range(NRAW)]
        self.loads = []
        self.units = []
        self.stackno = 0
        self.banks = []
        for i in range(4):
            t = ctx.enter_context(nc.psum_tensor(f"ps{i}", [128, 1024], F32))
            self.banks += [t[:, 0:512], t[:, 512:1024]]
            if i == 0:
                self.wide = []
            self.wide.append(t)
        self.XT = self.sb(ctx, "XT", [128, 8, T + TC], F32)
        self.RAW = self.sb(ctx, "RAW", [128, NRAW, 1024], F32)
        self.VT = self.sb(ctx, "VT", [128, NV], F32)
        self.K = self.sb(ctx, "K", [128, 256], F32)
        self.ONE, self.ID = self.K[:, 0:128], self.K[:, 128:256]
        self.MOD = self.sb(ctx, "MOD", [128, 9, 2, 24], F32)
        self.DER = self.sb(ctx, "DER", [128, 9, 3, 16], F32)
        self.SC = self.sb(ctx, "SC", [128, 8, 3], F32)
        self.modt = [None] * 9
        self.modread = None

    def sb(self, ctx, name, shape, dt):
        return ctx.enter_context(self.nc.sbuf_tensor(name, shape, dt))

    def chan(self):
        return Chan(self.free_sems.pop())

    def scope(self):
        self.stackno += 1
        return ExitStack()

    def name(self, s):
        return f"{s}_{self.stackno}"

    def barrier(self):
        es = [self.pe, self.act, self.dve, self.pool]
        toks = [e.tok() for e in es if e.items]
        for e in es:
            e.wait(toks)

    def vec(self, name, i=0, n=1):
        o = VOFF[name] + i
        return self.VT[:, o:o + n]


    def load(self, src):
        i = len(self.loads)
        prev = self.loads[i - NRAW] if i >= NRAW else None
        view = self.RAW[:, i % NRAW, :]
        ready = self.sp.dma(view, src, self.rawc[i % NRAW], (lambda: prev.free) if prev else None)
        ld = Load(view, ready)
        self.loads.append(ld)
        return ld

    def split(self, ld):
        i = len(self.units)
        prev = self.units[i - self.nunit] if i >= self.nunit else None
        hi, lo = self.WH[:, i % self.nunit, :], self.WL[:, i % self.nunit, :]
        th = self.act.do(lambda e: e.activation(hi, ld.view, ACT.Copy), ld.ready, prev.free if prev else None)
        tl = self.dve.do(lambda e: e.tensor_tensor(lo, ld.view, hi.bitcast(F32), ALU.subtract), th)
        ld.free = [th, tl]
        u = Unit(hi, lo, [th, tl])
        self.units.append(u)
        return u

    def unit_ring(self, ctx, n):
        self.WH = self.sb(ctx, self.name("WH"), [128, n, 1024], F32R)
        self.WL = self.sb(ctx, self.name("WL"), [128, n, 1024], F32R)
        self.nunit, self.units = n, []

    def prepare(self, job):
        job.tiles = [self.load(s) for s in job.srcs]
        if not job.raw:
            job.tiles = [self.split(t) for t in job.tiles]

    def run_jobs(self, jobs):
        ahead = 1
        for j in range(min(ahead, len(jobs))):
            self.prepare(jobs[j])
        for j, job in enumerate(jobs):
            if j + ahead < len(jobs):
                self.prepare(jobs[j + ahead])
            job.run(job.tiles)

    def mm3(self, out, w, x, first, last, *after):
        wh, wl = w
        xh, xl = x
        self.pe.put(lambda e: e.matmul(out, wh, xh, start=first, stop=False), *after)
        self.pe.put(lambda e: e.matmul(out, wh, xl, start=False, stop=False))
        self.pe.put(lambda e: e.matmul(out, wl, xh, start=False, stop=last))


    def setup(self):
        a, sp = self.a, self.sp
        c = self.chan()
        sp.dma(self.VT[:, :], a["vecs"], c)
        sp.dma(self.K[:, :], a["consts"], c)
        cx = self.chan()
        sp.dma(self.XT[:, :, 0:T], a["x_in"], cx)
        sp.dma(self.XT[:, :, T:T + TC], a["ctx_in"], cx)
        for q in (self.pe, self.act, self.dve, self.pool):
            q.wait(c.tok())
        for q in (self.act, self.dve):
            q.wait(cx.tok())
        for i, n in enumerate(("c", "c_ctx", "c_2")):
            self.act.do(lambda e, i=i, n=n: e.activation(self.SC[:, :, i], self.vec(n, 0, 8), ACT.Silu))
        self.sct = self.act.tok()


    def mod_ring(self, ctx):
        self.ACC = self.sb(ctx, self.name("ACC"), [128, 2, D], F32)
        self.accfree = None

    def mod_jobs(self, blk, third, bank):
        conds = (0, 1) if blk == 0 and third < 2 else ((0,) if blk < 2 else (2,))
        src = self.a["w_mod"][blk] if blk < 2 else self.a["w_ada_2"]
        bias = self.vec("b_mod" if blk < 2 else "b_ada_2", (blk if blk < 2 else 0) * 72 + 24 * third, 24)
        PS = self.banks[bank]
        jobs = []
        for jj in range(3):
            for k in range(8):
                def run(tiles, jj=jj, k=k):
                    ld = tiles[0]
                    t = []
                    for n, c in enumerate(conds):
                        acc, sc = self.ACC[:, n, :], self.SC[:, k, c:c + 1]
                        if k == 0:
                            t.append(self.dve.ts(acc, ld.view, sc, None, ALU.mult, None, ld.ready, self.sct, self.accfree))
                        else:
                            t.append(self.dve.stt(acc, ld.view, sc, acc, ALU.mult, ALU.add, ld.ready, self.acct[n]))
                    self.acct = t
                    ld.free = t
                    if k < 7:
                        return
                    for n in range(len(conds)):
                        for f in range(8):
                            o = n * 24 + jj * 8 + f
                            self.pe.mm(PS[:, o:o + 1], self.ACC[:, n, f * 128:(f + 1) * 128], self.ONE[:, 0:1],
                                       True, True, t, self.modread)
                    self.accfree = self.pe.tok()
                    if jj == 2:
                        self.mod_done(blk, third, PS, bias, len(conds), self.accfree)
                jobs.append(Job([src[k * 128:(k + 1) * 128, (3 * third + jj) * D:(3 * third + jj + 1) * D]], run, raw=True))
        return jobs

    def mod_done(self, blk, third, PS, bias, ncond, done):
        i = 3 * blk + third
        dve = self.dve
        for j in range(ncond):
            pv = PS[:, 24 * j:24 * j + 24]
            t = dve.do(lambda e, j=j, pv=pv: e.tensor_tensor(self.MOD[:, i, j, :], pv, bias, ALU.add), done)
        self.modread = t
        g = {0: lambda: self.vec("norm_g", 24 * blk + 8 * third, 8), 1: lambda: self.vec("norm_g", 24 * blk + 8 * third, 8),
             2: lambda: self.vec(("g_ffn1_2", "g_mix_2", "g_ffn2_2")[third], 0, 8)}[blk]()
        for j in range(ncond):
            M, R = self.MOD[:, i, j, :], self.DER[:, i, :, 8 * j:8 * j + 8]
            dve.do(lambda e, M=M, R=R: e.scalar_tensor_tensor(R[:, 0, :], M[:, 8:16], 1.0, g, ALU.add, ALU.mult), t)
            if blk == 1 and third == 1:
                dve.do(lambda e, M=M, R=R: e.tensor_tensor(R[:, 2, :], M[:, 16:24], self.vec("pool_scale", 0, 8), ALU.mult), t)
            else:
                f = 1.0 if third == 1 else 0.5
                dve.do(lambda e, M=M, R=R, f=f: e.tensor_scalar(R[:, 2, :], M[:, 16:24], f, None, ALU.mult), t)
        self.modt[i] = dve.tok()

    def mod_a(self, i, k, j=0):
        return self.DER[:, i, 0, 8 * j + k:8 * j + k + 1]

    def mod_b(self, i, k, j=0):
        return self.MOD[:, i, j, k:k + 1]

    def mod_g(self, i, k, j=0):
        return self.DER[:, i, 2, 8 * j + k:8 * j + k + 1]


    def rstd_of(self, ctx, name, n, ss, width, done, parts=128):
        R = self.sb(ctx, self.name(name), [128, n], F32)
        return R, self.rstd_into(R[0:parts, :], ss, width, done)

    def rstd_into(self, R, ss, width, done):
        t = self.dve.do(lambda e: e.tensor_scalar(R, ss, 1.0 / width, EPS, ALU.mult, ALU.add), done)
        t = self.dve.do(lambda e: e.reciprocal(R, R), t)
        return self.act.do(lambda e: e.activation(R, R, ACT.Sqrt), t)

    def norm(self, ctx, segs, banks, emit):
        SQ = self.sb(ctx, self.name("SQ"), [128, 2, 512], F32)
        R = self.sb(ctx, self.name("RS"), [128, T + TC], F32)
        xr = self.xready
        rt = {}
        free = [None, None]
        n = 0
        for (c0, c1, j), b in zip(segs, banks):
            w = c1 - c0
            for k in range(8):
                s = n % 2
                t = self.act.do(lambda e, s=s, k=k, c0=c0, c1=c1, w=w: e.activation(
                    SQ[:, s, 0:w], self.XT[:, k, c0:c1], ACT.Square), xr, free[s])
                self.pe.put(lambda e, s=s, k=k, w=w, b=b: e.matmul(self.banks[b][:, 0:w], self.ONE, SQ[:, s, 0:w],
                                                                   start=(k == 0), stop=(k == 7)), t)
                free[s] = self.pe.tok()
                n += 1
            rt[c0] = self.rstd_into(R[:, c0:c1], self.banks[b][:, 0:w], 1024, free[(n - 1) % 2])
        for k in range(8):
            for c0, c1, j in segs:
                emit(k, c0, c1, j, R[:, c0:c1], rt[c0])

    def norm_split(self, ctx, mi, segs, banks):
        w = max(s[1] for s in segs)
        self.HH = self.sb(ctx, self.name("HH"), [128, 8, w], F32R)
        self.HL = self.sb(ctx, self.name("HL"), [128, 8, w], F32R)
        tmp = ExitStack()
        TT = self.sb(tmp, self.name("TN"), [128, 2, 512], F32)
        self.ht = {}
        free = [None, None]
        cnt = [0]

        def emit(k, c0, c1, j, R, rt):
            s = cnt[0] % 2
            cnt[0] += 1
            t_ = TT[:, s, 0:c1 - c0]
            hh, hl = self.HH[:, k, c0:c1], self.HL[:, k, c0:c1]
            t1 = self.dve.do(lambda e: e.scalar_tensor_tensor(t_, self.XT[:, k, c0:c1], self.mod_a(mi, k, j), R,
                                                              ALU.mult, ALU.mult), rt, self.modt[mi], free[s])
            t2 = self.act.do(lambda e: e.activation(hh, t_, ACT.Identity, bias=self.mod_b(mi, k, j)), t1)
            t3 = self.dve.do(lambda e: e.scalar_tensor_tensor(hl, t_, self.mod_b(mi, k, j), hh.bitcast(F32),
                                                              ALU.add, ALU.subtract), t2)
            free[s] = t3
            self.ht[k, c0] = [t2, t3]

        self.norm(tmp, segs, banks, emit)
        tmp.close()

    def h(self, k, c0, c1):
        return self.HH[:, k, c0:c1], self.HL[:, k, c0:c1]


    def ffn(self, mi, segs, wi, wo, extra):
        with self.scope() as ctx:
            self.barrier()
            w = max(s[1] for s in segs)
            self.mod_ring(ctx)
            self.unit_ring(ctx, 5)
            NG = 5
            self.norm_split(ctx, mi, segs, (4, 5))
            GH = self.sb(ctx, self.name("GH"), [128, NG, w], F32R)
            GL = self.sb(ctx, self.name("GL"), [128, NG, w], F32R)
            S = self.sb(ctx, self.name("S"), [128, 2, w], F32)
            ub, db = [0, 1, 2, 3], [4, 5, 6]
            ufree, dfree = {b: None for b in ub}, {b: None for b in db}
            for b in (4, 5):
                dfree[b] = self.act.tok()
            cnt = {"u": 0, "d": 0}
            gfree, gready, sfree = {}, {}, {}
            xr = []

            def up(c):
                def run(tiles):
                    for q, u in enumerate(tiles):
                        for c0, c1, j in segs:
                            b = ub[cnt["u"] % len(ub)]
                            cnt["u"] += 1
                            out = self.banks[b][:, 0:c1 - c0]
                            for k in range(8):
                                ws = slice(k * 128, (k + 1) * 128)
                                self.mm3(out, (u.hi[:, ws], u.lo[:, ws]), self.h(k, c0, c1), k == 0, k == 7,
                                         u.ready, self.ht[k, c0], ufree[b] if k == 0 else None)
                            done = self.pe.tok()
                            u.free = done
                            s = S[:, c % 2, c0:c1]
                            if q == 0:
                                t = self.act.do(lambda e, s=s, out=out: e.activation(s, out, ACT.Silu),
                                                done, sfree.get((c % 2, c0)))
                                ufree[b] = t
                                sfree[c, c0, "t"] = t
                            else:
                                gh, gl = GH[:, c % NG, c0:c1], GL[:, c % NG, c0:c1]
                                t = self.dve.do(lambda e, s=s, out=out: e.tensor_tensor(s, s, out, ALU.mult),
                                                done, sfree[c, c0, "t"])
                                ufree[b] = t
                                t1 = self.act.do(lambda e, s=s, gh=gh: e.activation(gh, s, ACT.Copy), t,
                                                 gfree.get(c - NG))
                                t2 = self.dve.do(lambda e, s=s, gh=gh, gl=gl: e.tensor_tensor(
                                    gl, s, gh.bitcast(F32), ALU.subtract), t1)
                                sfree[c % 2, c0] = t2
                                gready[c, c0] = [t1, t2]
                return Job([wi[c], wi[NF + c]], run)

            def down(fs):
                def run(tiles):
                    for d in range(8):
                        for c0, c1, j in segs:
                            b = db[cnt["d"] % len(db)]
                            cnt["d"] += 1
                            out = self.banks[b][:, 0:c1 - c0]
                            ws = slice(d * 128, (d + 1) * 128)
                            for i, (f, u) in enumerate(zip(fs, tiles)):
                                self.mm3(out, (u.hi[:, ws], u.lo[:, ws]), (GH[:, f % NG, c0:c1], GL[:, f % NG, c0:c1]),
                                         i == 0, i == len(fs) - 1, u.ready, gready[f, c0], dfree[b] if i == 0 else None)
                            done = self.pe.tok()
                            x = self.XT[:, d, c0:c1]
                            dfree[b] = self.dve.do(lambda e, x=x, out=out, d=d, j=j: e.scalar_tensor_tensor(
                                x, out, self.mod_g(mi, d, j), x, ALU.mult, ALU.add), done)
                    for u in tiles:
                        u.free = done
                    for f in fs:
                        gfree[f] = done
                    xr[:] = [dfree[b]]
                return Job([wo[f] for f in fs], run)

            groups = [list(range(i, min(i + 3, NF))) for i in range(0, NF, 3)]
            jobs = []
            gi = 0
            for c in range(NF):
                jobs.append(up(c))
                while gi < len(groups) and groups[gi][-1] < c:
                    jobs.append(down(groups[gi]))
                    gi += 1
                n = len(extra) // (NF - c)
                jobs += extra[:n]
                extra = extra[n:]
            for g in groups[gi:]:
                jobs.append(down(g))
            self.run_jobs(jobs)
            self.xready = xr[0]


    def final_norm(self, gname):
        with self.scope() as ctx:
            self.barrier()

            def emit(k, c0, c1, j, R, rt):
                t = self.dve.do(lambda e: e.scalar_tensor_tensor(
                    self.XT[:, k, c0:c1], self.XT[:, k, c0:c1], self.vec(gname, k), R, ALU.mult, ALU.mult), rt)
                self.xready = t

            self.norm(ctx, [(0, T, 0)], (4,), emit)


    def projection(self, w, chunks, banks, segs_of, evac):
        free = {b: None for b in banks}
        cnt = [0]

        def job(ch):
            def run(tiles):
                u = tiles[0]
                for c0, c1 in segs_of(ch):
                    b = banks[cnt[0] % len(banks)]
                    cnt[0] += 1
                    out = self.banks[b][:, 0:c1 - c0]
                    for k in range(8):
                        ws = slice(k * 128, (k + 1) * 128)
                        self.mm3(out, (u.hi[:, ws], u.lo[:, ws]), self.h(k, c0, c1), k == 0, k == 7,
                                 u.ready, self.ht[k, c0], free[b] if k == 0 else None)
                    done = self.pe.tok()
                    u.free = done
                    free[b] = evac(ch, c0, c1, out, done)
            return Job([w[ch]], run)

        self.run_jobs([job(ch) for ch in chunks])

    def out_projection(self, mi, w, MIX, mready):
        with self.scope() as ctx:
            self.barrier()
            self.unit_ring(ctx, 4)
            MH = self.sb(ctx, self.name("MH"), [128, 8, T], F32R)
            ML = self.sb(ctx, self.name("ML"), [128, 8, T], F32R)
            mt = []
            for k in range(8):
                t1 = self.act.do(lambda e, k=k: e.activation(MH[:, k, :], MIX[:, k, :], ACT.Copy), mready)
                t2 = self.dve.do(lambda e, k=k: e.tensor_tensor(ML[:, k, :], MIX[:, k, :], MH[:, k, :].bitcast(F32),
                                                                ALU.subtract), t1)
                mt.append([t1, t2])
            free = {}

            def job(d):
                def run(tiles):
                    u = tiles[0]
                    b = d % 3
                    out = self.banks[b]
                    for k in range(8):
                        ws = slice(k * 128, (k + 1) * 128)
                        self.mm3(out, (u.hi[:, ws], u.lo[:, ws]), (MH[:, k, :], ML[:, k, :]), k == 0, k == 7,
                                 u.ready, mt[k], free.get(b) if k == 0 else None)
                    u.free = self.pe.tok()
                    x = self.XT[:, d, 0:T]
                    free[b] = self.dve.do(lambda e: e.scalar_tensor_tensor(
                        x, out, self.mod_g(mi, d), x, ALU.mult, ALU.add), u.free)
                    self.xready = free[b]
                return Job([w[d]], run)

            self.run_jobs([job(d) for d in range(8)])

    def mixer_pool(self, mi):
        PAD = 8
        W = T + 2 * PAD
        with self.scope() as ctx:
            self.barrier()
            sb = lambda n, s, dt=F32: self.sb(ctx, self.name(n), s, dt)
            H = sb("H", [128, 8, W])
            P2, P4, P8, PL = sb("P2", [128, 2, W]), sb("P4", [128, 2, W]), sb("P8", [128, 2, W]), sb("PL", [128, 2, T])
            CNT = sb("CNT", [128, 4, T])
            WP = sb("WP", [128, 4, 2, 256])
            cw = self.chan()
            self.pool.dma(CNT[:, :, :], self.a["pool_cnt"], cw)
            self.pool.dma(WP[:, :, :, :], self.a["pool_w"], cw)
            dve, act, pe = self.dve, self.act, self.pe
            z0 = dve.do(lambda e: e.memset(H[:, :, 0:PAD], 0.0))
            z1 = dve.do(lambda e: e.memset(H[:, :, PAD + T:W], 0.0))
            TT = sb("TN", [128, 2, 512])
            free = [None, None]
            ht = {}

            def emit(k, c0, c1, j, R, rt):
                s = k % 2
                t = dve.do(lambda e: e.scalar_tensor_tensor(TT[:, s, :], self.XT[:, k, 0:T], self.mod_a(mi, k), R,
                                                            ALU.mult, ALU.mult), rt, free[s])
                free[s] = ht[k] = act.do(lambda e: e.activation(H[:, k, PAD:PAD + T], TT[:, s, :], ACT.Identity,
                                                                bias=self.mod_b(mi, k)), t)

            self.norm(ctx, [(0, T, 0)], (4,), emit)
            add = lambda o, x, y, *w: dve.tt(o, x, y, ALU.add, *w)
            plfree = None
            bfree = {}
            for g in range(4):
                wt = [ht[2 * g], ht[2 * g + 1], z0, z1]
                h = lambda lo, hi, g=g: H[:, 2 * g:2 * g + 2, lo:hi]
                t = add(P2[:, :, 1:W], h(0, W - 1), h(1, W), wt)
                S, lo = P2, 0
                if g >= 1:
                    t = add(P4[:, :, 2:W - 1], P2[:, :, 1:W - 2], P2[:, :, 3:W], t)
                    S = P4
                if g >= 2:
                    t = add(P8[:, :, 4:W - 3], P4[:, :, 2:W - 5], P4[:, :, 6:W - 1], t)
                    S = P8
                if g >= 3:
                    t = add(P2[:, :, 8:8 + T], P8[:, :, 4:4 + T], P8[:, :, 12:12 + T], t)
                    S = P2
                cb = CNT[:, g:g + 1, :].broadcast_to([128, 2, T])
                t = dve.tt(PL[:, :, :], S[:, :, PAD:PAD + T], cb, ALU.mult, t, cw.tok(), plfree)
                t = dve.tt(PL[:, :, :], PL[:, :, :], h(PAD, PAD + T), ALU.subtract, t)
                for o in range(2):
                    b = 2 * (g % 2) + o
                    for i in range(2):
                        pe.put(lambda e, b=b, g=g, i=i, o=o: e.matmul(
                            self.banks[b], WP[:, g, i, o * 128:(o + 1) * 128], PL[:, i, :], start=(i == 0), stop=(i == 1)),
                            t, cw.tok(), bfree.get(b))
                    done = plfree = pe.tok()
                    k = 2 * g + o
                    x = self.XT[:, k, 0:T]
                    bfree[b] = dve.do(lambda e, x=x, b=b, k=k: e.scalar_tensor_tensor(
                        x, self.banks[b], self.mod_g(mi, k), x, ALU.mult, ALU.add), done)
            self.xready = dve.tok()


    def mixer_ab(self, mi):
        pe, act, dve, pool, a = self.pe, self.act, self.dve, self.pool, self.a
        W = T + TC
        with self.scope() as outer:
            self.barrier()
            sb = lambda n, s, dt=F32: self.sb(outer, self.name(n), s, dt)
            MIX = sb("MIX", [128, 8, T])
            QA, KA, VA = sb("QA", [128, 4, T]), sb("KA", [128, W]), sb("VA", [128, 6, 128])
            GQt, GKt, GRt = sb("GQt", [128, 2, T]), sb("GKt", [128, 2, W]), sb("GRt", [128, 4, T])
            ZG = sb("ZG", [32, W])
            VV = sb("VV", [128, 12, 2, 128])
            cc = self.chan()
            CB = sb("CB", [128, 384], BF16)
            WA = sb("WA", [32, 2, 256])
            pool.dma(WA[:, :, :], a["wa2"], cc)
            with ExitStack() as ctx:
                self.unit_ring(ctx, 2)
                RT = self.sb(ctx, self.name("RT"), [128, 2, T], F32)
                PR = self.sb(ctx, self.name("PR"), [128, 128], F32)
                pool.dma(RT[:, :, :], a["rope1"], cc)
                pool.dma(PR[:, :], a["perm1"], cc)
                segs = [(0, T, 0), (T, W, 1)]
                with ExitStack() as tmp:
                    CF = self.sb(tmp, self.name("CF"), [128, 384], F32)
                    pool.dma(CF[:, :], a["cb"][:, 0:384], cc)
                    act.fn(CB[:, :], CF[:, :], ACT.Copy, cc.tok())
                self.norm_split(ctx, mi, segs, (4, 5))
                VB = self.sb(ctx, self.name("VB"), [128, 2, W], F32)
                TMP = self.sb(ctx, self.name("TMP"), [128, T], F32)
                pfree = {6: None, 7: None}
                vbt, vbfree, nt = {}, {}, [0]
                tmpfree = [None]

                def tbank():
                    nt[0] += 1
                    return 6 + nt[0] % 2

                def rope(x, ready):
                    b = tbank()
                    pe.mm(self.banks[b], PR[:, :], x, True, True, ready, pfree[b], cc.tok())
                    t = dve.tt(TMP[:, :], self.banks[b], RT[:, 1, :], ALU.mult, pe.tok(), tmpfree[0], cc.tok())
                    pfree[b] = t
                    t2 = dve.tt(x, x, RT[:, 0, :], ALU.mult, pe.tok(), ready)
                    tmpfree[0] = dve.tt(x, x, TMP[:, :], ALU.add, t, t2)

                def evac(ch, c0, c1, out, done):
                    if ch < AK:
                        t = act.fn(QA[:, ch, :], out, ACT.Copy, done)
                        rope(QA[:, ch, :], t)
                    elif ch == AK:
                        t = act.fn(KA[:, c0:c1], out, ACT.Copy, done)
                        if c0 == 0:
                            rope(KA[:, 0:T], t)
                    elif ch == AV:
                        t = act.fn(VB[:, 0, c0:c1], out, ACT.Copy, done, vbfree.get(0))
                        b = tbank()
                        n = (c1 - c0) // 128
                        for i in range(n):
                            pe.tr(self.banks[b][:, i * 128:(i + 1) * 128], VB[:, 0, c0 + i * 128:c0 + (i + 1) * 128],
                                  self.ID, t, pfree[b])
                        vbfree[0] = pe.tok()
                        pfree[b] = dve.cp(VA[:, c0 // 128:c0 // 128 + n, :],
                                          self.banks[b][:, 0:n * 128].rearrange("p (n f) -> p n f", f=128), vbfree[0])
                    elif ch < GK:
                        t = act.fn(GQt[:, ch - GQ, :], out, ACT.Copy, done)
                    elif ch < GV:
                        t = act.fn(GKt[:, ch - GK, c0:c1], out, ACT.Copy, done)
                    elif ch < GR:
                        pair, par = (ch - GV) // 2, (ch - GV) % 2
                        t = act.fn(VB[:, par, c0:c1], out, ACT.Copy, done, vbfree.get(par))
                        vbt[par, c0] = t
                        if par == 1 and c0 == T:
                            for q in range(3):
                                b = tbank()
                                for i in range(4):
                                    cl = (4 * q + i) * 64
                                    for pr in range(2):
                                        pe.mm(self.banks[b][64 * pr:64 * pr + 64, i * 128:(i + 1) * 128],
                                              VB[:, pr, cl:cl + 64], self.ID, True, True,
                                              vbt[pr, 0], vbt[pr, T], pfree[b])
                                vbfree[0] = vbfree[1] = pe.tok()
                                pfree[b] = dve.cp(VV[:, 4 * q:4 * q + 4, pair, :],
                                                  self.banks[b].rearrange("p (n f) -> p n f", f=128), vbfree[0])
                    elif ch < GZ:
                        t = act.fn(GRt[:, ch - GR, :], out, ACT.Silu, done)
                    else:
                        t = act.fn(ZG[:, c0:c1], out[0:32, :], ACT.Copy, done)
                    return t

                xc = lambda ch: [(0, T)] if ch < AK or GQ <= ch < GK or GR <= ch < GZ else [(0, T), (T, W)]
                self.projection(a["w_in"], [GZ, AV, AK, 0, 1, 2, 3] + list(range(GQ, GZ)), (0, 1, 2, 3), xc, evac)
            self.window(outer, QA, KA, VA, CB, MIX)
            self.gla(outer, GQt, GKt, GRt, ZG, WA, VV, MIX, cc)
            self.out_ready = self.act.tok(), self.dve.tok()
            self.out_projection(mi, a["w_out"], MIX, list(self.out_ready))

    def window(self, outer, QA, KA, VA, CB, MIX):
        pe, act, dve = self.pe, self.act, self.dve
        IDB, ML = CB[:, 0:128], CB[:, 128:384]
        with ExitStack() as ctx:
            self.barrier()
            sb = lambda n, s: self.sb(ctx, self.name(n), s, F32)
            P, PT, ON = sb("P", [128, 2, 640]), sb("PT", [128, 3, 640]), sb("ON", [128, 2, 512])
            MX, NM, DEN, ES = (sb(n, [128, 2, 8]) for n in ("MX", "NM", "DEN", "ES"))
            SK, NSK, SD = sb("SK", [128, 8]), sb("NSK", [128, 8]), sb("SD", [8, 8])
            t = dve.ts(SD[:, :], self.ID[0:8, 0:8], self.VT[0:8, VOFF["sink"]:VOFF["sink"] + 1], None, ALU.mult, None)
            pe.mm(self.banks[7][:, 0:8], self.ONE[0:8, :], SD[:, :], True, True, t)
            t = dve.cp(SK[:, :], self.banks[7][:, 0:8], pe.tok())
            skt = dve.ts(NSK[:, :], SK[:, :], -1.0, None, ALU.mult, None, t)
            units = [(n, j, par) for n in range(4) for j in range(4) for par in range(2)]
            sfree, pfree, ptpfree, ptfree = {}, {}, None, {}
            expt, evt, pvt, maxt = {}, {}, {}, {}
            ofree, otfree, onfree = skt, skt, {}
            statfree = {}

            def blocks(n):
                return list(range(max(0, n - 1), min(4, n + 2)))

            for u in range(len(units) + 2):
                if u < len(units):
                    n, j, par = units[u]
                    rows = slice(64 * par, 64 * par + 64)
                    bl = blocks(n)
                    nk = 128 * len(bl)
                    w = self.wide[u % 2]
                    q = QA[rows, j, n * 128:(n + 1) * 128]
                    pe.mm(w[:, 512 - nk:512], q, KA[rows, bl[0] * 128:bl[0] * 128 + nk], True, True, sfree.get(u % 2))
                    edge = []
                    if n > 0:
                        edge.append((512 - nk, 0))
                    if n < 3:
                        edge.append((384, 1))
                    for i, (o, m) in enumerate(edge):
                        pe.mm(w[:, o:o + 128], IDB, ML[:, m * 128:(m + 1) * 128], False, True, share=True)
                    pe.mm(w[:, 512:768], q, KA[rows, T:T + TC], True, True)
                    ts_ = pe.tok()
                    hs = 2 * j + par
                    s = n % 2
                    view = w[:, 512 - nk:768]
                    tm = dve.maxr(MX[:, s, hs:hs + 1], view, ts_, statfree.get(n - 2))
                    h = j + 4 * par
                    tm = maxt[u] = dve.ts(NM[:, s, hs:hs + 1], MX[:, s, hs:hs + 1], -0.125, NSK[:, h:h + 1],
                                          ALU.mult, ALU.min, tm)
                    expt[u] = sfree[u % 2] = act.fn(P[:, u % 2, 0:nk + 256], view, ACT.Exp, tm, pfree.get(u % 2),
                                                    bias=NM[:, s, hs:hs + 1], scale=0.125, acc=DEN[:, s, hs:hs + 1])
                if 1 <= u <= len(units):
                    v = u - 1
                    n, j, par = units[v]
                    nb = len(blocks(n)) + 2
                    for i in range(nb):
                        pe.tr(self.wide[2][:, i * 128:(i + 1) * 128], P[:, v % 2, i * 128:(i + 1) * 128], self.ID,
                              expt[v], ptpfree)
                    pfree[v % 2] = pe.tok()
                    t1 = act.fn(PT[:, v % 3, 0:512], self.wide[2][:, 0:512], ACT.Copy, pfree[v % 2], ptfree.get(v % 3))
                    evt[v] = [t1]
                    if nb == 5:
                        evt[v].append(dve.cp(PT[:, v % 3, 512:640], self.wide[2][:, 512:640], pfree[v % 2], ptfree.get(v % 3)))
                    ptpfree = evt[v]
                if u >= 2:
                    v = u - 2
                    n, j, par = units[v]
                    hs = 2 * j + par
                    bl = blocks(n) + [4, 5]
                    for i, b in enumerate(bl):
                        pe.mm(self.banks[6][:, hs * 64:hs * 64 + 64], PT[:, v % 3, i * 128:(i + 1) * 128],
                              VA[:, b, par * 64:par * 64 + 64], i == 0, i == len(bl) - 1, evt[v],
                              ofree if hs == 0 and i == 0 else None)
                    ptfree[v % 3] = pe.tok()
                    if hs == 7:
                        s = n % 2
                        t = dve.do(lambda e, s=s: e.tensor_tensor(ES[:, s, 0:8:2], SK[:, 0:4], NM[:, s, 0:8:2], ALU.add),
                                   maxt[v])
                        t2 = dve.do(lambda e, s=s: e.tensor_tensor(ES[:, s, 1:8:2], SK[:, 4:8], NM[:, s, 1:8:2], ALU.add),
                                    maxt[v])
                        t = act.fn(ES[:, s, :], ES[:, s, :], ACT.Exp, t, t2)
                        t = dve.tt(DEN[:, s, :], DEN[:, s, :], ES[:, s, :], ALU.add, t, expt[v])
                        t = dve.recip(DEN[:, s, :], DEN[:, s, :], t)
                        o3 = self.banks[6].rearrange("p (h d) -> p h d", d=64)
                        rb = DEN[:, s, :].rearrange("p (h o) -> p h o", o=1).broadcast_to([128, 8, 64])
                        t = ofree = statfree[n] = dve.tt(ON[:, s, :].rearrange("p (h d) -> p h d", d=64), o3, rb,
                                                         ALU.mult, t, ptfree[v % 3], onfree.get(s))
                        for c in range(4):
                            pe.tr(self.banks[7][:, c * 128:(c + 1) * 128], ON[:, s, c * 128:(c + 1) * 128], self.ID,
                                  t, otfree)
                        onfree[s] = pe.tok()
                        otfree = act.fn(MIX[:, 0:4, n * 128:(n + 1) * 128],
                                        self.banks[7].rearrange("p (c t) -> p c t", t=128), ACT.Copy, onfree[s])

    def gla(self, outer, GQt, GKt, GRt, ZG, WA, VV, MIX, cc):
        pe, act, dve, pool = self.pe, self.act, self.dve, self.pool
        W = T + TC
        banks = self.banks
        with ExitStack() as ctx:
            self.barrier()
            sb = lambda n, s, dt=F32: self.sb(ctx, self.name(n), s, dt)
            GN = [sb(f"GN{d}", [128, 2, W]) for d in range(2)]
            KE = sb("KE", [128, 2, W])
            QT, KT = sb("QT", [128, 2, 2, T]), sb("KT", [128, 2, 2, T])
            KEN = [sb(f"KEN{d}", [128, 12, 2, 64]) for d in range(2)]
            ST = sb("ST", [128, 2, 10, 256])
            DEC = sb("DEC", [128, 2, 2, 12])
            SM = sb("SM", [128, 2, W])
            AS = sb("AS", [128, 2, 256])
            MK = sb("MK", [128, 256], I32)
            ck = self.chan()
            pool.dma(MK[:, :], self.a["gla_mask"], ck)
            z = [pool.fill(SM[:, :, :], 1.0)]
            z = [pool.do(lambda e: e.memset(SM[:, 0, 0:W:64], 0.0), z), pool.do(lambda e: e.memset(SM[:, 1, 63:W:64], 0.0), z),
                 pool.fill(AS[:, :, :], 0.0)]
            bfree = {}
            gt = {}
            nb = 0
            E = sb("E", [128, 2, T])
            efree = [None]
            for d in range(2):
                bias = self.vec("b_a_f" if d == 0 else "b_a_b", 0, 2)
                for p in range(2):
                    for c0, c1 in ((0, T), (T, W)):
                        b = nb % 4
                        nb += 1
                        out = banks[b][:, 0:c1 - c0]
                        pe.mm(out, WA[:, d, p * 128:(p + 1) * 128], ZG[:, c0:c1], True, True, bfree.get(b), cc.tok())
                        bp = bias[:, p:p + 1]
                        g = GN[d][:, p, c0:c1]
                        ab = KE[:, p, c0:c1]
                        t1 = act.fn(ab, out, ACT.Abs, pe.tok(), gt.get((d - 1, p)), bias=bp)
                        t2 = bfree[b] = dve.ts(g, out, bp, 0.0, ALU.add, ALU.min, t1)
                        t1 = act.fn(ab, ab, ACT.Exp, t1, scale=-1.0)
                        t1 = act.fn(ab, ab, ACT.Ln, t1, bias=1.0)
                        t = dve.stt(g, g, -1.0, ab, ALU.mult, ALU.add, t1, t2)
                    g, m = GN[d][:, p, :], SM[:, d, :]
                    if d == 1:
                        g, m = g[:, ::-1], m[:, ::-1]
                    gt[d, p] = dve.scan(g, m, g, 0.0, ALU.mult, ALU.add, t, z)
            ready = {}
            for d in range(2):
                G = GN[d]
                gs = [gt[d, 0], gt[d, 1]]
                ge = G[:, :, 63:W:64] if d == 0 else G[:, :, 0:W:64]
                dec = act.fn(DEC[:, d, :, :], ge, ACT.Exp, gs, scale=-0.0625)
                t = act.fn(E[:, :, :], G[:, :, 0:T], ACT.Exp, gs, efree[0], scale=-0.0625)
                tq = dve.stt(QT[:, d, :, :], GQt[:, :, :], 0.125, E[:, :, :], ALU.mult, ALU.mult, t)
                t = act.fn(E[:, :, :], G[:, :, 0:T], ACT.Exp, gs, tq, scale=0.0625)
                tk = efree[0] = dve.tt(KT[:, d, :, :], GKt[:, :, 0:T], E[:, :, :], ALU.mult, t)
                t = None
                for p in range(2):
                    last = ge[:, p, :].rearrange("p (c o) -> p c o", o=1).broadcast_to([128, 12, 64])
                    k3 = KE[:, p, :].rearrange("p (c t) -> p c t", t=64)
                    t = dve.tt(k3, G[:, p, :].rearrange("p (c t) -> p c t", t=64), last, ALU.subtract, gs, gt[1, 1],
                               ready.get((d - 1, "ken")))
                t = act.fn(KE[:, :, :], KE[:, :, :], ACT.Exp, t, scale=0.0625)
                t = dve.tt(KE[:, :, :], KE[:, :, :], GKt[:, :, :], ALU.mult, t)
                kt = []
                for q in range(3):
                    b = nb % 4
                    nb += 1
                    for i in range(4):
                        cl = (4 * q + i) * 64
                        for p in range(2):
                            for par in range(2):
                                r = slice(64 * par, 64 * par + 64)
                                o = (i * 2 + p) * 64
                                pe.mm(banks[b][r, o:o + 64], KE[r, p, cl:cl + 64], self.ID[r, r], True, True, t, bfree.get(b))
                    tt_ = pe.tok()
                    bfree[b] = act.fn(KEN[d][:, 4 * q:4 * q + 4, :, :],
                                      banks[b].rearrange("p (c q f) -> p c q f", q=2, f=64), ACT.Copy, tt_)
                    kt.append(bfree[b])
                ready[d] = (tq, tk, kt, dec)
                ready[d, "ken"] = tt_
            seq = [[8, 9, 10, 11] + list(range(8)), [11, 10, 9, 8] + list(range(7, -1, -1))]
            slot = lambda d, i: seq[d][i] if i >= 4 else 8 + i % 2
            stt_ = {}
            for i in range(11):
                for d in range(2):
                    c = seq[d][i]
                    b = nb % 4
                    nb += 1
                    for p in range(2):
                        for par in range(2):
                            r = slice(64 * par, 64 * par + 64)
                            pe.mm(banks[b][r, p * 128:(p + 1) * 128], KEN[d][r, c, p, :], VV[r, c, p, :], True, True,
                                  ready[d][2], bfree.get(b))
                    done = pe.tok()
                    new = ST[:, d, slot(d, i + 1), :]
                    if i == 0:
                        t = dve.cp(new, banks[b][:, 0:256], done)
                    else:
                        old = ST[:, d, slot(d, i), :]
                        for p in range(2):
                            ps = slice(p * 128, (p + 1) * 128)
                            t = dve.stt(new[:, ps], old[:, ps], DEC[:, d, p, c:c + 1], banks[b][:, ps], ALU.mult, ALU.add,
                                        done, stt_[d, i], ready[d][3])
                    stt_[d, i + 1] = bfree[b] = t
            sdone = {d: stt_[d, 11] for d in range(2)}
            asfree = {}
            attm = {}

            def att(c):
                b = c % 2
                cl = slice(c * 64, c * 64 + 64)
                for d in range(2):
                    for p in range(2):
                        for par in range(2):
                            r = slice(64 * par, 64 * par + 64)
                            o = (d * 2 + p) * 64
                            pe.mm(banks[b][r, o:o + 64], KT[r, d, p, cl], QT[r, d, p, cl], True, True,
                                  ready[d][0], ready[d][1], bfree.get(b))
                attm[c] = bfree[b] = dve.do(
                    lambda e: e.copy_predicated(AS[:, c % 2, :], MK[:, :], banks[b][:, 0:256]),
                    pe.tok(), asfree.get(c % 2), z, ck.tok())

            for b in range(4):
                bfree[b] = [bfree.get(b), self.dve.tok(), self.act.tok()]
            att(0)
            for c in range(8):
                if c < 7:
                    att(c + 1)
                cl = slice(c * 64, c * 64 + 64)
                for p in range(2):
                    for par in range(2):
                        r = slice(64 * par, 64 * par + 64)
                        out = banks[4 + 2 * p + par][:, cl]
                        for d in range(2):
                            o = (d * 2 + p) * 64
                            pe.mm(out, VV[r, c, p, :], AS[r, c % 2, o:o + 64], d == 0, False, attm[c], share=True)
                            pe.mm(out, ST[r, d, c, p * 128:(p + 1) * 128], QT[r, d, p, cl], False, d == 1, sdone[d],
                                  share=True)
                asfree[c % 2] = pe.tok()
            done = pe.tok()
            SQ, RS = E[:, 0, :], E[:, 1, :]
            fq = [efree[0], ready[1][1]]
            for h in range(4):
                t = act.fn(SQ, banks[4 + h], ACT.Square, done, fq)
                b = h % 2
                pe.mm(banks[b], self.ONE, SQ, True, True, t, attm[6], attm[7], bfree.get(b))
                t = bfree[b] = dve.ts(RS, banks[b], 1.0 / 128, EPS, ALU.mult, ALU.add, pe.tok(), fq)
                t = dve.recip(RS, RS, t)
                t = act.fn(RS, RS, ACT.Sqrt, t)
                m = MIX[:, 4 + h, :]
                t = dve.stt(m, banks[4 + h], self.vec("gla_g"), RS, ALU.mult, ALU.mult, t)
                t = dve.tt(m, m, GRt[:, h, :], ALU.mult, t)
                fq = [t]


    def mixer_hybrid(self, mi):
        pe, act, dve, pool, a = self.pe, self.act, self.dve, self.pool, self.a
        banks = self.banks
        with self.scope() as outer:
            self.barrier()
            sb = lambda n, s, dt=F32: self.sb(outer, self.name(n), s, dt)
            MIX = sb("MIX", [128, 8, T])
            MQt, MKt, MVt, MOt = sb("MQt", [128, 2, T]), sb("MKt", [128, 2, T]), sb("MVt", [128, 4, 512]), sb("MOt", [128, 4, T])
            DQt, DKt, DVt = sb("DQt", [128, 4, T]), sb("DKt", [128, 4, T]), sb("DVt", [128, 4, 512])
            GT = sb("GT", [4, 4, T])
            cc = self.chan()
            with ExitStack() as ctx:
                self.unit_ring(ctx, 2)
                RT = self.sb(ctx, self.name("RT"), [128, 2, T], F32)
                PR = self.sb(ctx, self.name("PR"), [128, 256], F32)
                GQ8 = self.sb(ctx, self.name("GQ8"), [128, 1], F32)
                pool.dma(RT[:, :, :], a["rope2"], cc)
                pool.dma(PR[:, :], a["perm2"], cc)
                gq8 = dve.ts(GQ8[:, :], self.vec("g_q_2"), 0.125, None, ALU.mult, None)
                self.norm_split(ctx, mi, [(0, T, 0)], (4,))
                VB = self.sb(ctx, self.name("VB"), [128, T], F32)
                TMP = self.sb(ctx, self.name("TMP"), [128, 3, T], F32)
                pfree = {5: None, 6: None, 7: None}
                free = {"vb": None, "tmp": None, "sq": None, "rs": None}
                nt = [0]

                def tbank():
                    nt[0] += 1
                    return 5 + nt[0] % 3

                def normed_rope(x, gain, t):
                    SQ, RS, TM = TMP[:, 0, :], TMP[:, 1, :], TMP[:, 2, :]
                    t1 = act.fn(SQ, x, ACT.Square, t, free["sq"])
                    b = tbank()
                    pe.mm(banks[b], PR[:, 128:256], SQ, True, True, t1, pfree[b], cc.tok())
                    free["sq"] = pe.tok()
                    t1 = pfree[b] = dve.ts(RS, banks[b], 1.0 / 64, EPS, ALU.mult, ALU.add, free["sq"], free["rs"])
                    t1 = dve.recip(RS, RS, t1)
                    t1 = act.fn(RS, RS, ACT.Sqrt, t1)
                    t1 = free["rs"] = dve.stt(x, x, gain, RS, ALU.mult, ALU.mult, t1, gq8)
                    b = tbank()
                    pe.mm(banks[b], PR[:, 0:128], x, True, True, t1, pfree[b])
                    t2 = pfree[b] = dve.tt(TM, banks[b], RT[:, 1, :], ALU.mult, pe.tok(), free["tmp"], cc.tok())
                    t3 = dve.tt(x, x, RT[:, 0, :], ALU.mult, pe.tok())
                    free["tmp"] = dve.tt(x, x, TM, ALU.add, t2, t3)

                def token_major(V, h, out, done):
                    t = act.fn(VB[:, :], out, ACT.Copy, done, free["vb"])
                    b = tbank()
                    for i in range(4):
                        pe.tr(banks[b][:, i * 128:(i + 1) * 128], VB[:, i * 128:(i + 1) * 128], self.ID, t, pfree[b])
                    free["vb"] = pe.tok()
                    pfree[b] = dve.cp(V[:, :, h * 128:(h + 1) * 128], banks[b].rearrange("p (n f) -> p n f", f=128), free["vb"])
                    return t

                def evac(ch, c0, c1, out, done):
                    if ch < MK:
                        return act.fn(MQt[:, ch - MQ, :], out, ACT.Copy, done)
                    if ch < MV:
                        return act.fn(MKt[:, ch - MK, :], out, ACT.Copy, done, scale=0.125)
                    if ch < MO:
                        return token_major(MVt, ch - MV, out, done)
                    if ch < MG:
                        return act.fn(MOt[:, ch - MO, :], out, ACT.Sigmoid, done)
                    if ch == MG:
                        for g in range(4):
                            o = VOFF["gate_bias_2"] + g
                            t = act.fn(GT[:, g, :], out[32 * g:32 * g + 4, :], ACT.Identity, done, bias=self.VT[0:4, o:o + 1])
                        return t
                    if ch < DV:
                        X, i, gain = (DQt, ch - DQ, GQ8[:, :]) if ch < DK else (DKt, ch - DK, self.vec("g_k_2"))
                        t = act.fn(X[:, i, :], out, ACT.Copy, done)
                        normed_rope(X[:, i, :], gain, t)
                        return t
                    return token_major(DVt, ch - DV, out, done)

                self.projection(a["w_in_2"], [MG] + list(range(DQ, NIN2)) + list(range(MQ, MG)), (0, 1, 2, 3),
                                lambda ch: [(0, T)], evac)
            self.mlstm(MQt, MKt, MVt, MOt, GT, MIX)
            self.dilated(DQt, DKt, DVt, MIX)
            self.out_projection(mi, a["w_out_2"], MIX, [act.tok(), dve.tok()])

    def mlstm(self, Q, K, V, O, GT, MIX):
        pe, act, dve, pool = self.pe, self.act, self.dve, self.pool
        banks = self.banks
        with ExitStack() as ctx:
            self.barrier()
            sb = lambda n, s, dt=F32: self.sb(ctx, self.name(n), s, dt)
            U, EM, R = sb("U", [4, 2, T]), sb("EM", [4, 2, T]), sb("R", [4, 2, T])
            B, MG_, ON = sb("B", [4, T]), sb("MG", [4, 2, T]), sb("ON1", [4, T])
            UT = sb("UT", [128, 8, 4])
            MB, MD = sb("MB", [128, 8, T]), sb("MD", [128, 2, T])
            NUM = sb("NUM", [128, 8, T])
            A = sb("A", [128, 4, T])
            SEL, OH, MKD = sb("SEL", [4, 4, 128]), sb("OH", [128, 4, 4]), sb("MKD", [128, 2, 128])
            ck = self.chan()
            pool.dma(SEL[:, :, :], self.a["sel"], ck)
            pool.dma(OH[:, :, :], self.a["onehot"], ck)
            pool.dma(MKD[:, :, :], self.a["tri"], ck)
            one = pool.fill(ON[:, :], 1.0)
            bfree = {}
            bt = None
            for d in range(2):
                li, z = GT[:, 2 * d, :], GT[:, 2 * d + 1, :]
                ab = EM[:, d, :]
                t = act.fn(ab, z, ACT.Abs)
                t = act.fn(ab, ab, ACT.Exp, t, scale=-1.0)
                t = act.fn(ab, ab, ACT.Ln, t, bias=1.0)
                t = dve.stt(z, z, 0.0, ab, ALU.min, ALU.subtract, t)
                rv = (lambda x: x) if d == 0 else (lambda x: x[:, ::-1])
                t = dve.scan(rv(B[:, :]), ON[:, :], rv(z), 0.0, ALU.mult, ALU.add, t, one, bt)
                t = dve.tt(U[:, d, :], li, B[:, :], ALU.subtract, t)
                u = rv(U[:, d, :])
                t = dve.scan(rv(MG_[:, d, :]), u, u, -BIG, ALU.max, ALU.max, t)
                bt = dve.tt(ab, B[:, :], MG_[:, d, :], ALU.add, t)
                emt = act.fn(ab, ab, ACT.Exp, bt, scale=-1.0)
                for s in range(4):
                    pe.tr(banks[0][:, (d * 4 + s) * 4:(d * 4 + s) * 4 + 4], U[:, d, s * 128:(s + 1) * 128], self.ID[0:4, 0:4], t)
            ut = bfree[0] = dve.cp(UT[:, :, :], banks[0][:, 0:32].rearrange("p (s h) -> p s h", h=4), pe.tok())
            mbt = {}

            def spread(d, h):
                i = d * 4 + h
                b = i % 2
                pe.mm(banks[b], SEL[:, h, :], MG_[:, d, :], True, True, bt, bfree.get(b), ck.tok())
                mbt[d, h] = bfree[b] = act.fn(MB[:, i, :], banks[b], ACT.Copy, pe.tok())

            for h in range(4):
                for d in range(2):
                    spread(d, h)
            afree, nfree, mdfree = {}, {}, {}
            na = 0
            numt = {}
            nq = 0
            prev = []
            for h in range(4):
                p, par = h // 2, h % 2
                r = slice(64 * par, 64 * par + 64)
                mdt = {}
                for d in range(2):
                    m = MKD[:, d:d + 1, :].broadcast_to([128, 4, 128])
                    mdt[d] = dve.tt(MD[:, d, :].rearrange("p (n t) -> p n t", t=128),
                                    MB[:, d * 4 + h, :].rearrange("p (n t) -> p n t", t=128), m, ALU.add,
                                    mbt[d, h], ck.tok(), mdfree.get(d))
                nb = [2 + 2 * (h % 2), 3 + 2 * (h % 2)]
                for j in range(4):
                    qb = nq % 2
                    nq += 1
                    js = slice(j * 128, j * 128 + 128)
                    pe.mm(banks[qb], K[r, p, js], Q[r, p, :], True, True, bfree.get(qb))
                    qt = pe.tok()
                    now = []
                    for d in range(2):
                        s = na % 4
                        na += 1
                        ub = UT[:, d * 4 + j, h:h + 1]
                        t1 = act.fn(A[:, s, js], MD[:, d, js], ACT.Exp, mdt[d], ut, afree.get(s), bias=ub, scale=-1.0)
                        mdfree[d] = t1
                        off = slice((j + 1) * 128, T) if d == 0 else slice(0, j * 128)
                        if off.stop > off.start:
                            t1 = act.fn(A[:, s, off], MB[:, d * 4 + h, off], ACT.Exp, afree.get(s), bias=ub, scale=-1.0)
                        full = slice(j * 128, T) if d == 0 else slice(0, (j + 1) * 128)
                        t = bfree[qb] = dve.tt(A[:, s, full], A[:, s, full], banks[qb][:, full], ALU.mult, t1, qt)
                        now.append((h, j, d, s, full, t, nb[d]))
                    for x in prev:
                        self.mlstm_sum(x, V, A, OH, NUM, afree, nfree, numt, ck)
                    prev = now
            for x in prev:
                self.mlstm_sum(x, V, A, OH, NUM, afree, nfree, numt, ck)
            rt = {}
            for d in range(2):
                t = act.fn(R[:, d, :], banks[6 + d][0:4, :], ACT.Abs, pe.tok())
                t = dve.tt(R[:, d, :], R[:, d, :], EM[:, d, :], ALU.max, t, emt)
                rt[d] = dve.recip(R[:, d, :], R[:, d, :], t)
            SQ, RS = A[:, 0, :], A[:, 1, :]
            fq = [afree[0], afree[1]]
            for h in range(4):
                t = []
                for d in range(2):
                    b = 2 * (h % 2) + d
                    pe.mm(banks[b], SEL[:, h, :], R[:, d, :], True, True, rt[d], numt[3, d], bfree.get(b), nfree.get(b))
                    x = NUM[:, d * 4 + h, :]
                    tt_ = dve.tt(x, x, banks[b], ALU.mult, pe.tok(), numt[h, d])
                    bfree[b] = tt_
                    t.append(tt_)
                x = NUM[:, h, :]
                t = dve.tt(x, x, NUM[:, 4 + h, :], ALU.add, t)
                t1 = act.fn(SQ, x, ACT.Square, t, fq)
                b = 4 + h % 2
                pe.mm(banks[b], self.ONE, SQ, True, True, t1, bfree.get(b), nfree.get(b), numt[3, 0], numt[3, 1])
                t1 = bfree[b] = dve.ts(RS, banks[b], 1.0 / 128, EPS, ALU.mult, ALU.add, pe.tok(), fq)
                t1 = dve.recip(RS, RS, t1)
                t1 = act.fn(RS, RS, ACT.Sqrt, t1)
                m = MIX[:, h, :]
                t1 = dve.stt(m, x, self.vec("g_mh_2", h), RS, ALU.mult, ALU.mult, t1)
                dve.tt(m, m, O[:, h, :], ALU.mult, t1)
                fq = [t1]

    def mlstm_sum(self, item, V, A, OH, NUM, afree, nfree, numt, ck):
        pe = self.pe
        h, j, d, s, full, t, b = item
        x = A[:, s, full]
        pe.mm(self.banks[b][:, full], V[:, j, h * 128:(h + 1) * 128], x, j == 0, True, t,
              nfree.get(b) if j == 0 else None, share=j > 0)
        pe.mm(self.banks[6 + d][0:4, full], OH[:, h, :], x, h == 0 and j == 0, True, ck.tok(), share=h + j > 0)
        afree[s] = pe.tok()
        if j == 3:
            numt[h, d] = nfree[b] = self.act.fn(NUM[:, d * 4 + h, :], self.banks[b], ACT.Copy, afree[s])

    def dilated(self, Q, K, V, MIX):
        pe, act, dve, pool = self.pe, self.act, self.dve, self.pool
        banks = self.banks
        with ExitStack() as ctx:
            self.barrier()
            sb = lambda n, s, dt=F32: self.sb(ctx, self.name(n), s, dt)
            CB, CM = sb("CB", [128, 1024], BF16), sb("CM", [128, 896])
            P, PT, ON = sb("P", [128, 3, 512]), sb("PT", [128, 3, 512]), sb("ON", [128, 2, 512])
            NM, DEN = sb("NM", [128, 2, 8]), sb("DEN", [128, 2, 8])
            ck = self.chan()
            CF = sb("CF", [128, 1024])
            pool.dma(CF[:, 0:128], self.a["cb"][:, 0:128], ck)
            pool.dma(CF[:, 128:1024], self.a["cb"][:, 384:1280], ck)
            pool.dma(CM[:, :], self.a["dil_count"], ck)
            cbt = act.fn(CB[:, :], CF[:, :], ACT.Copy, ck.tok())
            units = [(n, j, par) for n in range(4) for j in range(4) for par in range(2)]
            sfree, pfree, ptfree, pbfree, expt, pt_, evt, onfree, statfree = {}, {}, {}, {}, {}, {}, {}, {}, {}
            ofree = otfree = None
            for u in range(len(units) + 3):
                if u < len(units):
                    n, j, par = units[u]
                    r = slice(64 * par, 64 * par + 64)
                    b = u % 3
                    o = 384 - 128 * n
                    hs, s = 2 * j + par, n % 2
                    pe.mm(banks[b], Q[r, j, n * 128:(n + 1) * 128], K[r, j, :], True, True, sfree.get(b))
                    pe.mm(banks[b], CB[:, 0:128], CB[:, 128 + o:128 + o + 512], False, True, cbt, share=True)
                    t = dve.maxr(NM[:, s, hs:hs + 1], banks[b], pe.tok(), statfree.get(n - 2), negate=True)
                    expt[u] = sfree[b] = act.fn(P[:, u % 3, :], banks[b], ACT.Exp, t, pfree.get(u % 3),
                                                bias=NM[:, s, hs:hs + 1])
                if 1 <= u <= len(units):
                    v = u - 1
                    n, j, par = units[v]
                    o = 384 - 128 * n
                    hs, s = 2 * j + par, n % 2
                    x = P[:, v % 3, :]
                    pt_[v] = dve.stt(x, x, 1.0, CM[:, o:o + 512], ALU.mult, ALU.mult, expt[v], ck.tok(),
                                     acc=DEN[:, s, hs:hs + 1])
                    b = 3 + v % 2
                    for i in range(4):
                        pe.tr(banks[b][:, i * 128:(i + 1) * 128], P[:, v % 3, i * 128:(i + 1) * 128], self.ID,
                              pt_[v], pbfree.get(b))
                    pfree[v % 3] = pe.tok()
                    evt[v] = pbfree[b] = act.fn(PT[:, v % 3, :], banks[b], ACT.Copy, pfree[v % 3], ptfree.get(v % 3))
                if 2 <= u <= len(units) + 1:
                    v = u - 2
                    n, j, par = units[v]
                    hs, s = 2 * j + par, n % 2
                    for i in range(4):
                        pe.mm(banks[5][:, hs * 64:hs * 64 + 64], PT[:, v % 3, i * 128:(i + 1) * 128],
                              V[:, i, hs * 64:hs * 64 + 64], i == 0, i == 3, evt[v], ofree if hs == 0 and i == 0 else None)
                    ptfree[v % 3] = pe.tok()
                    if hs == 7:
                        t = dve.recip(DEN[:, s, :], DEN[:, s, :], pt_[v])
                        rb = DEN[:, s, :].rearrange("p (h o) -> p h o", o=1).broadcast_to([128, 8, 64])
                        t = ofree = statfree[n] = dve.tt(ON[:, s, :].rearrange("p (h d) -> p h d", d=64),
                                                         banks[5].rearrange("p (h d) -> p h d", d=64), rb,
                                                         ALU.mult, t, ptfree[v % 3], onfree.get(s))
                        for c in range(4):
                            pe.tr(banks[6][:, c * 128:(c + 1) * 128], ON[:, s, c * 128:(c + 1) * 128], self.ID, t, otfree)
                        onfree[s] = pe.tok()
                        otfree = act.fn(MIX[:, 4:8, n * 128:(n + 1) * 128], banks[6].rearrange("p (c t) -> p c t", t=128),
                                        ACT.Copy, onfree[s])


    def program(self):
        a = self.a
        st = self.stages
        self.setup()
        self.xready = None
        X = [(0, T, 0)]
        XC = [(0, T, 0), (T, T + TC, 1)]
        with self.scope() as sc:
            self.mod_ring(sc)
            for blk in range(3):
                for third in range(3):
                    if (blk, third) == (0, 0) or "f0" not in st:
                        self.run_jobs(self.mod_jobs(blk, third, 7))
        more = (lambda *bt: [j for b, t in bt for j in self.mod_jobs(b, t, 7)]) if "f0" in st else (lambda *bt: [])
        if "f0" in st:
            self.ffn(0, XC, a["ffn1_wi"][0], a["ffn1_wo"][0], more((0, 1), (0, 2)))
        if "m0" in st:
            self.mixer_ab(1)
        if "f1" in st:
            self.ffn(2, X, a["ffn2_wi"][0], a["ffn2_wo"][0], more((1, 0)))
        if "f2" in st:
            self.ffn(3, X, a["ffn1_wi"][1], a["ffn1_wo"][1], more((1, 1), (1, 2)))
        if "m1" in st:
            self.mixer_pool(4)
        if "f3" in st:
            self.ffn(5, X, a["ffn2_wi"][1], a["ffn2_wo"][1], more((2, 0)))
        if "n1" in st:
            self.final_norm("final_g")
        if "f4" in st:
            self.ffn(6, X, a["w_gu1_2"], a["w_down1_2"], more((2, 1), (2, 2)))
        if "m2" in st:
            self.mixer_hybrid(7)
        if "f5" in st:
            self.ffn(8, X, a["w_gu2_2"], a["w_down2_2"], [])
        if "n2" in st:
            self.final_norm("g_final_2")
        c = self.chan()
        self.barrier()
        self.sp.dma(a["out"], self.XT[:, :, 0:T], c, self.dve.tok())
        if "out_ctx" in a:
            self.sp.dma(a["out_ctx"], self.XT[:, :, T:T + TC], c)
        self.sp.wait(c.tok())

        block = self.ctx.enter_context(self.nc.Block())
        for name, q in (("sync", self.sp), ("tensor", self.pe), ("scalar", self.act), ("vector", self.dve),
                        ("gpsimd", self.pool)):
            if q.items:
                self.attach(block, name, q)

    def attach(self, block, name, q):
        on = {"sync": block.sync, "tensor": block.tensor, "scalar": block.scalar, "vector": block.vector,
              "gpsimd": block.gpsimd}[name]

        @on
        def _(eng):
            q.emit(eng)


ALL = ("f0", "m0", "f1", "f2", "m1", "f3", "n1", "f4", "m2", "f5", "n2")


def build(nc, a, stages=ALL):
    with ExitStack() as ctx:
        Program(nc, ctx, a, stages).program()



def cols(w):
    k, n = w.shape
    return np.ascontiguousarray(w.reshape(k // 128, 128, n // 128, 128).transpose(2, 1, 0, 3)).reshape(n // 128, 128, k)


def feat(v):
    return np.ascontiguousarray(v.reshape(-1, 128).T)


def constants():
    k = {}
    one = np.ones((128, 128), np.float32)
    idn = np.eye(128, dtype=np.float32)
    k["consts"] = np.concatenate([one, idn], axis=1)
    t = np.arange(T)
    cnt = []
    for w in (2, 4, 8, 16):
        lo, hi = np.maximum(t - w // 2, 0), np.minimum(t + (w - w // 2), T)
        cnt.append(1.0 / (hi - lo))
    k["pool_cnt"] = np.ascontiguousarray(np.broadcast_to(np.array(cnt, np.float32)[None], (128, 4, T)))
    i, j = np.arange(128)[:, None], np.arange(128)[None, :]
    left = np.where(j >= i, 0.0, -BIG)
    right = np.where(j <= i, 0.0, -BIG)
    y = np.arange(896)[None, :] - 384 - i
    near = [(np.abs(y) % d == 0) & (np.abs(y) // d <= 64) for d in (1, 4, 16)]
    count = near[0].astype(np.float32) + near[1] + near[2]
    add = np.where(count > 0, 0.0, -BIG)
    k["cb"] = np.concatenate([idn, left, right, add], axis=1).astype(np.float32)
    k["dil_count"] = np.ascontiguousarray(count.astype(np.float32))
    pos = np.arange(T)
    f = np.float32(10000.0) ** (-np.arange(16, dtype=np.float32) / np.float32(16))
    ang = [(pos // 64).astype(np.float32)[:, None] * f, (pos % 64).astype(np.float32)[:, None] * f]
    head = np.concatenate([np.concatenate([t_, t_], axis=1) for t_ in ang], axis=1).T
    ang = np.concatenate([head, head], axis=0)
    k["rope1"] = np.ascontiguousarray(np.stack([np.cos(ang), np.sin(ang)], axis=1).astype(np.float32))
    perm = np.zeros((128, 128), np.float32)
    for p in range(128):
        if p % 32 < 16:
            perm[p + 16, p] = -1.0
        else:
            perm[p - 16, p] = 1.0
    k["perm1"] = perm
    m = np.zeros((128, 2, 2, 64), np.int32)
    jj, ii = (np.arange(128) % 64)[:, None, None], np.arange(64)[None, None, :]
    m[:, 0] = jj <= ii
    m[:, 1] = jj >= ii
    k["gla_mask"] = m.reshape(128, 256)
    f = np.float32(500000.0) ** (-2.0 * np.arange(8, dtype=np.float32) / np.float32(16)).astype(np.float32)
    ang = pos.astype(np.float32)[:, None] * f
    c, s = np.ones((64, T), np.float32), np.zeros((64, T), np.float32)
    c[0:16], s[0:16] = np.tile(np.cos(ang).T, (2, 1)), np.tile(np.sin(ang).T, (2, 1))
    k["rope2"] = np.ascontiguousarray(np.stack([np.tile(c, (2, 1)), np.tile(s, (2, 1))], axis=1))
    perm = np.zeros((128, 256), np.float32)
    for p in range(128):
        if p % 64 < 8:
            perm[p + 8, p] = -1.0
        elif p % 64 < 16:
            perm[p - 8, p] = 1.0
        perm[64 * (p // 64):64 * (p // 64) + 64, 128 + p] = 1.0
    k["perm2"] = perm
    sel = np.zeros((4, 4, 128), np.float32)
    oh = np.zeros((128, 4, 4), np.float32)
    for h in range(4):
        sel[h, h] = 1.0
        oh[:, h, h] = 1.0
    k["sel"], k["onehot"] = sel, oh
    k["tri"] = np.ascontiguousarray(np.stack([np.where(i <= j, 0.0, BIG), np.where(i >= j, 0.0, BIG)], axis=1).astype(np.float32))
    return k


def arrange(i):
    f = {}
    vecs = []
    for name, n in VEC:
        v = np.asarray(i[name], np.float32)
        if name in ("g_q_2", "g_k_2"):
            v = np.tile(v.reshape(64, 1), (2, 1))
        elif name == "gate_bias_2":
            p = np.zeros((128, 4), np.float32)
            p[0:4] = v.reshape(4, 4).T
            v = p
        elif name == "sink":
            p = np.zeros((128, 1), np.float32)
            p[0:8, 0] = v.reshape(8)
            v = p
        else:
            v = feat(v.reshape(-1))
        assert v.shape == (128, n), name
        vecs.append(v)
    f["vecs"] = np.ascontiguousarray(np.concatenate(vecs, axis=1))
    tr = lambda x: np.ascontiguousarray(x[0].T.reshape(8, 128, -1).transpose(1, 0, 2))
    f["x_in"] = tr(i["x"])
    f["ctx_in"] = tr(i["ctx"])
    f["w_mod"] = i["w_mod"]
    f["w_ada_2"] = i["w_ada_2"][0]
    for n in ("ffn1_wi", "ffn2_wi"):
        f[n] = np.stack([cols(i[n][l]) for l in range(2)])
    for n in ("ffn1_wo", "ffn2_wo"):
        f[n] = i[n].reshape(2, NF, 128, D)
    f["w_gu1_2"] = cols(i["w_gu1_2"][0])
    f["w_gu2_2"] = cols(i["w_gu2_2"][0])
    f["w_down1_2"] = i["w_down1_2"].reshape(NF, 128, D)
    f["w_down2_2"] = i["w_down2_2"].reshape(NF, 128, D)
    f["pool_w"] = np.ascontiguousarray(i["w_pool"][0].reshape(4, 2, 128, 256).transpose(2, 0, 1, 3))
    w = i["w_in"][0]
    q = w[:, 0:512].reshape(D, 8, 64)
    q = np.stack([q[:, [j, j + 4]] for j in range(4)], axis=1).reshape(D, 512)
    f["w_in"] = cols(np.concatenate([q, w[:, 512:], np.zeros((D, 96), np.float32)], axis=1))
    wa = np.zeros((32, 2, 256), np.float32)
    wa[0:16, 0] = i["w_a2_f"][0]
    wa[16:32, 1] = i["w_a2_b"][0]
    f["wa2"] = wa
    w = i["w_out"][0]
    o = w[0:512].reshape(8, 64, D)
    o = np.stack([o[[j, j + 4]] for j in range(4)]).reshape(512, D)
    f["w_out"] = cols(np.concatenate([o, w[512:]]))
    w = i["w_in_2"][0]
    g = np.zeros((D, 4, 32), np.float32)
    g[:, :, 0:4] = w[:, 1536:1552].reshape(D, 4, 4)
    f["w_in_2"] = cols(np.concatenate([w[:, 0:1536], g.reshape(D, 128), w[:, 1552:]], axis=1))
    f["w_out_2"] = cols(i["w_out_2"][0])
    f.update(constants())
    return f


def kernel(**inputs):
    import concourse.bacc as bacc
    from concourse.bass_utils import run_bass_kernel_spmd

    inputs = {k: np.asarray(v) for k, v in inputs.items()}
    nc = bacc.Bacc("TRN2", target_bir_lowering=False, num_devices=1)
    arrays, a = {}, {}
    for name, v in arrange(inputs).items():
        arrays[f"in_{name}"] = v
        a[name] = nc.dram_tensor(f"in_{name}", v.shape, mybir.dt.from_np(v.dtype), kind="ExternalInput").ap()
    a["out"] = nc.dram_tensor("out_0", (128, 8, T), F32, kind="ExternalOutput").ap()
    build(nc, a)
    r = run_bass_kernel_spmd(nc, [arrays], core_ids=[0])
    o = np.asarray(r.results[0]["out_0"])
    return np.ascontiguousarray(o.transpose(2, 1, 0).reshape(1, T, D))
```

```python
from contextlib import ExitStack

import numpy as np

import concourse.bass as bass
from concourse import mybir

F32 = mybir.dt.float32
F32R = mybir.dt.float32r
BF16 = mybir.dt.bfloat16
I32 = mybir.dt.int32
ALU = mybir.AluOpType
ACT = mybir.ActivationFunctionType
AXX = mybir.AxisListType.X

D = 1024
T = 512
TC = 256
FF = 2816
NF = FF // 128
NRAW = 6
NUNIT = 5
EPS = 1e-6
BIG = 1e30

VEC = [("b_mod", 144), ("norm_g", 48), ("pool_scale", 8), ("final_g", 8), ("gla_g", 1),
       ("c", 8), ("c_ctx", 8), ("b_a_f", 2), ("b_a_b", 2), ("c_2", 8), ("b_ada_2", 72),
       ("g_ffn1_2", 8), ("g_mix_2", 8), ("g_ffn2_2", 8), ("g_final_2", 8), ("g_mh_2", 4),
       ("g_q_2", 1), ("g_k_2", 1), ("gate_bias_2", 4), ("sink", 1)]
VOFF = {}
_o = 0
for _n, _c in VEC:
    VOFF[_n] = _o
    _o += _c
NV = _o

AQ, AK, AV, GQ, GK, GV, GR, GZ = 0, 4, 5, 6, 8, 10, 14, 18
NIN1 = 19
MQ, MK, MV, MO, MG, DQ, DK, DV = 0, 2, 4, 8, 12, 13, 17, 21
NIN2 = 25


class Queue:

    def __init__(self, sem):
        self.sem, self.n, self.items = sem, 0, []

    def put(self, fn, *after):
        self.items.append([fn, after, None])

    def do(self, fn, *after):
        self.items.append([fn, after, (self.sem, 1)])
        self.n += 1
        return (self.sem, self.n)

    def tt(self, o, x, y, op, *after):
        return self.do(lambda e: e.tensor_tensor(o, x, y, op), *after)

    def stt(self, o, x, s, y, op0, op1, *after, acc=None):
        return self.do(lambda e: e.scalar_tensor_tensor(o, x, s, y, op0, op1, accum_out=acc) if acc is not None
                       else e.scalar_tensor_tensor(o, x, s, y, op0, op1), *after)

    def ts(self, o, x, s1, s2, op0, op1, *after):
        return self.do(lambda e: e.tensor_scalar(o, x, s1, s2, op0, op1) if op1 is not None
                       else e.tensor_scalar(o, x, s1, s2, op0), *after)

    def cp(self, o, x, *after):
        return self.do(lambda e: e.tensor_copy(o, x), *after)

    def recip(self, o, x, *after):
        return self.do(lambda e: e.reciprocal(o, x), *after)

    def maxr(self, o, x, *after, negate=False):
        return self.do(lambda e: e.tensor_reduce(o, x, AXX, ALU.max, negate=negate), *after)

    def scan(self, o, m, x, init, op0, op1, *after):
        return self.do(lambda e: e.tensor_tensor_scan(o, m, x, init, op0, op1), *after)

    def fill(self, o, v, *after):
        return self.do(lambda e: e.memset(o, v), *after)

    def fn(self, o, x, f, *after, bias=0.0, scale=1.0, acc=None):
        return self.do(lambda e: e.activation(o, x, f, bias=bias, scale=scale, accum_out=acc) if acc is not None
                       else e.activation(o, x, f, bias=bias, scale=scale), *after)

    def mm(self, o, l, r, start, stop, *after, share=False):
        self.put(lambda e: e.matmul(o, l, r, start=start, stop=stop, skip_group_check=share), *after)

    def tr(self, o, x, ident, *after):
        self.put(lambda e: e.transpose(o, x, ident), *after)

    def tok(self):
        last = next((i for i in reversed(self.items) if i[0] is not None), None)
        if last is None:
            return None
        if last[2] is None:
            last[2] = (self.sem, 1)
            self.n += 1
        return (self.sem, self.n)

    def wait(self, *after):
        self.items.append([None, after, None])

    def dma(self, out, in_, chan, *after):
        self.items.append([lambda e: e.dma_start(out, in_), after, (chan.sem, 16)])
        chan.n += 16
        return (chan.sem, chan.n)

    def emit(self, eng):
        seen = {}

        def wait(a):
            if a is None:
                return
            if callable(a):
                a = a()
            if isinstance(a, list):
                for b in a:
                    wait(b)
                return
            if a is None:
                return
            sem, v = a
            if seen.get(id(sem), 0) < v:
                eng.wait_ge(sem, v)
                seen[id(sem)] = v

        for fn, after, sig in self.items:
            for a in after:
                wait(a)
            if fn is not None:
                ins = fn(eng)
                if sig is not None:
                    ins.then_inc(*sig)


class Chan:

    def __init__(self, sem):
        self.sem, self.n = sem, 0

    def tok(self):
        return (self.sem, self.n)


class Load:

    def __init__(self, view, ready):
        self.view, self.ready, self.free = view, ready, None


class Unit:

    def __init__(self, hi, lo, ready):
        self.hi, self.lo, self.ready, self.free = hi, lo, ready, None


class Job:

    def __init__(self, srcs, run, raw=False):
        self.srcs, self.run, self.raw, self.tiles = srcs, run, raw, None


class Program:
    def __init__(self, nc, ctx, a, stages):
        self.nc, self.ctx, self.a, self.stages = nc, ctx, a, stages
        sem = lambda n: ctx.enter_context(nc.semaphore(n))
        self.pe, self.act, self.dve, self.pool = (Queue(sem(f"s_{n}")) for n in ("pe", "act", "dve", "pool"))
        self.sp = Queue(None)
        self.free_sems = [sem(f"s_m{i}") for i in range(60)]
        self.rawc = [Chan(sem(f"s_raw{i}")) for i in range(NRAW)]
        self.loads = []
        self.units = []
        self.stackno = 0
        self.banks = []
        for i in range(4):
            t = ctx.enter_context(nc.psum_tensor(f"ps{i}", [128, 1024], F32))
            self.banks += [t[:, 0:512], t[:, 512:1024]]
            if i == 0:
                self.wide = []
            self.wide.append(t)
        self.XT = self.sb(ctx, "XT", [128, 8, T + TC], F32)
        self.RAW = self.sb(ctx, "RAW", [128, NRAW, 1024], F32)
        self.VT = self.sb(ctx, "VT", [128, NV], F32)
        self.K = self.sb(ctx, "K", [128, 268], F32)
        self.ONE, self.ID = self.K[:, 0:128], self.K[:, 128:256]
        self.MOD = self.sb(ctx, "MOD", [128, 9, 2, 24], F32)
        self.DER = self.sb(ctx, "DER", [128, 9, 3, 16], F32)
        self.SC = self.sb(ctx, "SC", [128, 8, 3], F32)
        self.ring_at = nc.sbuf_base
        self.WH = self.sb(ctx, "WH", [128, NUNIT, 1024], F32R)
        self.WL = self.sb(ctx, "WL", [128, NUNIT, 1024], F32R)
        self.SQ = self.sb(ctx, "SQ", [128, 2, T + TC], F32)
        self.SA = self.sb(ctx, "SA", [128, T + TC], F32)
        self.R6 = self.sb(ctx, "R6", [6, 128], F32)
        self.SEL6 = self.sb(ctx, "SEL6", [6, 6, 128], F32)
        self.nunit = NUNIT
        self.modt = {}
        self.modread = None
        self.sqfree, self.safree, self.sat = [None, None], None, None
        self.tiles0, self.next = None, []
        self.later = []

    def sb(self, ctx, name, shape, dt):
        return ctx.enter_context(self.nc.sbuf_tensor(name, shape, dt))

    def over_ring(self, name, shape, dt, offset):
        return self.nc.alloc_sbuf_tensor_at(self.name(name), shape, dt, offset=self.ring_at + offset)

    def chan(self):
        return Chan(self.free_sems.pop())

    def scope(self):
        self.stackno += 1
        return ExitStack()

    def name(self, s):
        return f"{s}_{self.stackno}"

    def barrier(self):
        es = [self.pe, self.act, self.dve, self.pool]
        toks = [e.tok() for e in es if e.items]
        for e in es:
            e.wait(toks)

    def vec(self, name, i=0, n=1):
        o = VOFF[name] + i
        return self.VT[:, o:o + n]


    def load(self, src):
        i = len(self.loads)
        prev = self.loads[i - NRAW] if i >= NRAW else None
        view = self.RAW[:, i % NRAW, :]
        ready = self.sp.dma(view, src, self.rawc[i % NRAW], (lambda: prev.free) if prev else None)
        ld = Load(view, ready)
        self.loads.append(ld)
        return ld

    def split(self, ld):
        i = len(self.units)
        prev = self.units[i - self.nunit] if i >= self.nunit else None
        hi, lo = self.WH[:, i % self.nunit, :], self.WL[:, i % self.nunit, :]
        th = self.act.do(lambda e: e.activation(hi, ld.view, ACT.Copy), ld.ready, prev.free if prev else None)
        tl = self.dve.do(lambda e: e.tensor_tensor(lo, ld.view, hi.bitcast(F32), ALU.subtract), th)
        ld.free = [th, tl]
        u = Unit(hi, lo, [th, tl])
        self.units.append(u)
        return u

    def unit_ring(self, n):
        self.WH = self.over_ring("WH", [128, n, 1024], F32R, 0)
        self.WL = self.over_ring("WL", [128, n, 1024], F32R, n * 4096)
        self.nunit, self.units = n, []

    def prepare(self, job):
        job.tiles = [self.load(s) for s in job.srcs]
        if not job.raw:
            job.tiles = [self.split(t) for t in job.tiles]

    def run_jobs(self, jobs):
        if self.tiles0 is not None:
            jobs[0].tiles, self.tiles0 = self.tiles0, None
        elif not jobs[0].raw:
            self.prepare(jobs[0])
        main = [j for j, job in enumerate(jobs) if not job.raw]
        after = dict(zip(main, main[1:]))
        for j, job in enumerate(jobs):
            if job.raw:
                if job.tiles is None:
                    self.prepare(job)
                if j + 1 < len(jobs) and jobs[j + 1].raw:
                    self.prepare(jobs[j + 1])
                job.run(job.tiles)
                continue
            if j in after:
                self.prepare(jobs[after[j]])
            elif self.next:
                self.tiles0 = [self.split(self.load(s)) for s in self.next]
                self.next = []
            if j + 1 < len(jobs) and jobs[j + 1].raw:
                self.prepare(jobs[j + 1])
            before, self.later = self.later, []
            job.run(job.tiles)
            for _, f in before:
                f()
        self.finish_rows()

    def mm3(self, out, w, x, first, last, *after):
        wh, wl = w
        xh, xl = x
        self.pe.put(lambda e: e.matmul(out, wh, xh, start=first, stop=False), *after)
        self.pe.put(lambda e: e.matmul(out, wh, xl, start=False, stop=False))
        self.pe.put(lambda e: e.matmul(out, wl, xh, start=False, stop=last))

    def mm2(self, out, w, x, first, last, *after):
        wh, wl = w
        self.pe.put(lambda e: e.matmul(out, wh, x, start=first, stop=True, skip_group_check=not first), *after)
        self.pe.put(lambda e: e.matmul(out[:, 0:TC], wl, x[:, 0:TC], start=False, stop=True, skip_group_check=True))


    def setup(self):
        a, sp = self.a, self.sp
        c = self.chan()
        sp.dma(self.VT[:, :], a["vecs"], c)
        sp.dma(self.K[:, :], a["consts"], c)
        sp.dma(self.SEL6[:, :, :], a["sel6"], c)
        cx = self.chan()
        sp.dma(self.XT[:, :, 0:T], a["x_in"], cx)
        sp.dma(self.XT[:, :, T:T + TC], a["ctx_in"], cx)
        for q in (self.pe, self.act, self.dve, self.pool):
            q.wait(c.tok())
        for q in (self.act, self.dve):
            q.wait(cx.tok())
        self.Z11, self.EPSC = self.K[:, 256:267], self.K[:, 267:268]
        for i, n in enumerate(("c", "c_ctx", "c_2")):
            self.act.do(lambda e, i=i, n=n: e.activation(self.SC[:, :, i], self.vec(n, 0, 8), ACT.Silu))
        self.sct = self.act.tok()


    def mod_ring(self, ctx):
        self.ACC = self.sb(ctx, self.name("ACC"), [128, 2, D], F32)
        self.accfree, self.acct = [None, None], [None, None]

    def mod_conds(self, blk, row):
        return (0, 1) if blk == 0 and row < 5 else ((0,) if blk < 2 else (2,))

    def mod_jobs(self, blk, rows, bank=7):
        src = self.a["w_mod"][blk] if blk < 2 else self.a["w_ada_2"]
        PS = self.banks[bank]
        jobs = []
        for row in rows:
            conds = self.mod_conds(blk, row)
            for k in range(8):
                def run(tiles, row=row, k=k, conds=conds):
                    ld = tiles[0]
                    ld.free = []
                    for n, c in enumerate(conds):
                        n = n if len(conds) == 2 else row % 2
                        self.mod_add(n, c, k, ld, k == 0)
                    if k < 7:
                        return
                    slots = (0, 1) if len(conds) == 2 else (row % 2,)
                    toks = [self.acct[n] for n in slots]
                    self.later.append((slots, lambda: self.mod_rows(blk, row, PS, slots, toks)))
                jobs.append(Job([src[k * 128:(k + 1) * 128, row * D:(row + 1) * D]], run, raw=True))
        return jobs

    def mod_rows(self, blk, row, PS, slots, toks):
        for i, n in enumerate(slots):
            for f in range(8):
                o = (row % 2) * 16 + 2 * f + i
                self.pe.mm(PS[:, o:o + 1], self.ACC[:, n, f * 128:(f + 1) * 128], self.ONE[:, 0:1],
                           True, True, toks[i], self.modread)
            self.accfree[n] = self.pe.tok()
        self.mod_done(blk, row, PS, len(slots), self.pe.tok())

    def finish_rows(self):
        now, self.later = self.later, []
        for _, f in now:
            f()

    def mod_add(self, n, c, k, ld, first):
        acc, sc = self.ACC[:, n, :], self.SC[:, k, c:c + 1]
        if first:
            if any(n in slots for slots, _ in self.later):
                self.finish_rows()
            t = self.dve.ts(acc, ld.view, sc, None, ALU.mult, None, ld.ready, self.sct, self.accfree[n])
        else:
            t = self.dve.stt(acc, ld.view, sc, acc, ALU.mult, ALU.add, ld.ready, self.acct[n])
        self.acct[n] = t
        ld.free.append(t)

    def mod_first(self):
        src = self.a["w_mod"][0]
        PS = self.banks[7]
        for row in range(2):
            for k in range(8):
                ld = self.load(src[k * 128:(k + 1) * 128, row * D:(row + 1) * D])
                ld.free = []
                if k % 4 == 3:
                    for f in range(8):
                        o = row * 16 + 2 * f
                        self.pe.mm(PS[:, o:o + 2], ld.view[:, f * 128:(f + 1) * 128], self.SC[:, k, 0:2],
                                   row == 0 and k == 3 and f == 0, True, ld.ready, self.sct, share=True)
                    ld.free.append(self.pe.tok())
                else:
                    for n in range(2):
                        self.mod_add(n, n, k, ld, k == 0)
            for n in range(2):
                for f in range(8):
                    o = row * 16 + 2 * f + n
                    self.pe.mm(PS[:, o:o + 1], self.ACC[:, n, f * 128:(f + 1) * 128], self.ONE[:, 0:1],
                               False, True, self.acct[n], share=True)
                self.accfree[n] = self.pe.tok()
        for row in range(2):
            self.mod_done(0, row, PS, 2, self.pe.tok())

    def mod_done(self, blk, row, PS, ncond, done):
        third, jj = row // 3, row % 3
        i = 3 * blk + third
        dve = self.dve
        bias = self.vec("b_mod" if blk < 2 else "b_ada_2", (blk if blk < 2 else 0) * 72 + 8 * row, 8)
        g = self.vec("norm_g", 24 * blk + 8 * third, 8) if blk < 2 else self.vec(("g_ffn1_2", "g_mix_2", "g_ffn2_2")[third], 0, 8)
        for j in range(ncond):
            pv = PS[:, (row % 2) * 16 + j:(row % 2) * 16 + 16:2]
            M, R = self.MOD[:, i, j, 8 * jj:8 * jj + 8], self.DER[:, i, :, 8 * j:8 * j + 8]
            t = self.modread = dve.tt(M, pv, bias, ALU.add, done)
            if jj == 1:
                t = dve.stt(R[:, 0, :], M, 1.0, g, ALU.add, ALU.mult, t)
            elif jj == 2 and blk == 1 and third == 1:
                t = dve.tt(R[:, 2, :], M, self.vec("pool_scale", 0, 8), ALU.mult, t)
            elif jj == 2:
                t = dve.ts(R[:, 2, :], M, 1.0 if third == 1 else 0.5, None, ALU.mult, None, t)
        self.modt[i, jj] = t

    def mod_a(self, i, k, j=0):
        return self.DER[:, i, 0, 8 * j + k:8 * j + k + 1]

    def mod_b(self, i, k, j=0):
        return self.MOD[:, i, j, k:k + 1]

    def mod_g(self, i, k, j=0):
        return self.DER[:, i, 2, 8 * j + k:8 * j + k + 1]


    def rstd_of(self, ctx, name, n, ss, width, done, parts=128):
        R = self.sb(ctx, self.name(name), [128, n], F32)
        return R, self.rstd_into(R[0:parts, :], ss, width, done)

    def rstd_into(self, R, ss, width, done):
        t = self.act.do(lambda e: e.activation(R, ss, ACT.Sqrt, scale=1.0 / width, bias=self.EPSC[0:R.shape[0], :]), done)
        return self.dve.do(lambda e: e.reciprocal(R, R), t)

    def sums(self, k, w, ready):
        s = k % 2
        dst = self.SA[:, 0:w] if k == 0 else self.SQ[:, s, 0:w]
        t = self.act.fn(dst, self.XT[:, k, 0:w], ACT.Square, ready, self.safree if k == 0 else self.sqfree[s], self.sat)
        if k > 0:
            t = self.sqfree[s] = self.dve.tt(self.SA[:, 0:w], self.SA[:, 0:w], dst, ALU.add, t, self.sat)
        self.sat = t

    def rstd(self, nq):
        pe = self.pe
        out = self.banks[7][0:6, 256:384]
        for q in range(nq):
            pe.mm(out, self.Z11[:, 5 - q:11 - q], self.SA[:, q * 128:(q + 1) * 128], q == 0, True,
                  self.sat, self.modread, share=q > 0)
        self.safree = pe.tok()
        t = self.rstd_into(self.R6[:, :], out, 1024, self.safree)
        for q in range(nq):
            pe.mm(self.banks[4 + q // 4][:, (q % 4) * 128:(q % 4) * 128 + 128],
                  self.SEL6[:, q, :], self.R6[:, :], True, True, t)
        return pe.tok()

    def norm(self, segs, emit):
        rt = self.rstd(segs[-1][1] // 128)
        for n, (c0, c1, j) in enumerate(segs):
            for k in range(8):
                emit(k, c0, c1, j, self.banks[4 + n][:, 0:c1 - c0], rt)

    def norm_split(self, ctx, mi, segs):
        self.HH = self.sb(ctx, self.name("HH"), [128, 8, T], F32R)
        self.HL = self.sb(ctx, self.name("HL"), [128, 8, T], F32R)
        if len(segs) == 2:
            self.HC = self.sb(ctx, self.name("HC"), [128, 8, 2 * TC], F32R)
        self.ht = {}

        def emit(k, c0, c1, j, R, rt):
            s = k % 2
            t_ = self.SQ[:, s, 0:c1 - c0]
            hh, hl = (self.HH[:, k, :], self.HL[:, k, :]) if c0 == 0 else (self.HC[:, k, 0:TC], self.HC[:, k, TC:2 * TC])
            t1 = self.dve.do(lambda e: e.scalar_tensor_tensor(t_, self.XT[:, k, c0:c1], self.mod_a(mi, k, j), R,
                                                              ALU.mult, ALU.mult),
                             rt, self.modt[mi, 0], self.modt[mi, 1], self.sqfree[s])
            t2 = self.act.do(lambda e: e.activation(hh, t_, ACT.Identity, bias=self.mod_b(mi, k, j)), t1)
            low()

            def rest():
                t3 = self.dve.do(lambda e: e.scalar_tensor_tensor(hl, t_, self.mod_b(mi, k, j), hh.bitcast(F32),
                                                                  ALU.add, ALU.subtract), t2)
                self.sqfree[s] = t3
                self.ht[k, c0] = [t2, t3]
            pending.append(rest)

        pending = []

        def low():
            while pending:
                pending.pop()()

        self.norm(segs, emit)
        low()

    def product(self, out, u, c0, first, last, ws, x, *after):
        w = (u.hi[:, ws], u.lo[:, ws])
        (self.mm3 if c0 == 0 else self.mm2)(out, w, x, first, last, *after)

    def h(self, k, c0):
        return (self.HH[:, k, :], self.HL[:, k, :]) if c0 == 0 else self.HC[:, k, :]


    def ffn(self, mi, segs, wi, wo, extra, early=()):
        with self.scope() as ctx:
            self.barrier()
            w = segs[-1][1]
            two = len(segs) == 2
            if not early:
                self.mod_ring(ctx)
            NG = 5
            self.norm_split(ctx, mi, segs)
            GH = self.sb(ctx, self.name("GH"), [128, NG, T], F32R)
            GL = self.sb(ctx, self.name("GL"), [128, NG, T], F32R)
            GC = self.sb(ctx, self.name("GC"), [128, NG, 2 * TC], F32R) if two else None
            S = self.sb(ctx, self.name("S"), [128, 2, w], F32)
            SX = self.sb(ctx, self.name("SX"), [128, TC], F32) if two else None
            ub, db = [0, 1, 2, 3], [4, 5, 6]
            ufree, dfree = {b: None for b in ub}, {b: None for b in db}
            for b in (4, 5):
                dfree[b] = self.dve.tok()
            cnt = {"u": 0, "d": 0}
            gfree, gready, sfree = {}, {}, {}
            act, dve = self.act, self.dve

            def gv(c, c0):
                return (GH[:, c % NG, :], GL[:, c % NG, :]) if c0 == 0 else GC[:, c % NG, :]

            def up(c):
                def run(tiles):
                    for q, u in enumerate(tiles):
                        for c0, c1, j in segs:
                            b = ub[cnt["u"] % len(ub)]
                            cnt["u"] += 1
                            out = self.banks[b]
                            for k in range(8):
                                self.product(out, u, c0, k == 0, k == 7, slice(k * 128, (k + 1) * 128), self.h(k, c0),
                                             u.ready, self.ht[k, c0], ufree[b] if k == 0 else None)
                            done = self.pe.tok()
                            u.free = done
                            s = S[:, c % 2, c0:c1]
                            if q == 0 and c0 == 0:
                                t = act.fn(s, out, ACT.Silu, done, sfree.get((c % 2, c0)))
                                ufree[b] = t
                                sfree[c, c0, "t"] = t
                            elif q == 0:
                                t = act.fn(s, out[:, TC:2 * TC], ACT.Copy, done, sfree.get((c % 2, c0)))
                                t = ufree[b] = dve.tt(s, s, out[:, 0:TC], ALU.add, done, t)
                                sfree[c, c0, "t"] = act.fn(s, s, ACT.Silu, t)
                            else:
                                if c0 == 0:
                                    t = ufree[b] = dve.tt(s, s, out, ALU.mult, done, sfree[c, c0, "t"])
                                    gh, gl = gv(c, c0)
                                else:
                                    t = act.fn(SX[:, :], out[:, TC:2 * TC], ACT.Copy, done, sfree.get("sx"))
                                    t = ufree[b] = dve.tt(SX[:, :], SX[:, :], out[:, 0:TC], ALU.add, done, t)
                                    t = sfree["sx"] = dve.tt(s, s, SX[:, :], ALU.mult, t, sfree[c, c0, "t"])
                                    gh, gl = GC[:, c % NG, 0:TC], GC[:, c % NG, TC:2 * TC]
                                t1 = act.fn(gh, s, ACT.Copy, t, gfree.get(c - NG))
                                t2 = dve.tt(gl, s, gh.bitcast(F32), ALU.subtract, t1)
                                sfree[c % 2, c0] = t2
                                gready[c, c0] = [t1, t2]
                return Job([wi[c], wi[NF + c]], run)

            def down(fs):
                def run(tiles):
                    for d in range(8):
                        for c0, c1, j in segs:
                            b = db[cnt["d"] % len(db)]
                            cnt["d"] += 1
                            out = self.banks[b]
                            ws = slice(d * 128, (d + 1) * 128)
                            for i, (f, u) in enumerate(zip(fs, tiles)):
                                self.product(out, u, c0, i == 0, i == len(fs) - 1, ws, gv(f, c0),
                                             u.ready, gready[f, c0], dfree[b] if i == 0 else None)
                            done = self.pe.tok()
                            x = self.XT[:, d, c0:c1]
                            for o in ([out] if c0 == 0 else [out[:, 0:TC], out[:, TC:2 * TC]]):
                                dfree[b] = dve.stt(x, o, self.mod_g(mi, d, j), x, ALU.mult, ALU.add, done,
                                                   self.modt[mi, 2], dve.tok() if c0 else None)
                        if fs[-1] == NF - 1:
                            self.sums(d, w, dfree[b])
                    for u in tiles:
                        u.free = done
                    for f in fs:
                        gfree[f] = done
                return Job([wo[f] for f in fs], run)

            groups = [list(range(i, min(i + 3, NF))) for i in range(0, NF, 3)]
            jobs = []
            gi = 0
            for c in range(NF):
                jobs.append(up(c))
                if c < 2:
                    jobs += early[4 * c:4 * c + 4]
                while gi < len(groups) and groups[gi][-1] < c:
                    jobs.append(down(groups[gi]))
                    gi += 1
                n = len(extra) // (NF - c) if c > 1 else 0
                jobs += extra[:n]
                extra = extra[n:]
            for g in groups[gi:]:
                jobs.append(down(g))
            self.run_jobs(jobs)


    def final_norm(self, gname, store=None):
        self.barrier()
        last = []

        def emit(k, c0, c1, j, R, rt):
            t = self.dve.do(lambda e: e.scalar_tensor_tensor(
                self.XT[:, k, c0:c1], self.XT[:, k, c0:c1], self.vec(gname, k), R, ALU.mult, ALU.mult), rt)
            if store is None:
                self.sums(k, T, t)
            else:
                self.sp.dma(self.a["out"][:, k, :], self.XT[:, k, 0:T], store, t)

        self.norm([(0, T, 0)], emit)


    def projection(self, w, chunks, banks, segs_of, evac, XS=None):
        free = {b: None for b in banks}
        cnt = [0]
        xs = [None, None]

        def job(ch):
            def run(tiles):
                u = tiles[0]
                for c0, c1 in segs_of(ch):
                    b = banks[cnt[0] % len(banks)]
                    cnt[0] += 1
                    out = self.banks[b]
                    for k in range(8):
                        self.product(out, u, c0, k == 0, k == 7, slice(k * 128, (k + 1) * 128), self.h(k, c0),
                                     u.ready, self.ht[k, c0], free[b] if k == 0 else None)
                    done = self.pe.tok()
                    u.free = done
                    if c0 == 0:
                        free[b] = evac(ch, c0, c1, out, done)
                    else:
                        s = cnt[0] % 2
                        t = self.act.fn(XS[:, s, :], out[:, TC:2 * TC], ACT.Copy, done, xs[s])
                        t = free[b] = self.dve.tt(XS[:, s, :], XS[:, s, :], out[:, 0:TC], ALU.add, done, t)
                        xs[s] = evac(ch, c0, c1, XS[:, s, :], t)
            return Job([w[ch]], run)

        following, self.next = self.next, []
        self.run_jobs([job(ch) for ch in chunks])
        self.next = following

    def out_projection(self, mi, w, MIX, mready):
        with self.scope() as ctx:
            self.barrier()
            self.unit_ring(NUNIT)
            MH = self.sb(ctx, self.name("MH"), [128, 8, T], F32R)
            ML = self.sb(ctx, self.name("ML"), [128, 8, T], F32R)
            mt = []
            for k in range(8):
                t1 = self.act.do(lambda e, k=k: e.activation(MH[:, k, :], MIX[:, k, :], ACT.Copy), mready)
                t2 = self.dve.do(lambda e, k=k: e.tensor_tensor(ML[:, k, :], MIX[:, k, :], MH[:, k, :].bitcast(F32),
                                                                ALU.subtract), t1)
                mt.append([t1, t2])
            free = {}

            def job(d):
                def run(tiles):
                    u = tiles[0]
                    b = d % 3
                    out = self.banks[b]
                    for k in range(8):
                        ws = slice(k * 128, (k + 1) * 128)
                        self.mm3(out, (u.hi[:, ws], u.lo[:, ws]), (MH[:, k, :], ML[:, k, :]), k == 0, k == 7,
                                 u.ready, mt[k], free.get(b) if k == 0 else None)
                    u.free = self.pe.tok()
                    x = self.XT[:, d, 0:T]
                    free[b] = self.dve.do(lambda e: e.scalar_tensor_tensor(
                        x, out, self.mod_g(mi, d), x, ALU.mult, ALU.add), u.free, self.modt[mi, 2])
                    self.sums(d, T, free[b])
                return Job([w[d]], run)

            self.run_jobs([job(d) for d in range(8)])

    def mixer_pool(self, mi):
        PAD = 8
        W = T + 2 * PAD
        with self.scope() as ctx:
            self.tiles0, self.next = [self.split(self.load(w)) for w in self.next] or None, []
            self.barrier()
            sb = lambda n, s, dt=F32: self.sb(ctx, self.name(n), s, dt)
            H = sb("H", [128, 8, W])
            P2, P4, P8, PL = sb("P2", [128, 2, W]), sb("P4", [128, 2, W]), sb("P8", [128, 2, W]), sb("PL", [128, 2, T])
            CNT = sb("CNT", [128, 4, T])
            WP = sb("WP", [128, 4, 2, 256])
            cw = self.chan()
            self.pool.dma(CNT[:, :, :], self.a["pool_cnt"], cw)
            self.pool.dma(WP[:, :, :, :], self.a["pool_w"], cw)
            dve, act, pe = self.dve, self.act, self.pe
            z0 = dve.do(lambda e: e.memset(H[:, :, 0:PAD], 0.0))
            z1 = dve.do(lambda e: e.memset(H[:, :, PAD + T:W], 0.0))
            TT = sb("TN", [128, 2, 512])
            free = [None, None]
            ht = {}

            def emit(k, c0, c1, j, R, rt):
                s = k % 2
                t = dve.do(lambda e: e.scalar_tensor_tensor(TT[:, s, :], self.XT[:, k, 0:T], self.mod_a(mi, k), R,
                                                            ALU.mult, ALU.mult), rt, free[s],
                             self.modt[mi, 0], self.modt[mi, 1])
                free[s] = ht[k] = act.do(lambda e: e.activation(H[:, k, PAD:PAD + T], TT[:, s, :], ACT.Identity,
                                                                bias=self.mod_b(mi, k)), t)

            self.norm([(0, T, 0)], emit)
            add = lambda o, x, y, *w: dve.tt(o, x, y, ALU.add, *w)
            plfree = None
            bfree = {}
            for g in range(4):
                wt = [ht[2 * g], ht[2 * g + 1], z0, z1]
                h = lambda lo, hi, g=g: H[:, 2 * g:2 * g + 2, lo:hi]
                t = add(P2[:, :, 1:W], h(0, W - 1), h(1, W), wt)
                S, lo = P2, 0
                if g >= 1:
                    t = add(P4[:, :, 2:W - 1], P2[:, :, 1:W - 2], P2[:, :, 3:W], t)
                    S = P4
                if g >= 2:
                    t = add(P8[:, :, 4:W - 3], P4[:, :, 2:W - 5], P4[:, :, 6:W - 1], t)
                    S = P8
                if g >= 3:
                    t = add(P2[:, :, 8:8 + T], P8[:, :, 4:4 + T], P8[:, :, 12:12 + T], t)
                    S = P2
                cb = CNT[:, g:g + 1, :].broadcast_to([128, 2, T])
                t = dve.tt(PL[:, :, :], S[:, :, PAD:PAD + T], cb, ALU.mult, t, cw.tok(), plfree)
                t = dve.tt(PL[:, :, :], PL[:, :, :], h(PAD, PAD + T), ALU.subtract, t)
                for o in range(2):
                    b = 2 * (g % 2) + o
                    for i in range(2):
                        pe.put(lambda e, b=b, g=g, i=i, o=o: e.matmul(
                            self.banks[b], WP[:, g, i, o * 128:(o + 1) * 128], PL[:, i, :], start=(i == 0), stop=(i == 1)),
                            t, cw.tok(), bfree.get(b))
                    done = plfree = pe.tok()
                    k = 2 * g + o
                    x = self.XT[:, k, 0:T]
                    bfree[b] = dve.do(lambda e, x=x, b=b, k=k: e.scalar_tensor_tensor(
                        x, self.banks[b], self.mod_g(mi, k), x, ALU.mult, ALU.add), done, self.modt[mi, 2])
                    self.sums(k, T, bfree[b])


    def mixer_ab(self, mi):
        pe, act, dve, pool, a = self.pe, self.act, self.dve, self.pool, self.a
        W = T + TC
        with self.scope() as outer:
            self.barrier()
            sb = lambda n, s, dt=F32: self.sb(outer, self.name(n), s, dt)
            MIX = sb("MIX", [128, 8, T])
            QA, GRt = MIX[:, 0:4, :], MIX[:, 4:8, :]
            KA, VA = sb("KA", [128, W]), sb("VA", [128, 6, 128])
            GQt, GKt = sb("GQt", [128, 2, T]), sb("GKt", [128, 2, W])
            ZG = self.SA[0:32, :]
            VV = sb("VV", [128, 12, 2, 128])
            cc = self.chan()
            CB = sb("CB", [128, 384], BF16)
            WA = sb("WA", [32, 2, 256])
            pool.dma(WA[:, :, :], a["wa2"], cc)
            with ExitStack() as ctx:
                RT, TMP = MIX[:, 6:8, :], MIX[:, 5, :]
                XS = MIX[:, 4, :].rearrange("p (n t) -> p n t", t=TC)
                PR = self.sb(ctx, self.name("PR"), [128, 128], F32)
                pool.dma(RT, a["rope1"], cc)
                pool.dma(PR[:, :], a["perm1"], cc)
                segs = [(0, T, 0), (T, W, 1)]
                with ExitStack() as tmp:
                    CF = self.sb(tmp, self.name("CF"), [128, 384], F32)
                    pool.dma(CF[:, :], a["cb"][:, 0:384], cc)
                    act.fn(CB[:, :], CF[:, :], ACT.Copy, cc.tok())
                self.norm_split(ctx, mi, segs)
                VB = self.SQ[:, :, :]
                pfree = {6: None, 7: None}
                vbt, vbfree, nt = {}, {}, [0]
                tmpfree = [None]

                def tbank():
                    nt[0] += 1
                    return 6 + nt[0] % 2

                def rope(x, ready):
                    b = tbank()
                    pe.mm(self.banks[b], PR[:, :], x, True, True, ready, pfree[b], cc.tok())
                    t = dve.tt(TMP, self.banks[b], RT[:, 1, :], ALU.mult, pe.tok(), tmpfree[0], cc.tok())
                    pfree[b] = t
                    t2 = dve.tt(x, x, RT[:, 0, :], ALU.mult, pe.tok(), ready)
                    tmpfree[0] = dve.tt(x, x, TMP, ALU.add, t, t2)

                grfree = []

                def evac(ch, c0, c1, out, done):
                    if ch == GR:
                        grfree[:] = [dve.tok(), act.tok()]
                    if ch < AK:
                        t = act.fn(QA[:, ch, :], out, ACT.Copy, done)
                        rope(QA[:, ch, :], t)
                    elif ch == AK:
                        t = act.fn(KA[:, c0:c1], out, ACT.Copy, done)
                        if c0 == 0:
                            rope(KA[:, 0:T], t)
                    elif ch == AV:
                        t = act.fn(VB[:, 0, c0:c1], out, ACT.Copy, done, vbfree.get(0))
                        b = tbank()
                        n = (c1 - c0) // 128
                        for i in range(n):
                            pe.tr(self.banks[b][:, i * 128:(i + 1) * 128], VB[:, 0, c0 + i * 128:c0 + (i + 1) * 128],
                                  self.ID, t, pfree[b])
                        vbfree[0] = pe.tok()
                        pfree[b] = dve.cp(VA[:, c0 // 128:c0 // 128 + n, :],
                                          self.banks[b][:, 0:n * 128].rearrange("p (n f) -> p n f", f=128), vbfree[0])
                    elif ch < GK:
                        t = act.fn(GQt[:, ch - GQ, :], out, ACT.Copy, done)
                    elif ch < GV:
                        t = act.fn(GKt[:, ch - GK, c0:c1], out, ACT.Copy, done)
                    elif ch < GR:
                        pair, par = (ch - GV) // 2, (ch - GV) % 2
                        t = act.fn(VB[:, par, c0:c1], out, ACT.Copy, done, vbfree.get(par))
                        vbt[par, c0] = t
                        if par == 1 and c0 == T:
                            for q in range(3):
                                b = tbank()
                                for i in range(4):
                                    cl = (4 * q + i) * 64
                                    for pr in range(2):
                                        pe.mm(self.banks[b][64 * pr:64 * pr + 64, i * 128:(i + 1) * 128],
                                              VB[:, pr, cl:cl + 64], self.ID, True, True,
                                              vbt[pr, 0], vbt[pr, T], pfree[b])
                                vbfree[0] = vbfree[1] = pe.tok()
                                pfree[b] = dve.cp(VV[:, 4 * q:4 * q + 4, pair, :],
                                                  self.banks[b].rearrange("p (n f) -> p n f", f=128), vbfree[0])
                    elif ch < GZ:
                        t = act.fn(GRt[:, ch - GR, :], out, ACT.Silu, done, grfree)
                    else:
                        t = act.fn(ZG[:, c0:c1], out[0:32, :], ACT.Copy, done)
                    return t

                xc = lambda ch: [(0, T)] if ch < AK or GQ <= ch < GK or GR <= ch < GZ else [(0, T), (T, W)]
                self.projection(a["w_in"], [GZ, AV, AK, 0, 1, 2, 3] + list(range(GQ, GZ)), (0, 1, 2, 3), xc, evac, XS)
            self.window(outer, QA, KA, VA, CB, MIX)
            self.gla(outer, GQt, GKt, GRt, ZG, WA, VV, MIX, cc)
            self.out_ready = self.act.tok(), self.dve.tok()
            self.out_projection(mi, a["w_out"], MIX, list(self.out_ready))

    def window(self, outer, QA, KA, VA, CB, MIX):
        pe, act, dve = self.pe, self.act, self.dve
        IDB, ML = CB[:, 0:128], CB[:, 128:384]
        with ExitStack() as ctx:
            self.barrier()
            sb = lambda n, s: self.sb(ctx, self.name(n), s, F32)
            P, PT, ON = sb("P", [128, 2, 640]), sb("PT", [128, 3, 640]), sb("ON", [128, 2, 512])
            MX, NM, DEN, ES = (sb(n, [128, 2, 8]) for n in ("MX", "NM", "DEN", "ES"))
            SK, NSK, SD = sb("SK", [128, 8]), sb("NSK", [128, 8]), sb("SD", [8, 8])
            t = dve.ts(SD[:, :], self.ID[0:8, 0:8], self.VT[0:8, VOFF["sink"]:VOFF["sink"] + 1], None, ALU.mult, None)
            pe.mm(self.banks[7][:, 0:8], self.ONE[0:8, :], SD[:, :], True, True, t)
            t = dve.cp(SK[:, :], self.banks[7][:, 0:8], pe.tok())
            skt = dve.ts(NSK[:, :], SK[:, :], -1.0, None, ALU.mult, None, t)
            units = [(n, j, par) for n in range(4) for j in range(4) for par in range(2)]
            sfree, pfree, ptpfree, ptfree = {}, {}, None, {}
            expt, evt, pvt, maxt = {}, {}, {}, {}
            ofree, otfree, onfree = skt, skt, {}
            statfree = {}

            def blocks(n):
                return list(range(max(0, n - 1), min(4, n + 2)))

            for u in range(len(units) + 2):
                if u < len(units):
                    n, j, par = units[u]
                    rows = slice(64 * par, 64 * par + 64)
                    bl = blocks(n)
                    nk = 128 * len(bl)
                    w = self.wide[u % 2]
                    q = QA[rows, j, n * 128:(n + 1) * 128]
                    pe.mm(w[:, 512 - nk:512], q, KA[rows, bl[0] * 128:bl[0] * 128 + nk], True, True, sfree.get(u % 2))
                    edge = []
                    if n > 0:
                        edge.append((512 - nk, 0))
                    if n < 3:
                        edge.append((384, 1))
                    for i, (o, m) in enumerate(edge):
                        pe.mm(w[:, o:o + 128], IDB, ML[:, m * 128:(m + 1) * 128], False, True, share=True)
                    pe.mm(w[:, 512:768], q, KA[rows, T:T + TC], True, True)
                    ts_ = pe.tok()
                    hs = 2 * j + par
                    s = n % 2
                    view = w[:, 512 - nk:768]
                    tm = dve.maxr(MX[:, s, hs:hs + 1], view, ts_, statfree.get(n - 2))
                    h = j + 4 * par
                    tm = maxt[u] = dve.ts(NM[:, s, hs:hs + 1], MX[:, s, hs:hs + 1], -0.125, NSK[:, h:h + 1],
                                          ALU.mult, ALU.min, tm)
                    expt[u] = sfree[u % 2] = act.fn(P[:, u % 2, 0:nk + 256], view, ACT.Exp, tm, pfree.get(u % 2),
                                                    bias=NM[:, s, hs:hs + 1], scale=0.125, acc=DEN[:, s, hs:hs + 1])
                if 1 <= u <= len(units):
                    v = u - 1
                    n, j, par = units[v]
                    nb = len(blocks(n)) + 2
                    for i in range(nb):
                        pe.tr(self.wide[2][:, i * 128:(i + 1) * 128], P[:, v % 2, i * 128:(i + 1) * 128], self.ID,
                              expt[v], ptpfree)
                    pfree[v % 2] = pe.tok()
                    t1 = act.fn(PT[:, v % 3, 0:512], self.wide[2][:, 0:512], ACT.Copy, pfree[v % 2], ptfree.get(v % 3))
                    evt[v] = [t1]
                    if nb == 5:
                        evt[v].append(dve.cp(PT[:, v % 3, 512:640], self.wide[2][:, 512:640], pfree[v % 2], ptfree.get(v % 3)))
                    ptpfree = evt[v]
                if u >= 2:
                    v = u - 2
                    n, j, par = units[v]
                    hs = 2 * j + par
                    bl = blocks(n) + [4, 5]
                    for i, b in enumerate(bl):
                        pe.mm(self.banks[6][:, hs * 64:hs * 64 + 64], PT[:, v % 3, i * 128:(i + 1) * 128],
                              VA[:, b, par * 64:par * 64 + 64], i == 0, i == len(bl) - 1, evt[v],
                              ofree if hs == 0 and i == 0 else None)
                    ptfree[v % 3] = pe.tok()
                    if hs == 7:
                        s = n % 2
                        t = dve.do(lambda e, s=s: e.tensor_tensor(ES[:, s, 0:8:2], SK[:, 0:4], NM[:, s, 0:8:2], ALU.add),
                                   maxt[v])
                        t2 = dve.do(lambda e, s=s: e.tensor_tensor(ES[:, s, 1:8:2], SK[:, 4:8], NM[:, s, 1:8:2], ALU.add),
                                    maxt[v])
                        t = act.fn(ES[:, s, :], ES[:, s, :], ACT.Exp, t, t2)
                        t = dve.tt(DEN[:, s, :], DEN[:, s, :], ES[:, s, :], ALU.add, t, expt[v])
                        t = dve.recip(DEN[:, s, :], DEN[:, s, :], t)
                        o3 = self.banks[6].rearrange("p (h d) -> p h d", d=64)
                        rb = DEN[:, s, :].rearrange("p (h o) -> p h o", o=1).broadcast_to([128, 8, 64])
                        t = ofree = statfree[n] = dve.tt(ON[:, s, :].rearrange("p (h d) -> p h d", d=64), o3, rb,
                                                         ALU.mult, t, ptfree[v % 3], onfree.get(s))
                        for c in range(4):
                            pe.tr(self.banks[7][:, c * 128:(c + 1) * 128], ON[:, s, c * 128:(c + 1) * 128], self.ID,
                                  t, otfree)
                        onfree[s] = pe.tok()
                        otfree = act.fn(MIX[:, 0:4, n * 128:(n + 1) * 128],
                                        self.banks[7].rearrange("p (c t) -> p c t", t=128), ACT.Copy, onfree[s])

    def gla(self, outer, GQt, GKt, GRt, ZG, WA, VV, MIX, cc):
        pe, act, dve, pool = self.pe, self.act, self.dve, self.pool
        W = T + TC
        banks = self.banks
        with ExitStack() as ctx:
            self.barrier()
            sb = lambda n, s, dt=F32: self.sb(ctx, self.name(n), s, dt)
            GN = [sb(f"GN{d}", [128, 2, W]) for d in range(2)]
            KE = sb("KE", [128, 2, W])
            ST = self.over_ring("ST", [128, 2, 10, 256], F32, 0)
            QT = self.over_ring("QT", [128, 2, 2, T], F32, 20480)
            KT = self.over_ring("KT", [128, 2, 2, T], F32, 28672)
            KEN = [sb(f"KEN{d}", [128, 12, 2, 64]) for d in range(2)]
            DEC = sb("DEC", [128, 2, 2, 12])
            SM = sb("SM", [128, 2, W])
            AS = sb("AS", [128, 2, 256])
            MK = sb("MK", [128, 256], I32)
            ck = self.chan()
            pool.dma(MK[:, :], self.a["gla_mask"], ck)
            z = [pool.fill(SM[:, :, :], 1.0)]
            z = [pool.do(lambda e: e.memset(SM[:, 0, 0:W:64], 0.0), z), pool.do(lambda e: e.memset(SM[:, 1, 63:W:64], 0.0), z),
                 pool.fill(AS[:, :, :], 0.0)]
            bfree = {}
            gt = {}
            nb = 0
            E = self.SQ[:, :, 0:T]
            efree = [None]
            for d in range(2):
                bias = self.vec("b_a_f" if d == 0 else "b_a_b", 0, 2)
                for p in range(2):
                    for c0, c1 in ((0, T), (T, W)):
                        b = nb % 4
                        nb += 1
                        out = banks[b][:, 0:c1 - c0]
                        pe.mm(out, WA[:, d, p * 128:(p + 1) * 128], ZG[:, c0:c1], True, True, bfree.get(b), cc.tok())
                        bp = bias[:, p:p + 1]
                        g = GN[d][:, p, c0:c1]
                        ab = KE[:, p, c0:c1]
                        t1 = act.fn(ab, out, ACT.Abs, pe.tok(), gt.get((d - 1, p)), bias=bp)
                        t2 = bfree[b] = dve.ts(g, out, bp, 0.0, ALU.add, ALU.min, t1)
                        t1 = act.fn(ab, ab, ACT.Exp, t1, scale=-1.0)
                        t1 = act.fn(ab, ab, ACT.Ln, t1, bias=1.0)
                        t = dve.stt(g, g, -1.0, ab, ALU.mult, ALU.add, t1, t2)
                    g, m = GN[d][:, p, :], SM[:, d, :]
                    if d == 1:
                        g, m = g[:, ::-1], m[:, ::-1]
                    gt[d, p] = dve.scan(g, m, g, 0.0, ALU.mult, ALU.add, t, z)
            ready = {}
            for d in range(2):
                G = GN[d]
                gs = [gt[d, 0], gt[d, 1]]
                ge = G[:, :, 63:W:64] if d == 0 else G[:, :, 0:W:64]
                dec = act.fn(DEC[:, d, :, :], ge, ACT.Exp, gs, scale=-0.0625)
                t = act.fn(E, G[:, :, 0:T], ACT.Exp, gs, efree[0], scale=-0.0625)
                tq = dve.stt(QT[:, d, :, :], GQt[:, :, :], 0.125, E, ALU.mult, ALU.mult, t)
                t = act.fn(E, G[:, :, 0:T], ACT.Exp, gs, tq, scale=0.0625)
                tk = efree[0] = dve.tt(KT[:, d, :, :], GKt[:, :, 0:T], E, ALU.mult, t)
                t = None
                for p in range(2):
                    last = ge[:, p, :].rearrange("p (c o) -> p c o", o=1).broadcast_to([128, 12, 64])
                    k3 = KE[:, p, :].rearrange("p (c t) -> p c t", t=64)
                    t = dve.tt(k3, G[:, p, :].rearrange("p (c t) -> p c t", t=64), last, ALU.subtract, gs, gt[1, 1],
                               ready.get((d - 1, "ken")))
                t = act.fn(KE[:, :, :], KE[:, :, :], ACT.Exp, t, scale=0.0625)
                t = dve.tt(KE[:, :, :], KE[:, :, :], GKt[:, :, :], ALU.mult, t)
                kt = []
                for q in range(3):
                    b = nb % 4
                    nb += 1
                    for i in range(4):
                        cl = (4 * q + i) * 64
                        for p in range(2):
                            for par in range(2):
                                r = slice(64 * par, 64 * par + 64)
                                o = (i * 2 + p) * 64
                                pe.mm(banks[b][r, o:o + 64], KE[r, p, cl:cl + 64], self.ID[r, r], True, True, t, bfree.get(b))
                    tt_ = pe.tok()
                    bfree[b] = act.fn(KEN[d][:, 4 * q:4 * q + 4, :, :],
                                      banks[b].rearrange("p (c q f) -> p c q f", q=2, f=64), ACT.Copy, tt_)
                    kt.append(bfree[b])
                ready[d] = (tq, tk, kt, dec)
                ready[d, "ken"] = tt_
            seq = [[8, 9, 10, 11] + list(range(8)), [11, 10, 9, 8] + list(range(7, -1, -1))]
            slot = lambda d, i: seq[d][i] if i >= 4 else 8 + i % 2
            stt_ = {}
            for i in range(11):
                for d in range(2):
                    c = seq[d][i]
                    b = nb % 4
                    nb += 1
                    for p in range(2):
                        for par in range(2):
                            r = slice(64 * par, 64 * par + 64)
                            pe.mm(banks[b][r, p * 128:(p + 1) * 128], KEN[d][r, c, p, :], VV[r, c, p, :], True, True,
                                  ready[d][2], bfree.get(b))
                    done = pe.tok()
                    new = ST[:, d, slot(d, i + 1), :]
                    if i == 0:
                        t = dve.cp(new, banks[b][:, 0:256], done)
                    else:
                        old = ST[:, d, slot(d, i), :]
                        for p in range(2):
                            ps = slice(p * 128, (p + 1) * 128)
                            t = dve.stt(new[:, ps], old[:, ps], DEC[:, d, p, c:c + 1], banks[b][:, ps], ALU.mult, ALU.add,
                                        done, stt_[d, i], ready[d][3])
                    stt_[d, i + 1] = bfree[b] = t
            sdone = {d: stt_[d, 11] for d in range(2)}
            asfree = {}
            attm = {}

            def att(c):
                b = c % 2
                cl = slice(c * 64, c * 64 + 64)
                for d in range(2):
                    for p in range(2):
                        for par in range(2):
                            r = slice(64 * par, 64 * par + 64)
                            o = (d * 2 + p) * 64
                            pe.mm(banks[b][r, o:o + 64], KT[r, d, p, cl], QT[r, d, p, cl], True, True,
                                  ready[d][0], ready[d][1], bfree.get(b))
                attm[c] = bfree[b] = dve.do(
                    lambda e: e.copy_predicated(AS[:, c % 2, :], MK[:, :], banks[b][:, 0:256]),
                    pe.tok(), asfree.get(c % 2), z, ck.tok())

            for b in range(4):
                bfree[b] = [bfree.get(b), self.dve.tok(), self.act.tok()]
            att(0)
            for c in range(8):
                if c < 7:
                    att(c + 1)
                cl = slice(c * 64, c * 64 + 64)
                for p in range(2):
                    for par in range(2):
                        r = slice(64 * par, 64 * par + 64)
                        out = banks[4 + 2 * p + par][:, cl]
                        for d in range(2):
                            o = (d * 2 + p) * 64
                            pe.mm(out, VV[r, c, p, :], AS[r, c % 2, o:o + 64], d == 0, False, attm[c], share=True)
                            pe.mm(out, ST[r, d, c, p * 128:(p + 1) * 128], QT[r, d, p, cl], False, d == 1, sdone[d],
                                  share=True)
                asfree[c % 2] = pe.tok()
            done = pe.tok()
            SQ, RS = E[:, 0, :], E[:, 1, :]
            fq = [efree[0], ready[1][1]]
            for h in range(4):
                t = act.fn(SQ, banks[4 + h], ACT.Square, done, fq)
                b = h % 2
                pe.mm(banks[b], self.ONE, SQ, True, True, t, attm[6], attm[7], bfree.get(b))
                t = bfree[b] = dve.ts(RS, banks[b], 1.0 / 128, EPS, ALU.mult, ALU.add, pe.tok(), fq)
                t = dve.recip(RS, RS, t)
                t = act.fn(RS, RS, ACT.Sqrt, t)
                t = dve.stt(RS, banks[4 + h], self.vec("gla_g"), RS, ALU.mult, ALU.mult, t)
                t = dve.tt(MIX[:, 4 + h, :], RS, GRt[:, h, :], ALU.mult, t)
                fq = [t]


    def mixer_hybrid(self, mi):
        pe, act, dve, pool, a = self.pe, self.act, self.dve, self.pool, self.a
        banks = self.banks
        with self.scope() as outer:
            self.barrier()
            sb = lambda n, s, dt=F32: self.sb(outer, self.name(n), s, dt)
            MIX = sb("MIX", [128, 8, T])
            MQt, MKt, MVt, MOt = sb("MQt", [128, 2, T]), sb("MKt", [128, 2, T]), sb("MVt", [128, 4, 512]), MIX[:, 0:4, :]
            DQt, DKt, DVt = MIX[:, 4:8, :], sb("DKt", [128, 4, T]), sb("DVt", [128, 4, 512])
            GT = sb("GT", [4, 4, T])
            cc = self.chan()
            with ExitStack() as ctx:
                RT = self.sb(ctx, self.name("RT"), [128, 2, T], F32)
                PR = self.sb(ctx, self.name("PR"), [128, 256], F32)
                GQ8 = self.sb(ctx, self.name("GQ8"), [128, 1], F32)
                pool.dma(RT[:, :, :], a["rope2"], cc)
                pool.dma(PR[:, :], a["perm2"], cc)
                gq8 = dve.ts(GQ8[:, :], self.vec("g_q_2"), 0.125, None, ALU.mult, None)
                self.norm_split(ctx, mi, [(0, T, 0)])
                VB = self.SQ[:, 0, 0:T]
                TMP = self.sb(ctx, self.name("TMP"), [128, 3, T], F32)
                pfree = {5: None, 6: None, 7: None}
                free = {"vb": None, "tmp": None, "sq": None, "rs": None}
                nt = [0]

                def tbank():
                    nt[0] += 1
                    return 5 + nt[0] % 3

                def normed_rope(x, gain, t):
                    SQ, RS, TM = TMP[:, 0, :], TMP[:, 1, :], TMP[:, 2, :]
                    t1 = act.fn(SQ, x, ACT.Square, t, free["sq"])
                    b = tbank()
                    pe.mm(banks[b], PR[:, 128:256], SQ, True, True, t1, pfree[b], cc.tok())
                    free["sq"] = pe.tok()
                    t1 = pfree[b] = act.fn(RS, banks[b], ACT.Sqrt, free["sq"], free["rs"], scale=1.0 / 64, bias=self.EPSC)
                    t1 = dve.recip(RS, RS, t1)
                    t1 = free["rs"] = dve.stt(x, x, gain, RS, ALU.mult, ALU.mult, t1, gq8)
                    b = tbank()
                    pe.mm(banks[b], PR[:, 0:128], x, True, True, t1, pfree[b])
                    t2 = pfree[b] = dve.tt(TM, banks[b], RT[:, 1, :], ALU.mult, pe.tok(), free["tmp"], cc.tok())
                    t3 = dve.tt(x, x, RT[:, 0, :], ALU.mult, pe.tok())
                    free["tmp"] = dve.tt(x, x, TM, ALU.add, t2, t3)

                def token_major(V, h, out, done):
                    t = act.fn(VB, out, ACT.Copy, done, free["vb"])
                    b = tbank()
                    for i in range(4):
                        pe.tr(banks[b][:, i * 128:(i + 1) * 128], VB[:, i * 128:(i + 1) * 128], self.ID, t, pfree[b])
                    free["vb"] = pe.tok()
                    pfree[b] = dve.cp(V[:, :, h * 128:(h + 1) * 128], banks[b].rearrange("p (n f) -> p n f", f=128), free["vb"])
                    return t

                def evac(ch, c0, c1, out, done):
                    if ch < MK:
                        return act.fn(MQt[:, ch - MQ, :], out, ACT.Copy, done)
                    if ch < MV:
                        return act.fn(MKt[:, ch - MK, :], out, ACT.Copy, done, scale=0.125)
                    if ch < MO:
                        return token_major(MVt, ch - MV, out, done)
                    if ch < MG:
                        return act.fn(MOt[:, ch - MO, :], out, ACT.Sigmoid, done)
                    if ch == MG:
                        for g in range(4):
                            o = VOFF["gate_bias_2"] + g
                            t = act.fn(GT[:, g, :], out[32 * g:32 * g + 4, :], ACT.Identity, done, bias=self.VT[0:4, o:o + 1])
                        return t
                    if ch < DV:
                        X, i, gain = (DQt, ch - DQ, GQ8[:, :]) if ch < DK else (DKt, ch - DK, self.vec("g_k_2"))
                        t = act.fn(X[:, i, :], out, ACT.Copy, done)
                        normed_rope(X[:, i, :], gain, t)
                        return t
                    return token_major(DVt, ch - DV, out, done)

                self.projection(a["w_in_2"], [MG] + list(range(DQ, NIN2)) + list(range(MQ, MG)), (0, 1, 2, 3),
                                lambda ch: [(0, T)], evac)
            self.mlstm(MQt, MKt, MVt, MOt, GT, MIX)
            self.dilated(DQt, DKt, DVt, MIX)
            self.out_projection(mi, a["w_out_2"], MIX, [act.tok(), dve.tok()])

    def mlstm(self, Q, K, V, O, GT, MIX):
        pe, act, dve, pool = self.pe, self.act, self.dve, self.pool
        banks = self.banks
        with ExitStack() as ctx:
            self.barrier()
            sb = lambda n, s, dt=F32: self.sb(ctx, self.name(n), s, dt)
            U, EM, R = sb("U", [4, 2, T]), sb("EM", [4, 2, T]), sb("R", [4, 2, T])
            B, MG_, ON = sb("B", [4, T]), sb("MG", [4, 2, T]), sb("ON1", [4, T])
            UT = sb("UT", [128, 8, 4])
            MB = self.over_ring("MB", [128, 8, T], F32, 0)
            NUM = self.over_ring("NUM", [128, 8, T], F32, 16384)
            MD = self.over_ring("MD", [128, 2, T], F32, 32768)
            A = sb("A", [128, 4, T])
            SEL, OH, MKD = sb("SEL", [4, 4, 128]), sb("OH", [128, 4, 4]), sb("MKD", [128, 2, 128])
            ck = self.chan()
            pool.dma(SEL[:, :, :], self.a["sel"], ck)
            pool.dma(OH[:, :, :], self.a["onehot"], ck)
            pool.dma(MKD[:, :, :], self.a["tri"], ck)
            one = pool.fill(ON[:, :], 1.0)
            bfree = {}
            bt = None
            for d in range(2):
                li, z = GT[:, 2 * d, :], GT[:, 2 * d + 1, :]
                ab = EM[:, d, :]
                t = act.fn(ab, z, ACT.Abs)
                t = act.fn(ab, ab, ACT.Exp, t, scale=-1.0)
                t = act.fn(ab, ab, ACT.Ln, t, bias=1.0)
                t = dve.stt(z, z, 0.0, ab, ALU.min, ALU.subtract, t)
                rv = (lambda x: x) if d == 0 else (lambda x: x[:, ::-1])
                t = dve.scan(rv(B[:, :]), ON[:, :], rv(z), 0.0, ALU.mult, ALU.add, t, one, bt)
                t = dve.tt(U[:, d, :], li, B[:, :], ALU.subtract, t)
                u = rv(U[:, d, :])
                t = dve.scan(rv(MG_[:, d, :]), u, u, -BIG, ALU.max, ALU.max, t)
                bt = dve.tt(ab, B[:, :], MG_[:, d, :], ALU.add, t)
                emt = act.fn(ab, ab, ACT.Exp, bt, scale=-1.0)
                for s in range(4):
                    pe.tr(banks[0][:, (d * 4 + s) * 4:(d * 4 + s) * 4 + 4], U[:, d, s * 128:(s + 1) * 128], self.ID[0:4, 0:4], t)
            ut = bfree[0] = dve.cp(UT[:, :, :], banks[0][:, 0:32].rearrange("p (s h) -> p s h", h=4), pe.tok())
            mbt = {}

            def spread(d, h):
                i = d * 4 + h
                b = i % 2
                pe.mm(banks[b], SEL[:, h, :], MG_[:, d, :], True, True, bt, bfree.get(b), ck.tok())
                mbt[d, h] = bfree[b] = act.fn(MB[:, i, :], banks[b], ACT.Copy, pe.tok())

            for h in range(4):
                for d in range(2):
                    spread(d, h)
            afree, nfree, mdfree = {}, {}, {}
            na = 0
            numt = {}
            nq = 0
            prev = []
            for h in range(4):
                p, par = h // 2, h % 2
                r = slice(64 * par, 64 * par + 64)
                mdt = {}
                for d in range(2):
                    m = MKD[:, d:d + 1, :].broadcast_to([128, 4, 128])
                    mdt[d] = dve.tt(MD[:, d, :].rearrange("p (n t) -> p n t", t=128),
                                    MB[:, d * 4 + h, :].rearrange("p (n t) -> p n t", t=128), m, ALU.add,
                                    mbt[d, h], ck.tok(), mdfree.get(d))
                nb = [2 + 2 * (h % 2), 3 + 2 * (h % 2)]
                for j in range(4):
                    qb = nq % 2
                    nq += 1
                    js = slice(j * 128, j * 128 + 128)
                    pe.mm(banks[qb], K[r, p, js], Q[r, p, :], True, True, bfree.get(qb))
                    qt = pe.tok()
                    now = []
                    for d in range(2):
                        s = na % 4
                        na += 1
                        ub = UT[:, d * 4 + j, h:h + 1]
                        t1 = act.fn(A[:, s, js], MD[:, d, js], ACT.Exp, mdt[d], ut, afree.get(s), bias=ub, scale=-1.0)
                        mdfree[d] = t1
                        off = slice((j + 1) * 128, T) if d == 0 else slice(0, j * 128)
                        if off.stop > off.start:
                            t1 = act.fn(A[:, s, off], MB[:, d * 4 + h, off], ACT.Exp, afree.get(s), bias=ub, scale=-1.0)
                        full = slice(j * 128, T) if d == 0 else slice(0, (j + 1) * 128)
                        t = bfree[qb] = dve.tt(A[:, s, full], A[:, s, full], banks[qb][:, full], ALU.mult, t1, qt)
                        now.append((h, j, d, s, full, t, nb[d]))
                    for x in prev:
                        self.mlstm_sum(x, V, A, OH, NUM, afree, nfree, numt, ck)
                    prev = now
            for x in prev:
                self.mlstm_sum(x, V, A, OH, NUM, afree, nfree, numt, ck)
            rt = {}
            for d in range(2):
                t = act.fn(R[:, d, :], banks[6 + d][0:4, :], ACT.Abs, pe.tok())
                t = dve.tt(R[:, d, :], R[:, d, :], EM[:, d, :], ALU.max, t, emt)
                rt[d] = dve.recip(R[:, d, :], R[:, d, :], t)
            SQ, RS = A[:, 0, :], A[:, 1, :]
            fq = [afree[0], afree[1]]
            for h in range(4):
                t = []
                for d in range(2):
                    b = 2 * (h % 2) + d
                    pe.mm(banks[b], SEL[:, h, :], R[:, d, :], True, True, rt[d], numt[3, d], bfree.get(b), nfree.get(b))
                    x = NUM[:, d * 4 + h, :]
                    tt_ = dve.tt(x, x, banks[b], ALU.mult, pe.tok(), numt[h, d])
                    bfree[b] = tt_
                    t.append(tt_)
                x = NUM[:, h, :]
                t = dve.tt(x, x, NUM[:, 4 + h, :], ALU.add, t)
                t1 = act.fn(SQ, x, ACT.Square, t, fq)
                b = 4 + h % 2
                pe.mm(banks[b], self.ONE, SQ, True, True, t1, bfree.get(b), nfree.get(b), numt[3, 0], numt[3, 1])
                t1 = bfree[b] = dve.ts(RS, banks[b], 1.0 / 128, EPS, ALU.mult, ALU.add, pe.tok(), fq)
                t1 = dve.recip(RS, RS, t1)
                t1 = act.fn(RS, RS, ACT.Sqrt, t1)
                t1 = dve.stt(x, x, self.vec("g_mh_2", h), RS, ALU.mult, ALU.mult, t1)
                dve.tt(MIX[:, h, :], x, O[:, h, :], ALU.mult, t1)
                fq = [t1]

    def mlstm_sum(self, item, V, A, OH, NUM, afree, nfree, numt, ck):
        pe = self.pe
        h, j, d, s, full, t, b = item
        x = A[:, s, full]
        pe.mm(self.banks[b][:, full], V[:, j, h * 128:(h + 1) * 128], x, j == 0, True, t,
              nfree.get(b) if j == 0 else None, share=j > 0)
        pe.mm(self.banks[6 + d][0:4, full], OH[:, h, :], x, h == 0 and j == 0, True, ck.tok(), share=h + j > 0)
        afree[s] = pe.tok()
        if j == 3:
            numt[h, d] = nfree[b] = self.act.fn(NUM[:, d * 4 + h, :], self.banks[b], ACT.Copy, afree[s])

    def dilated(self, Q, K, V, MIX):
        pe, act, dve, pool = self.pe, self.act, self.dve, self.pool
        banks = self.banks
        with ExitStack() as ctx:
            self.barrier()
            sb = lambda n, s, dt=F32: self.sb(ctx, self.name(n), s, dt)
            CB, CM = sb("CB", [128, 1024], BF16), sb("CM", [128, 896])
            P, PT, ON = sb("P", [128, 3, 512]), sb("PT", [128, 3, 512]), sb("ON", [128, 2, 512])
            NM, DEN = sb("NM", [128, 2, 8]), sb("DEN", [128, 2, 8])
            ck = self.chan()
            CF = self.SQ[:, :, :].rearrange("p n t -> p (n t)")[:, 0:1024]
            pool.dma(CF[:, 0:128], self.a["cb"][:, 0:128], ck)
            pool.dma(CF[:, 128:1024], self.a["cb"][:, 384:1280], ck)
            pool.dma(CM[:, :], self.a["dil_count"], ck)
            cbt = act.fn(CB[:, :], CF, ACT.Copy, ck.tok())
            units = [(n, j, par) for n in range(4) for j in range(4) for par in range(2)]
            sfree, pfree, ptfree, pbfree, expt, pt_, evt, onfree, statfree = {}, {}, {}, {}, {}, {}, {}, {}, {}
            ofree = otfree = None
            for u in range(len(units) + 3):
                if u < len(units):
                    n, j, par = units[u]
                    r = slice(64 * par, 64 * par + 64)
                    b = u % 3
                    o = 384 - 128 * n
                    hs, s = 2 * j + par, n % 2
                    pe.mm(banks[b], Q[r, j, n * 128:(n + 1) * 128], K[r, j, :], True, True, sfree.get(b))
                    pe.mm(banks[b], CB[:, 0:128], CB[:, 128 + o:128 + o + 512], False, True, cbt, share=True)
                    t = dve.maxr(NM[:, s, hs:hs + 1], banks[b], pe.tok(), statfree.get(n - 2), negate=True)
                    expt[u] = sfree[b] = act.fn(P[:, u % 3, :], banks[b], ACT.Exp, t, pfree.get(u % 3),
                                                bias=NM[:, s, hs:hs + 1])
                if 1 <= u <= len(units):
                    v = u - 1
                    n, j, par = units[v]
                    o = 384 - 128 * n
                    hs, s = 2 * j + par, n % 2
                    x = P[:, v % 3, :]
                    pt_[v] = dve.stt(x, x, 1.0, CM[:, o:o + 512], ALU.mult, ALU.mult, expt[v], ck.tok(),
                                     acc=DEN[:, s, hs:hs + 1])
                    b = 3 + v % 2
                    for i in range(4):
                        pe.tr(banks[b][:, i * 128:(i + 1) * 128], P[:, v % 3, i * 128:(i + 1) * 128], self.ID,
                              pt_[v], pbfree.get(b))
                    pfree[v % 3] = pe.tok()
                    evt[v] = pbfree[b] = act.fn(PT[:, v % 3, :], banks[b], ACT.Copy, pfree[v % 3], ptfree.get(v % 3))
                if 2 <= u <= len(units) + 1:
                    v = u - 2
                    n, j, par = units[v]
                    hs, s = 2 * j + par, n % 2
                    for i in range(4):
                        pe.mm(banks[5][:, hs * 64:hs * 64 + 64], PT[:, v % 3, i * 128:(i + 1) * 128],
                              V[:, i, hs * 64:hs * 64 + 64], i == 0, i == 3, evt[v], ofree if hs == 0 and i == 0 else None)
                    ptfree[v % 3] = pe.tok()
                    if hs == 7:
                        t = dve.recip(DEN[:, s, :], DEN[:, s, :], pt_[v])
                        rb = DEN[:, s, :].rearrange("p (h o) -> p h o", o=1).broadcast_to([128, 8, 64])
                        t = ofree = statfree[n] = dve.tt(ON[:, s, :].rearrange("p (h d) -> p h d", d=64),
                                                         banks[5].rearrange("p (h d) -> p h d", d=64), rb,
                                                         ALU.mult, t, ptfree[v % 3], onfree.get(s))
                        for c in range(4):
                            pe.tr(banks[6][:, c * 128:(c + 1) * 128], ON[:, s, c * 128:(c + 1) * 128], self.ID, t, otfree)
                        onfree[s] = pe.tok()
                        otfree = act.fn(MIX[:, 4:8, n * 128:(n + 1) * 128], banks[6].rearrange("p (c t) -> p c t", t=128),
                                        ACT.Copy, onfree[s])


    def program(self):
        a = self.a
        st = self.stages
        self.setup()
        X = [(0, T, 0)]
        XC = [(0, T, 0), (T, T + TC, 1)]
        up = lambda w: [w[0], w[NF]]
        plan = {"f0": up(a["ffn1_wi"][0]), "m0": [a["w_in"][GZ]], "f1": up(a["ffn2_wi"][0]), "f2": up(a["ffn1_wi"][1]),
                "f3": up(a["ffn2_wi"][1]), "f4": up(a["w_gu1_2"]), "m2": [a["w_in_2"][MG]], "f5": up(a["w_gu2_2"])}

        def on(s):
            if s not in st:
                return False
            nxt = [x for x in ALL[ALL.index(s) + 1:] if x in st and x not in ("n1", "n2")]
            self.next = list(plan.get(nxt[0], ())) if nxt else []
            return True

        w0 = T + TC if "m0" in st or "f0" in st else T
        for k in range(8):
            self.sums(k, w0, None)
        with self.scope() as sc:
            self.mod_ring(sc)
            if "f0" in st:
                self.mod_first()
                self.tiles0 = [self.split(self.load(s)) for s in plan["f0"]]
            else:
                self.barrier()
                for blk in range(3):
                    self.run_jobs(self.mod_jobs(blk, range(9)))
            more = (lambda b, *r: self.mod_jobs(b, r)) if "f0" in st else (lambda *bt: [])
            if on("f0"):
                self.ffn(0, XC, a["ffn1_wi"][0], a["ffn1_wo"][0], more(0, 3, 4, 5, 6, 7, 8), more(0, 2))
        if on("m0"):
            self.mixer_ab(1)
        if on("f1"):
            self.ffn(2, X, a["ffn2_wi"][0], a["ffn2_wo"][0], more(1, 0, 1, 2))
        if on("f2"):
            self.ffn(3, X, a["ffn1_wi"][1], a["ffn1_wo"][1], more(1, 3, 4, 5, 6, 7, 8))
        if on("m1"):
            self.mixer_pool(4)
        if on("f3"):
            self.ffn(5, X, a["ffn2_wi"][1], a["ffn2_wo"][1], more(2, 0, 1, 2))
        if on("n1"):
            self.final_norm("final_g")
        if on("f4"):
            self.ffn(6, X, a["w_gu1_2"], a["w_down1_2"], more(2, 3, 4, 5, 6, 7, 8))
        if on("m2"):
            self.mixer_hybrid(7)
        if on("f5"):
            self.ffn(8, X, a["w_gu2_2"], a["w_down2_2"], [])
        c = self.chan()
        if on("n2"):
            self.final_norm("g_final_2", c)
        else:
            self.barrier()
            self.sp.dma(a["out"], self.XT[:, :, 0:T], c, self.dve.tok())
        if "out_ctx" in a:
            self.sp.dma(a["out_ctx"], self.XT[:, :, T:T + TC], c)
        self.sp.wait(c.tok())

        block = self.ctx.enter_context(self.nc.Block())
        for name, q in (("sync", self.sp), ("tensor", self.pe), ("scalar", self.act), ("vector", self.dve),
                        ("gpsimd", self.pool)):
            if q.items:
                self.attach(block, name, q)

    def attach(self, block, name, q):
        on = {"sync": block.sync, "tensor": block.tensor, "scalar": block.scalar, "vector": block.vector,
              "gpsimd": block.gpsimd}[name]

        @on
        def _(eng):
            q.emit(eng)


ALL = ("f0", "m0", "f1", "f2", "m1", "f3", "n1", "f4", "m2", "f5", "n2")


def build(nc, a, stages=ALL):
    with ExitStack() as ctx:
        Program(nc, ctx, a, stages).program()



def cols(w):
    k, n = w.shape
    return np.ascontiguousarray(w.reshape(k // 128, 128, n // 128, 128).transpose(2, 1, 0, 3)).reshape(n // 128, 128, k)


def feat(v):
    return np.ascontiguousarray(v.reshape(-1, 128).T)


def constants():
    k = {}
    one = np.ones((128, 128), np.float32)
    idn = np.eye(128, dtype=np.float32)
    z = np.zeros((128, 12), np.float32)
    z[:, 5], z[:, 11] = 1.0, EPS
    k["sel6"] = np.ascontiguousarray(np.broadcast_to(np.eye(6, dtype=np.float32)[:, :, None], (6, 6, 128)))
    k["consts"] = np.concatenate([one, idn, z], axis=1)
    t = np.arange(T)
    cnt = []
    for w in (2, 4, 8, 16):
        lo, hi = np.maximum(t - w // 2, 0), np.minimum(t + (w - w // 2), T)
        cnt.append(1.0 / (hi - lo))
    k["pool_cnt"] = np.ascontiguousarray(np.broadcast_to(np.array(cnt, np.float32)[None], (128, 4, T)))
    i, j = np.arange(128)[:, None], np.arange(128)[None, :]
    left = np.where(j >= i, 0.0, -BIG)
    right = np.where(j <= i, 0.0, -BIG)
    y = np.arange(896)[None, :] - 384 - i
    near = [(np.abs(y) % d == 0) & (np.abs(y) // d <= 64) for d in (1, 4, 16)]
    count = near[0].astype(np.float32) + near[1] + near[2]
    add = np.where(count > 0, 0.0, -BIG)
    k["cb"] = np.concatenate([idn, left, right, add], axis=1).astype(np.float32)
    k["dil_count"] = np.ascontiguousarray(count.astype(np.float32))
    pos = np.arange(T)
    f = np.float32(10000.0) ** (-np.arange(16, dtype=np.float32) / np.float32(16))
    ang = [(pos // 64).astype(np.float32)[:, None] * f, (pos % 64).astype(np.float32)[:, None] * f]
    head = np.concatenate([np.concatenate([t_, t_], axis=1) for t_ in ang], axis=1).T
    ang = np.concatenate([head, head], axis=0)
    k["rope1"] = np.ascontiguousarray(np.stack([np.cos(ang), np.sin(ang)], axis=1).astype(np.float32))
    perm = np.zeros((128, 128), np.float32)
    for p in range(128):
        if p % 32 < 16:
            perm[p + 16, p] = -1.0
        else:
            perm[p - 16, p] = 1.0
    k["perm1"] = perm
    m = np.zeros((128, 2, 2, 64), np.int32)
    jj, ii = (np.arange(128) % 64)[:, None, None], np.arange(64)[None, None, :]
    m[:, 0] = jj <= ii
    m[:, 1] = jj >= ii
    k["gla_mask"] = m.reshape(128, 256)
    f = np.float32(500000.0) ** (-2.0 * np.arange(8, dtype=np.float32) / np.float32(16)).astype(np.float32)
    ang = pos.astype(np.float32)[:, None] * f
    c, s = np.ones((64, T), np.float32), np.zeros((64, T), np.float32)
    c[0:16], s[0:16] = np.tile(np.cos(ang).T, (2, 1)), np.tile(np.sin(ang).T, (2, 1))
    k["rope2"] = np.ascontiguousarray(np.stack([np.tile(c, (2, 1)), np.tile(s, (2, 1))], axis=1))
    perm = np.zeros((128, 256), np.float32)
    for p in range(128):
        if p % 64 < 8:
            perm[p + 8, p] = -1.0
        elif p % 64 < 16:
            perm[p - 8, p] = 1.0
        perm[64 * (p // 64):64 * (p // 64) + 64, 128 + p] = 1.0
    k["perm2"] = perm
    sel = np.zeros((4, 4, 128), np.float32)
    oh = np.zeros((128, 4, 4), np.float32)
    for h in range(4):
        sel[h, h] = 1.0
        oh[:, h, h] = 1.0
    k["sel"], k["onehot"] = sel, oh
    k["tri"] = np.ascontiguousarray(np.stack([np.where(i <= j, 0.0, BIG), np.where(i >= j, 0.0, BIG)], axis=1).astype(np.float32))
    return k


def arrange(i):
    f = {}
    vecs = []
    for name, n in VEC:
        v = np.asarray(i[name], np.float32)
        if name in ("g_q_2", "g_k_2"):
            v = np.tile(v.reshape(64, 1), (2, 1))
        elif name == "gate_bias_2":
            p = np.zeros((128, 4), np.float32)
            p[0:4] = v.reshape(4, 4).T
            v = p
        elif name == "sink":
            p = np.zeros((128, 1), np.float32)
            p[0:8, 0] = v.reshape(8)
            v = p
        else:
            v = feat(v.reshape(-1))
        assert v.shape == (128, n), name
        vecs.append(v)
    f["vecs"] = np.ascontiguousarray(np.concatenate(vecs, axis=1))
    tr = lambda x: np.ascontiguousarray(x[0].T.reshape(8, 128, -1).transpose(1, 0, 2))
    f["x_in"] = tr(i["x"])
    f["ctx_in"] = tr(i["ctx"])
    f["w_mod"] = i["w_mod"]
    f["w_ada_2"] = i["w_ada_2"][0]
    for n in ("ffn1_wi", "ffn2_wi"):
        f[n] = np.stack([cols(i[n][l]) for l in range(2)])
    for n in ("ffn1_wo", "ffn2_wo"):
        f[n] = i[n].reshape(2, NF, 128, D)
    f["w_gu1_2"] = cols(i["w_gu1_2"][0])
    f["w_gu2_2"] = cols(i["w_gu2_2"][0])
    f["w_down1_2"] = i["w_down1_2"].reshape(NF, 128, D)
    f["w_down2_2"] = i["w_down2_2"].reshape(NF, 128, D)
    f["pool_w"] = np.ascontiguousarray(i["w_pool"][0].reshape(4, 2, 128, 256).transpose(2, 0, 1, 3))
    w = i["w_in"][0]
    q = w[:, 0:512].reshape(D, 8, 64)
    q = np.stack([q[:, [j, j + 4]] for j in range(4)], axis=1).reshape(D, 512)
    f["w_in"] = cols(np.concatenate([q, w[:, 512:], np.zeros((D, 96), np.float32)], axis=1))
    wa = np.zeros((32, 2, 256), np.float32)
    wa[0:16, 0] = i["w_a2_f"][0]
    wa[16:32, 1] = i["w_a2_b"][0]
    f["wa2"] = wa
    w = i["w_out"][0]
    o = w[0:512].reshape(8, 64, D)
    o = np.stack([o[[j, j + 4]] for j in range(4)]).reshape(512, D)
    f["w_out"] = cols(np.concatenate([o, w[512:]]))
    w = i["w_in_2"][0]
    g = np.zeros((D, 4, 32), np.float32)
    g[:, :, 0:4] = w[:, 1536:1552].reshape(D, 4, 4)
    f["w_in_2"] = cols(np.concatenate([w[:, 0:1536], g.reshape(D, 128), w[:, 1552:]], axis=1))
    f["w_out_2"] = cols(i["w_out_2"][0])
    f.update(constants())
    return f


def kernel(**inputs):
    import concourse.bacc as bacc
    from concourse.bass_utils import run_bass_kernel_spmd

    inputs = {k: np.asarray(v) for k, v in inputs.items()}
    nc = bacc.Bacc("TRN2", target_bir_lowering=False, num_devices=1)
    arrays, a = {}, {}
    for name, v in arrange(inputs).items():
        arrays[f"in_{name}"] = v
        a[name] = nc.dram_tensor(f"in_{name}", v.shape, mybir.dt.from_np(v.dtype), kind="ExternalInput").ap()
    a["out"] = nc.dram_tensor("out_0", (128, 8, T), F32, kind="ExternalOutput").ap()
    build(nc, a)
    r = run_bass_kernel_spmd(nc, [arrays], core_ids=[0])
    o = np.asarray(r.results[0]["out_0"])
    return np.ascontiguousarray(o.transpose(2, 1, 0).reshape(1, T, D))
```

```python
from contextlib import ExitStack

import numpy as np

import concourse.bass as bass
from concourse import mybir

F32 = mybir.dt.float32
F32R = mybir.dt.float32r
BF16 = mybir.dt.bfloat16
I32 = mybir.dt.int32
ALU = mybir.AluOpType
ACT = mybir.ActivationFunctionType
AXX = mybir.AxisListType.X

D = 1024
T = 512
TC = 256
FF = 2816
NF = FF // 128
NRAW = 6
NUNIT = 5
EPS = 1e-6
BIG = 1e30

VEC = [("b_mod", 144), ("norm_g", 48), ("pool_scale", 8), ("final_g", 8), ("gla_g", 1),
       ("c", 8), ("c_ctx", 8), ("b_a_f", 2), ("b_a_b", 2), ("c_2", 8), ("b_ada_2", 72),
       ("g_ffn1_2", 8), ("g_mix_2", 8), ("g_ffn2_2", 8), ("g_final_2", 8), ("g_mh_2", 4),
       ("g_q_2", 1), ("g_k_2", 1), ("gate_bias_2", 4), ("sink", 1)]
VOFF = {}
_o = 0
for _n, _c in VEC:
    VOFF[_n] = _o
    _o += _c
NV = _o

AQ, AK, AV, GQ, GK, GV, GR, GZ = 0, 4, 5, 6, 8, 10, 14, 18
NIN1 = 19
MQ, MK, MV, MO, MG, DQ, DK, DV = 0, 2, 4, 8, 12, 13, 17, 21
NIN2 = 25


class Queue:

    def __init__(self, sem):
        self.sem, self.n, self.items = sem, 0, []

    def put(self, fn, *after):
        self.items.append([fn, after, None])

    def do(self, fn, *after):
        self.items.append([fn, after, (self.sem, 1)])
        self.n += 1
        return (self.sem, self.n)

    def tt(self, o, x, y, op, *after):
        return self.do(lambda e: e.tensor_tensor(o, x, y, op), *after)

    def stt(self, o, x, s, y, op0, op1, *after, acc=None):
        return self.do(lambda e: e.scalar_tensor_tensor(o, x, s, y, op0, op1, accum_out=acc) if acc is not None
                       else e.scalar_tensor_tensor(o, x, s, y, op0, op1), *after)

    def ts(self, o, x, s1, s2, op0, op1, *after):
        return self.do(lambda e: e.tensor_scalar(o, x, s1, s2, op0, op1) if op1 is not None
                       else e.tensor_scalar(o, x, s1, s2, op0), *after)

    def cp(self, o, x, *after):
        return self.do(lambda e: e.tensor_copy(o, x), *after)

    def recip(self, o, x, *after):
        return self.do(lambda e: e.reciprocal(o, x), *after)

    def maxr(self, o, x, *after, negate=False):
        return self.do(lambda e: e.tensor_reduce(o, x, AXX, ALU.max, negate=negate), *after)

    def scan(self, o, m, x, init, op0, op1, *after):
        return self.do(lambda e: e.tensor_tensor_scan(o, m, x, init, op0, op1), *after)

    def fill(self, o, v, *after):
        return self.do(lambda e: e.memset(o, v), *after)

    def fn(self, o, x, f, *after, bias=0.0, scale=1.0, acc=None):
        return self.do(lambda e: e.activation(o, x, f, bias=bias, scale=scale, accum_out=acc) if acc is not None
                       else e.activation(o, x, f, bias=bias, scale=scale), *after)

    def mm(self, o, l, r, start, stop, *after, share=False):
        self.put(lambda e: e.matmul(o, l, r, start=start, stop=stop, skip_group_check=share), *after)

    def tr(self, o, x, ident, *after):
        self.put(lambda e: e.transpose(o, x, ident), *after)

    def tok(self):
        last = next((i for i in reversed(self.items) if i[0] is not None), None)
        if last is None:
            return None
        if last[2] is None:
            last[2] = (self.sem, 1)
            self.n += 1
        return (self.sem, self.n)

    def wait(self, *after):
        self.items.append([None, after, None])

    def dma(self, out, in_, chan, *after):
        self.items.append([lambda e: e.dma_start(out, in_), after, (chan.sem, 16)])
        chan.n += 16
        return (chan.sem, chan.n)

    def emit(self, eng):
        seen = {}

        def wait(a):
            if a is None:
                return
            if callable(a):
                a = a()
            if isinstance(a, list):
                for b in a:
                    wait(b)
                return
            if a is None:
                return
            sem, v = a
            if seen.get(id(sem), 0) < v:
                eng.wait_ge(sem, v)
                seen[id(sem)] = v

        for fn, after, sig in self.items:
            for a in after:
                wait(a)
            if fn is not None:
                ins = fn(eng)
                if sig is not None:
                    ins.then_inc(*sig)


class Chan:

    def __init__(self, sem):
        self.sem, self.n = sem, 0

    def tok(self):
        return (self.sem, self.n)


class Load:

    def __init__(self, view, ready):
        self.view, self.ready, self.free = view, ready, None


class Unit:

    def __init__(self, hi, lo, ready):
        self.hi, self.lo, self.ready, self.free = hi, lo, ready, None


class Job:

    def __init__(self, srcs, run, raw=False):
        self.srcs, self.run, self.raw, self.tiles = srcs, run, raw, None


class Program:
    def __init__(self, nc, ctx, a, stages):
        self.nc, self.ctx, self.a, self.stages = nc, ctx, a, stages
        sem = lambda n: ctx.enter_context(nc.semaphore(n))
        self.pe, self.act, self.dve, self.pool = (Queue(sem(f"s_{n}")) for n in ("pe", "act", "dve", "pool"))
        self.sp = Queue(None)
        self.free_sems = [sem(f"s_m{i}") for i in range(60)]
        self.rawc = [Chan(sem(f"s_raw{i}")) for i in range(NRAW)]
        self.loads = []
        self.units = []
        self.stackno = 0
        self.banks = []
        for i in range(4):
            t = ctx.enter_context(nc.psum_tensor(f"ps{i}", [128, 1024], F32))
            self.banks += [t[:, 0:512], t[:, 512:1024]]
            if i == 0:
                self.wide = []
            self.wide.append(t)
        self.XT = self.sb(ctx, "XT", [128, 8, T + TC], F32)
        self.RAW = self.sb(ctx, "RAW", [128, NRAW, 1024], F32)
        self.VT = self.sb(ctx, "VT", [128, NV], F32)
        self.K = self.sb(ctx, "K", [128, 268], F32)
        self.ONE, self.ID = self.K[:, 0:128], self.K[:, 128:256]
        self.MOD = self.sb(ctx, "MOD", [128, 9, 2, 24], F32)
        self.DER = self.sb(ctx, "DER", [128, 9, 3, 16], F32)
        self.SC = self.sb(ctx, "SC", [128, 8, 3], F32)
        self.ring_at = nc.sbuf_base
        self.WH = self.sb(ctx, "WH", [128, NUNIT, 1024], F32R)
        self.WL = self.sb(ctx, "WL", [128, NUNIT, 1024], F32R)
        self.SQ = self.sb(ctx, "SQ", [128, 2, T + TC], F32)
        self.SA = self.sb(ctx, "SA", [128, T + TC], F32)
        self.R6 = self.sb(ctx, "R6", [6, 256], F32)
        self.SEL6 = self.sb(ctx, "SEL6", [6, 6, 128], F32)
        self.nunit = NUNIT
        self.modt = {}
        self.modread = None
        self.sqfree, self.safree, self.sat = [None, None], None, None
        self.tiles0, self.next = None, []
        self.later = []
        self.sumlate = None

    def sb(self, ctx, name, shape, dt):
        return ctx.enter_context(self.nc.sbuf_tensor(name, shape, dt))

    def over_ring(self, name, shape, dt, offset):
        return self.nc.alloc_sbuf_tensor_at(self.name(name), shape, dt, offset=self.ring_at + offset)

    def chan(self):
        return Chan(self.free_sems.pop())

    def scope(self):
        self.stackno += 1
        return ExitStack()

    def name(self, s):
        return f"{s}_{self.stackno}"

    def barrier(self):
        es = [self.pe, self.act, self.dve, self.pool]
        toks = [e.tok() for e in es if e.items]
        for e in es:
            e.wait(toks)

    def vec(self, name, i=0, n=1):
        o = VOFF[name] + i
        return self.VT[:, o:o + n]


    def load(self, src):
        i = len(self.loads)
        prev = self.loads[i - NRAW] if i >= NRAW else None
        view = self.RAW[:, i % NRAW, :]
        ready = self.sp.dma(view, src, self.rawc[i % NRAW], (lambda: prev.free) if prev else None)
        ld = Load(view, ready)
        self.loads.append(ld)
        return ld

    def split(self, ld):
        i = len(self.units)
        prev = self.units[i - self.nunit] if i >= self.nunit else None
        hi, lo = self.WH[:, i % self.nunit, :], self.WL[:, i % self.nunit, :]
        th = self.act.do(lambda e: e.activation(hi, ld.view, ACT.Copy), ld.ready, prev.free if prev else None)
        tl = self.dve.do(lambda e: e.tensor_tensor(lo, ld.view, hi.bitcast(F32), ALU.subtract), th)
        ld.free = [th, tl]
        u = Unit(hi, lo, [th, tl])
        self.units.append(u)
        return u

    def unit_ring(self, n):
        self.WH = self.over_ring("WH", [128, n, 1024], F32R, 0)
        self.WL = self.over_ring("WL", [128, n, 1024], F32R, n * 4096)
        self.nunit, self.units = n, []

    def prepare(self, job):
        job.tiles = [self.load(s) for s in job.srcs]
        if not job.raw:
            job.tiles = [self.split(t) for t in job.tiles]

    def run_jobs(self, jobs):
        if self.tiles0 is not None:
            jobs[0].tiles, self.tiles0 = self.tiles0, None
        elif not jobs[0].raw:
            self.prepare(jobs[0])
        main = [j for j, job in enumerate(jobs) if not job.raw]
        after = dict(zip(main, main[1:]))
        for j, job in enumerate(jobs):
            if job.raw:
                if job.tiles is None:
                    self.prepare(job)
                if j + 1 < len(jobs) and jobs[j + 1].raw:
                    self.prepare(jobs[j + 1])
                job.run(job.tiles)
                continue
            if j in after:
                self.prepare(jobs[after[j]])
            elif self.next:
                self.tiles0 = [self.split(self.load(s)) for s in self.next]
                self.next = []
            if j + 1 < len(jobs) and jobs[j + 1].raw:
                self.prepare(jobs[j + 1])
            before, self.later = self.later, []
            job.run(job.tiles)
            for _, f in before:
                f()
        self.finish_rows()

    def mm3(self, out, w, x, first, last, *after):
        wh, wl = w
        xh, xl = x
        self.pe.put(lambda e: e.matmul(out, wh, xh, start=first, stop=False), *after)
        self.pe.put(lambda e: e.matmul(out, wh, xl, start=False, stop=False))
        self.pe.put(lambda e: e.matmul(out, wl, xh, start=False, stop=last))

    def mm2(self, out, w, x, first, last, *after):
        wh, wl = w
        self.pe.put(lambda e: e.matmul(out, wh, x, start=first, stop=True, skip_group_check=not first), *after)
        self.pe.put(lambda e: e.matmul(out[:, 0:TC], wl, x[:, 0:TC], start=False, stop=True, skip_group_check=True))


    def setup(self):
        a, sp = self.a, self.sp
        c = self.chan()
        sp.dma(self.VT[:, :], a["vecs"], c)
        sp.dma(self.K[:, :], a["consts"], c)
        sp.dma(self.SEL6[:, :, :], a["sel6"], c)
        for q in (self.pe, self.act, self.dve, self.pool):
            q.wait(c.tok())
        self.Z11, self.EPSC = self.K[:, 256:267], self.K[:, 267:268]
        for i, n in enumerate(("c", "c_ctx", "c_2")):
            self.act.do(lambda e, i=i, n=n: e.activation(self.SC[:, :, i], self.vec(n, 0, 8), ACT.Silu))
        self.sct = self.act.tok()

    def load_x(self):
        cx = self.chan()
        self.sp.dma(self.XT[:, :, 0:T], self.a["x_in"], cx)
        self.sp.dma(self.XT[:, :, T:T + TC], self.a["ctx_in"], cx)
        self.xt = cx.tok()


    def mod_ring(self, ctx):
        self.ACC = self.sb(ctx, self.name("ACC"), [128, 2, D], F32)
        self.accfree, self.acct = [None, None], [None, None]

    def mod_conds(self, blk, row):
        return (0, 1) if blk == 0 and row < 5 else ((0,) if blk < 2 else (2,))

    def mod_jobs(self, blk, rows, bank=7):
        src = self.a["w_mod"][blk] if blk < 2 else self.a["w_ada_2"]
        PS = self.banks[bank]
        jobs = []
        for row in rows:
            conds = self.mod_conds(blk, row)
            for k in range(8):
                def run(tiles, row=row, k=k, conds=conds):
                    ld = tiles[0]
                    ld.free = []
                    for n, c in enumerate(conds):
                        n = n if len(conds) == 2 else row % 2
                        self.mod_add(n, c, k, ld, k == 0)
                    if k < 7:
                        return
                    slots = (0, 1) if len(conds) == 2 else (row % 2,)
                    toks = [self.acct[n] for n in slots]
                    self.later.append((slots, lambda: self.mod_rows(blk, row, PS, slots, toks)))
                jobs.append(Job([src[k * 128:(k + 1) * 128, row * D:(row + 1) * D]], run, raw=True))
        return jobs

    def mod_rows(self, blk, row, PS, slots, toks):
        for i, n in enumerate(slots):
            for f in range(8):
                o = (row % 2) * 16 + 2 * f + i
                self.pe.mm(PS[:, o:o + 1], self.ACC[:, n, f * 128:(f + 1) * 128], self.ONE[:, 0:1],
                           True, True, toks[i], self.modread)
            self.accfree[n] = self.pe.tok()
        self.mod_done(blk, row, PS, len(slots), self.pe.tok())

    def finish_rows(self):
        now, self.later = self.later, []
        for _, f in now:
            f()

    def mod_add(self, n, c, k, ld, first):
        acc, sc = self.ACC[:, n, :], self.SC[:, k, c:c + 1]
        if first:
            if any(n in slots for slots, _ in self.later):
                self.finish_rows()
            t = self.dve.ts(acc, ld.view, sc, None, ALU.mult, None, ld.ready, self.sct, self.accfree[n])
        else:
            t = self.dve.stt(acc, ld.view, sc, acc, ALU.mult, ALU.add, ld.ready, self.acct[n])
        self.acct[n] = t
        ld.free.append(t)

    def mod_first(self):
        src = self.a["w_mod"][0]
        PS = self.banks[7]
        for row in range(2):
            for k in range(8):
                ld = self.load(src[k * 128:(k + 1) * 128, row * D:(row + 1) * D])
                ld.free = []
                if row == 1 and k == 1:
                    self.load_x()
                if k % 2 == 1:
                    for f in range(8):
                        o = row * 16 + 2 * f
                        self.pe.mm(PS[:, o:o + 2], ld.view[:, f * 128:(f + 1) * 128], self.SC[:, k, 0:2],
                                   row == 0 and k == 1 and f == 0, True, ld.ready, self.sct, share=True)
                    ld.free.append(self.pe.tok())
                else:
                    for n in range(2):
                        self.mod_add(n, n, k, ld, k == 0)
            for n in range(2):
                for f in range(8):
                    o = row * 16 + 2 * f + n
                    self.pe.mm(PS[:, o:o + 1], self.ACC[:, n, f * 128:(f + 1) * 128], self.ONE[:, 0:1],
                               False, True, self.acct[n], share=True)
                self.accfree[n] = self.pe.tok()
            if row == 1:
                for k in range(8):
                    self.sums(k, T + TC, self.xt)
        for row in range(2):
            self.mod_done(0, row, PS, 2, self.pe.tok())

    def mod_done(self, blk, row, PS, ncond, done):
        third, jj = row // 3, row % 3
        i = 3 * blk + third
        dve = self.dve
        bias = self.vec("b_mod" if blk < 2 else "b_ada_2", (blk if blk < 2 else 0) * 72 + 8 * row, 8)
        g = self.vec("norm_g", 24 * blk + 8 * third, 8) if blk < 2 else self.vec(("g_ffn1_2", "g_mix_2", "g_ffn2_2")[third], 0, 8)
        for j in range(ncond):
            pv = PS[:, (row % 2) * 16 + j:(row % 2) * 16 + 16:2]
            M, R = self.MOD[:, i, j, 8 * jj:8 * jj + 8], self.DER[:, i, :, 8 * j:8 * j + 8]
            t = self.modread = dve.tt(M, pv, bias, ALU.add, done)
            if jj == 1:
                t = dve.stt(R[:, 0, :], M, 1.0, g, ALU.add, ALU.mult, t)
            elif jj == 2 and blk == 1 and third == 1:
                t = dve.tt(R[:, 2, :], M, self.vec("pool_scale", 0, 8), ALU.mult, t)
            elif jj == 2:
                t = dve.ts(R[:, 2, :], M, 1.0 if third == 1 else 0.5, None, ALU.mult, None, t)
        self.modt[i, jj] = t

    def mod_a(self, i, k, j=0):
        return self.DER[:, i, 0, 8 * j + k:8 * j + k + 1]

    def mod_b(self, i, k, j=0):
        return self.MOD[:, i, j, k:k + 1]

    def mod_g(self, i, k, j=0):
        return self.DER[:, i, 2, 8 * j + k:8 * j + k + 1]


    def rstd_of(self, ctx, name, n, ss, width, done, parts=128):
        R = self.sb(ctx, self.name(name), [128, n], F32)
        return R, self.rstd_into(R[0:parts, :], ss, width, done)

    def rstd_into(self, R, V, ss, width, *after):
        dve = self.dve
        v = dve.ts(V, ss, 1.0 / width, EPS, ALU.mult, ALU.add, *after)
        t = self.act.fn(R, V, ACT.Sqrt, v, *after)
        t = dve.recip(R, R, t)
        t = dve.stt(V, V, -0.5, R, ALU.mult, ALU.mult, t)
        t = dve.tt(V, V, R, ALU.mult, t)
        return v, dve.stt(R, V, 1.5, R, ALU.add, ALU.mult, t)

    def sums(self, k, w, ready):
        s = k % 2
        dst = self.SA[:, 0:w] if k == 0 else self.SQ[:, s, 0:w]
        t = self.act.fn(dst, self.XT[:, k, 0:w], ACT.Square, ready, self.safree if k == 0 else self.sqfree[s])
        prev, self.sumlate = self.sumlate, None
        if prev:
            prev()
        if k == 0:
            self.sat = t
            return

        def add():
            self.sat = self.sqfree[s] = self.dve.tt(self.SA[:, 0:w], self.SA[:, 0:w], dst, ALU.add, t, self.sat)
        if k < 7:
            self.sumlate = add
            return
        self.act.fn(self.R6[:, 0:1], self.EPSC[0:6, :], ACT.Sqrt)
        add()

    def rstd(self, nq):
        pe = self.pe
        out = self.banks[7][0:6, 256:384]
        for q in range(nq):
            pe.mm(out, self.Z11[:, 5 - q:11 - q], self.SA[:, q * 128:(q + 1) * 128], q == 0, True,
                  self.sat, self.modread, share=q > 0)
        self.safree = pe.tok()
        t = self.rstd_into(self.R6[:, 0:128], self.R6[:, 128:256], out, 1024, self.safree)[1]
        for q in range(nq):
            pe.mm(self.banks[4 + q // 4][:, (q % 4) * 128:(q % 4) * 128 + 128],
                  self.SEL6[:, q, :], self.R6[:, 0:128], True, True, t)
        return pe.tok()

    def norm(self, segs, emit):
        rt = self.rstd(segs[-1][1] // 128)
        for n, (c0, c1, j) in enumerate(segs):
            for k in range(8):
                emit(k, c0, c1, j, self.banks[4 + n][:, 0:c1 - c0], rt)

    def norm_split(self, ctx, mi, segs):
        self.HH = self.sb(ctx, self.name("HH"), [128, 8, T], F32R)
        self.HL = self.sb(ctx, self.name("HL"), [128, 8, T], F32R)
        if len(segs) == 2:
            self.HC = self.sb(ctx, self.name("HC"), [128, 8, 2 * TC], F32R)
        self.ht = {}

        def emit(k, c0, c1, j, R, rt):
            s = k % 2
            t_ = self.SQ[:, s, 0:c1 - c0]
            hh, hl = (self.HH[:, k, :], self.HL[:, k, :]) if c0 == 0 else (self.HC[:, k, 0:TC], self.HC[:, k, TC:2 * TC])
            t1 = self.dve.do(lambda e: e.scalar_tensor_tensor(t_, self.XT[:, k, c0:c1], self.mod_a(mi, k, j), R,
                                                              ALU.mult, ALU.mult),
                             rt, self.modt[mi, 0], self.modt[mi, 1], self.sqfree[s])
            t2 = self.act.do(lambda e: e.activation(hh, t_, ACT.Identity, bias=self.mod_b(mi, k, j)), t1)
            low()

            def rest():
                t3 = self.dve.do(lambda e: e.scalar_tensor_tensor(hl, t_, self.mod_b(mi, k, j), hh.bitcast(F32),
                                                                  ALU.add, ALU.subtract), t2)
                self.sqfree[s] = t3
                self.ht[k, c0] = [t2, t3]
            pending.append(rest)

        pending = []

        def low():
            while pending:
                pending.pop()()

        self.norm(segs, emit)
        low()

    def product(self, out, u, c0, first, last, ws, x, *after):
        w = (u.hi[:, ws], u.lo[:, ws])
        (self.mm3 if c0 == 0 else self.mm2)(out, w, x, first, last, *after)

    def h(self, k, c0):
        return (self.HH[:, k, :], self.HL[:, k, :]) if c0 == 0 else self.HC[:, k, :]


    def ffn(self, mi, segs, wi, wo, extra, early=()):
        with self.scope() as ctx:
            self.barrier()
            w = segs[-1][1]
            two = len(segs) == 2
            if not early:
                self.mod_ring(ctx)
            NG = 5
            self.norm_split(ctx, mi, segs)
            GH = self.sb(ctx, self.name("GH"), [128, NG, T], F32R)
            GL = self.sb(ctx, self.name("GL"), [128, NG, T], F32R)
            GC = self.sb(ctx, self.name("GC"), [128, NG, 2 * TC], F32R) if two else None
            S = self.sb(ctx, self.name("S"), [128, 2, w], F32)
            SX = self.sb(ctx, self.name("SX"), [128, TC], F32) if two else None
            ub, db = [0, 1, 2, 3], [4, 5, 6]
            ufree, dfree = {b: None for b in ub}, {b: None for b in db}
            for b in (4, 5):
                dfree[b] = self.dve.tok()
            cnt = {"u": 0, "d": 0}
            gfree, gready, sfree = {}, {}, {}
            act, dve = self.act, self.dve

            def gv(c, c0):
                return (GH[:, c % NG, :], GL[:, c % NG, :]) if c0 == 0 else GC[:, c % NG, :]

            def up(c):
                def products(b, u, c0, k):
                    self.product(self.banks[b], u, c0, k == 0, k == 7, slice(k * 128, (k + 1) * 128), self.h(k, c0),
                                 u.ready, self.ht[k, c0], ufree[b] if k == 0 else None)

                def run(tiles):
                    if c == 0:
                        for n, (c0, c1, j) in enumerate(segs):
                            for k in range(8):
                                for q, u in enumerate(tiles):
                                    products(ub[q * len(segs) + n], u, c0, k)
                    for q, u in enumerate(tiles):
                        for c0, c1, j in segs:
                            b = ub[cnt["u"] % len(ub)]
                            cnt["u"] += 1
                            out = self.banks[b]
                            for k in range(8 if c > 0 else 0):
                                products(b, u, c0, k)
                            done = self.pe.tok()
                            u.free = done
                            s = S[:, c % 2, c0:c1]
                            if q == 0 and c0 == 0:
                                t = act.fn(s, out, ACT.Silu, done, sfree.get((c % 2, c0)))
                                ufree[b] = t
                                sfree[c, c0, "t"] = t
                            elif q == 0:
                                t = act.fn(s, out[:, TC:2 * TC], ACT.Copy, done, sfree.get((c % 2, c0)))
                                t = ufree[b] = dve.tt(s, s, out[:, 0:TC], ALU.add, done, t)
                                sfree[c, c0, "t"] = act.fn(s, s, ACT.Silu, t)
                            else:
                                if c0 == 0:
                                    t = ufree[b] = dve.tt(s, s, out, ALU.mult, done, sfree[c, c0, "t"])
                                    gh, gl = gv(c, c0)
                                else:
                                    t = act.fn(SX[:, :], out[:, TC:2 * TC], ACT.Copy, done, sfree.get("sx"))
                                    t = ufree[b] = dve.tt(SX[:, :], SX[:, :], out[:, 0:TC], ALU.add, done, t)
                                    t = sfree["sx"] = dve.tt(s, s, SX[:, :], ALU.mult, t, sfree[c, c0, "t"])
                                    gh, gl = GC[:, c % NG, 0:TC], GC[:, c % NG, TC:2 * TC]
                                t1 = act.fn(gh, s, ACT.Copy, t, gfree.get(c - NG))
                                t2 = dve.tt(gl, s, gh.bitcast(F32), ALU.subtract, t1)
                                sfree[c % 2, c0] = t2
                                gready[c, c0] = [t1, t2]
                return Job([wi[c], wi[NF + c]], run)

            def down(fs):
                def run(tiles):
                    for d in range(8):
                        for c0, c1, j in segs:
                            b = db[cnt["d"] % len(db)]
                            cnt["d"] += 1
                            out = self.banks[b]
                            ws = slice(d * 128, (d + 1) * 128)
                            for i, (f, u) in enumerate(zip(fs, tiles)):
                                self.product(out, u, c0, i == 0, i == len(fs) - 1, ws, gv(f, c0),
                                             u.ready, gready[f, c0], dfree[b] if i == 0 else None)
                            done = self.pe.tok()
                            x = self.XT[:, d, c0:c1]
                            for o in ([out] if c0 == 0 else [out[:, 0:TC], out[:, TC:2 * TC]]):
                                dfree[b] = dve.stt(x, o, self.mod_g(mi, d, j), x, ALU.mult, ALU.add, done,
                                                   self.modt[mi, 2], dve.tok() if c0 else None)
                        if fs[-1] == NF - 1:
                            self.sums(d, w, dfree[b])
                    for u in tiles:
                        u.free = done
                    for f in fs:
                        gfree[f] = done
                return Job([wo[f] for f in fs], run)

            groups = [[0]] + [list(range(i, i + 3)) for i in range(1, NF, 3)]
            jobs = []
            gi = 0
            for c in range(NF):
                jobs.append(up(c))
                if c < 2:
                    jobs += early[4 * c:4 * c + 4]
                while gi < len(groups) and groups[gi][-1] < c and c > 2:
                    jobs.append(down(groups[gi]))
                    gi += 1
                n = -(-len(extra) // max(NF - 4 - c, 1)) if c > 1 else 0
                jobs += extra[:n]
                extra = extra[n:]
            for g in groups[gi:]:
                jobs.append(down(g))
            self.run_jobs(jobs)


    def final_norm(self, gname, store=None):
        self.barrier()
        last = []

        def emit(k, c0, c1, j, R, rt):
            t = self.dve.do(lambda e: e.scalar_tensor_tensor(
                self.XT[:, k, c0:c1], self.XT[:, k, c0:c1], self.vec(gname, k), R, ALU.mult, ALU.mult), rt)
            if store is None:
                self.sums(k, T, t)
            else:
                self.sp.dma(self.a["out"][:, k, :], self.XT[:, k, 0:T], store, t)

        self.norm([(0, T, 0)], emit)


    def projection(self, w, chunks, banks, segs_of, evac, XS=None):
        free = {b: None for b in banks}
        cnt = [0]
        xs = [None, None]

        def job(chs):
            def run(tiles):
                parts = [(ch, u, c0, c1) for ch, u in zip(chs, tiles) for c0, c1 in segs_of(ch)]
                bank = {}
                for ch, u, c0, c1 in parts:
                    bank[ch, c0] = banks[cnt[0] % len(banks)]
                    cnt[0] += 1

                def products(part, k):
                    ch, u, c0, c1 = part
                    b = bank[ch, c0]
                    self.product(self.banks[b], u, c0, k == 0, k == 7, slice(k * 128, (k + 1) * 128), self.h(k, c0),
                                 u.ready, self.ht[k, c0], free[b] if k == 0 else None)

                if len(chs) > 1:
                    for at in (0, T):
                        for k in range(8):
                            for part in parts:
                                if part[2] == at:
                                    products(part, k)
                for part in parts:
                    ch, u, c0, c1 = part
                    b = bank[ch, c0]
                    out = self.banks[b]
                    for k in range(8 if len(chs) == 1 else 0):
                        products(part, k)
                    done = self.pe.tok()
                    u.free = done
                    if c0 == 0:
                        self.advance()
                        free[b] = evac(ch, c0, c1, out, done)
                    else:
                        s = cnt[0] % 2
                        t = self.act.fn(XS[:, s, :], out[:, TC:2 * TC], ACT.Copy, done, xs[s])
                        t = free[b] = self.dve.tt(XS[:, s, :], XS[:, s, :], out[:, 0:TC], ALU.add, done, t)
                        xs[s] = evac(ch, c0, c1, XS[:, s, :], t)
            return Job([w[ch] for ch in chs], run)

        following, self.next = self.next, []
        self.lag = []
        self.run_jobs([job(chunks[0:2])] + [job([ch]) for ch in chunks[2:]])
        while self.lag:
            self.advance()
        self.next = following

    def follow(self, g):
        next(g)
        self.lag.append(g)

    def advance(self):
        self.lag = [g for g in self.lag if next(g, "end") != "end"]

    def out_projection(self, mi, w, MIX, mready):
        with self.scope() as ctx:
            self.barrier()
            self.unit_ring(NUNIT)
            MH = self.sb(ctx, self.name("MH"), [128, 8, T], F32R)
            ML = self.sb(ctx, self.name("ML"), [128, 8, T], F32R)
            self.tiles0 = [self.split(self.load(w[0]))]
            mt = []
            for k in range(8):
                t1 = self.act.do(lambda e, k=k: e.activation(MH[:, k, :], MIX[:, k, :], ACT.Copy), mready)
                t2 = self.dve.do(lambda e, k=k: e.tensor_tensor(ML[:, k, :], MIX[:, k, :], MH[:, k, :].bitcast(F32),
                                                                ALU.subtract), t1)
                mt.append([t1, t2])
            free = {}

            def job(d):
                def run(tiles):
                    u = tiles[0]
                    b = d % 3
                    out = self.banks[b]
                    for k in range(8):
                        ws = slice(k * 128, (k + 1) * 128)
                        self.mm3(out, (u.hi[:, ws], u.lo[:, ws]), (MH[:, k, :], ML[:, k, :]), k == 0, k == 7,
                                 u.ready, mt[k], free.get(b) if k == 0 else None)
                    u.free = self.pe.tok()
                    x = self.XT[:, d, 0:T]
                    free[b] = self.dve.do(lambda e: e.scalar_tensor_tensor(
                        x, out, self.mod_g(mi, d), x, ALU.mult, ALU.add), u.free, self.modt[mi, 2])
                    self.sums(d, T, free[b])
                return Job([w[d]], run)

            self.run_jobs([job(d) for d in range(8)])

    def mixer_pool(self, mi):
        PAD = 8
        W = T + 2 * PAD
        with self.scope() as ctx:
            self.tiles0, self.next = [self.split(self.load(w)) for w in self.next] or None, []
            self.barrier()
            sb = lambda n, s, dt=F32: self.sb(ctx, self.name(n), s, dt)
            H = sb("H", [128, 8, W])
            P2, P4, P8, PL = sb("P2", [128, 2, W]), sb("P4", [128, 2, W]), sb("P8", [128, 2, W]), sb("PL", [128, 2, 2, T])
            CNT = sb("CNT", [128, 4, T])
            WP = sb("WP", [128, 4, 2, 256])
            cw = self.chan()
            self.pool.dma(CNT[:, :, :], self.a["pool_cnt"], cw)
            self.pool.dma(WP[:, :, :, :], self.a["pool_w"], cw)
            dve, act, pe = self.dve, self.act, self.pe
            z0 = dve.do(lambda e: e.memset(H[:, :, 0:PAD], 0.0))
            z1 = dve.do(lambda e: e.memset(H[:, :, PAD + T:W], 0.0))
            TT = sb("TN", [128, 2, 512])
            free = [None, None]
            ht = {}

            def emit(k, c0, c1, j, R, rt):
                s = k % 2
                t = dve.do(lambda e: e.scalar_tensor_tensor(TT[:, s, :], self.XT[:, k, 0:T], self.mod_a(mi, k), R,
                                                            ALU.mult, ALU.mult), rt, free[s],
                             self.modt[mi, 0], self.modt[mi, 1])
                free[s] = ht[k] = act.do(lambda e: e.activation(H[:, k, PAD:PAD + T], TT[:, s, :], ACT.Identity,
                                                                bias=self.mod_b(mi, k)), t)

            self.norm([(0, T, 0)], emit)
            add = lambda o, x, y, *w: dve.tt(o, x, y, ALU.add, *w)
            plfree = {}
            late = []
            bfree = {}
            for g in range(4):
                wt = [ht[2 * g], ht[2 * g + 1], z0, z1]
                h = lambda lo, hi, g=g: H[:, 2 * g:2 * g + 2, lo:hi]
                t = add(P2[:, :, 1:W], h(0, W - 1), h(1, W), wt)
                S, lo = P2, 0
                if g >= 1:
                    t = add(P4[:, :, 2:W - 1], P2[:, :, 1:W - 2], P2[:, :, 3:W], t)
                    S = P4
                if g >= 2:
                    t = add(P8[:, :, 4:W - 3], P4[:, :, 2:W - 5], P4[:, :, 6:W - 1], t)
                    S = P8
                if g >= 3:
                    t = add(P2[:, :, 8:8 + T], P8[:, :, 4:4 + T], P8[:, :, 12:12 + T], t)
                    S = P2
                cb = CNT[:, g:g + 1, :].broadcast_to([128, 2, T])
                P = PL[:, g % 2, :, :]
                t = dve.tt(P, S[:, :, PAD:PAD + T], cb, ALU.mult, t, cw.tok(), plfree.get(g - 2))
                t = dve.tt(P, P, h(PAD, PAD + T), ALU.subtract, t)
                now = []
                for o in range(2):
                    b = 2 * (g % 2) + o
                    for i in range(2):
                        pe.mm(self.banks[b], WP[:, g, i, o * 128:(o + 1) * 128], PL[:, g % 2, i, :], i == 0, i == 1,
                              t, cw.tok(), bfree.get(b))
                    plfree[g] = pe.tok()
                    now.append((2 * g + o, b, plfree[g]))
                for k, b, done in late:
                    x = self.XT[:, k, 0:T]
                    bfree[b] = dve.stt(x, self.banks[b], self.mod_g(mi, k), x, ALU.mult, ALU.add, done, self.modt[mi, 2])
                    self.sums(k, T, bfree[b])
                late = now
            for k, b, done in late:
                x = self.XT[:, k, 0:T]
                t = dve.stt(x, self.banks[b], self.mod_g(mi, k), x, ALU.mult, ALU.add, done, self.modt[mi, 2])
                self.sums(k, T, t)


    def mixer_ab(self, mi):
        pe, act, dve, pool, a = self.pe, self.act, self.dve, self.pool, self.a
        W = T + TC
        with self.scope() as outer:
            self.barrier()
            sb = lambda n, s, dt=F32: self.sb(outer, self.name(n), s, dt)
            MIX = sb("MIX", [128, 8, T])
            QA, GRt = MIX[:, 0:4, :], MIX[:, 4:8, :]
            KA, VA = sb("KA", [128, W]), sb("VA", [128, 6, 128])
            GQt, GKt = sb("GQt", [128, 2, T]), sb("GKt", [128, 2, W])
            ZG = self.SA[0:32, :]
            VV = sb("VV", [128, 12, 2, 128])
            cc = self.chan()
            CB = sb("CB", [128, 384], BF16)
            WA = sb("WA", [32, 2, 256])
            pool.dma(WA[:, :, :], a["wa2"], cc)
            with ExitStack() as ctx:
                RT, TMP = MIX[:, 6:8, :], MIX[:, 5, :]
                XS = MIX[:, 4, :].rearrange("p (n t) -> p n t", t=TC)
                PR = self.sb(ctx, self.name("PR"), [128, 128], F32)
                pool.dma(RT, a["rope1"], cc)
                pool.dma(PR[:, :], a["perm1"], cc)
                segs = [(0, T, 0), (T, W, 1)]
                with ExitStack() as tmp:
                    CF = self.sb(tmp, self.name("CF"), [128, 384], F32)
                    pool.dma(CF[:, :], a["cb"][:, 0:384], cc)
                    act.fn(CB[:, :], CF[:, :], ACT.Copy, cc.tok())
                self.norm_split(ctx, mi, segs)
                VB = self.SQ[:, :, :]
                pfree = {6: None, 7: None}
                vbt, vbfree, nt = {}, {}, [0]
                tmpfree = [None]

                def tbank():
                    nt[0] += 1
                    return 6 + nt[0] % 2

                def rope(x, ready):
                    yield
                    b = tbank()
                    pe.mm(self.banks[b], PR[:, :], x, True, True, ready, pfree[b], cc.tok())
                    t = dve.tt(TMP, self.banks[b], RT[:, 1, :], ALU.mult, pe.tok(), tmpfree[0], cc.tok())
                    pfree[b] = t
                    t2 = dve.tt(x, x, RT[:, 0, :], ALU.mult, pe.tok(), ready)
                    tmpfree[0] = dve.tt(x, x, TMP, ALU.add, t, t2)

                def turn(c0, c1, t):
                    yield
                    b = tbank()
                    n = (c1 - c0) // 128
                    for i in range(n):
                        pe.tr(self.banks[b][:, i * 128:(i + 1) * 128], VB[:, 0, c0 + i * 128:c0 + (i + 1) * 128],
                              self.ID, t, pfree[b])
                    vbfree[0] = pe.tok()
                    pfree[b] = dve.cp(VA[:, c0 // 128:c0 // 128 + n, :],
                                      self.banks[b][:, 0:n * 128].rearrange("p (n f) -> p n f", f=128), vbfree[0])

                def halves(pair):
                    yield
                    for q in range(3):
                        b = tbank()
                        for i in range(4):
                            cl = (4 * q + i) * 64
                            for pr in range(2):
                                pe.mm(self.banks[b][64 * pr:64 * pr + 64, i * 128:(i + 1) * 128],
                                      VB[:, pr, cl:cl + 64], self.ID, True, True,
                                      vbt[pr, 0], vbt[pr, T], pfree[b])
                        vbfree[0] = vbfree[1] = pe.tok()
                        pfree[b] = dve.cp(VV[:, 4 * q:4 * q + 4, pair, :],
                                          self.banks[b].rearrange("p (n f) -> p n f", f=128), vbfree[0])

                grfree = []

                def evac(ch, c0, c1, out, done):
                    if ch == GR:
                        grfree[:] = [dve.tok(), act.tok()]
                    if ch < AK:
                        t = act.fn(QA[:, ch, :], out, ACT.Copy, done)
                        self.follow(rope(QA[:, ch, :], t))
                    elif ch == AK:
                        t = act.fn(KA[:, c0:c1], out, ACT.Copy, done)
                        if c0 == 0:
                            self.follow(rope(KA[:, 0:T], t))
                    elif ch == AV:
                        t = act.fn(VB[:, 0, c0:c1], out, ACT.Copy, done, vbfree.get(0))
                        self.follow(turn(c0, c1, t))
                    elif ch < GK:
                        t = act.fn(GQt[:, ch - GQ, :], out, ACT.Copy, done)
                    elif ch < GV:
                        t = act.fn(GKt[:, ch - GK, c0:c1], out, ACT.Copy, done)
                    elif ch < GR:
                        pair, par = (ch - GV) // 2, (ch - GV) % 2
                        t = act.fn(VB[:, par, c0:c1], out, ACT.Copy, done, vbfree.get(par))
                        vbt[par, c0] = t
                        if par == 1 and c0 == T:
                            self.follow(halves(pair))
                    elif ch < GZ:
                        t = act.fn(GRt[:, ch - GR, :], out, ACT.Silu, done, grfree)
                    else:
                        t = act.fn(ZG[:, c0:c1], out[0:32, :], ACT.Copy, done)
                    return t

                xc = lambda ch: [(0, T)] if ch < AK or GQ <= ch < GK or GR <= ch < GZ else [(0, T), (T, W)]
                self.projection(a["w_in"], [GZ, AV, AK, 0, 1, 2, 3] + list(range(GQ, GZ)), (0, 1, 2, 3), xc, evac, XS)
            with ExitStack() as both:
                self.barrier()
                gla = self.gla(both, GQt, GKt, GRt, ZG, WA, VV, MIX, cc)
                self.side_by_side(self.window(both, QA, KA, VA, CB, MIX), gla)
            self.out_ready = self.act.tok(), self.dve.tok()
            self.out_projection(mi, a["w_out"], MIX, list(self.out_ready))

    def window(self, ctx, QA, KA, VA, CB, MIX):
        self.window_on = True
        pe, act, dve = self.pe, self.act, self.dve
        IDB, ML = CB[:, 0:128], CB[:, 128:384]
        sb = lambda n, s: self.sb(ctx, self.name(n), s, F32)
        P, PT, ON = sb("P", [128, 2, 640]), sb("PT", [128, 3, 640]), sb("ON", [128, 2, 512])
        MX, NM, DEN, ES = (sb(n, [128, 2, 8]) for n in ("MX", "NM", "DEN", "ES"))
        SK, NSK, SD = sb("SK", [128, 8]), sb("NSK", [128, 8]), sb("SD", [8, 8])
        t = dve.ts(SD[:, :], self.ID[0:8, 0:8], self.VT[0:8, VOFF["sink"]:VOFF["sink"] + 1], None, ALU.mult, None)
        pe.mm(self.banks[6][:, 0:8], self.ONE[0:8, :], SD[:, :], True, True, t)
        t = dve.cp(SK[:, :], self.banks[6][:, 0:8], pe.tok())
        skt = dve.ts(NSK[:, :], SK[:, :], -1.0, None, ALU.mult, None, t)
        units = [(n, j, par) for n in range(4) for j in range(4) for par in range(2)]
        sfree, pfree, ptpfree, ptfree = {}, {}, None, {}
        expt, evt, pvt, maxt = {}, {}, {}, {}
        ofree, onfree = skt, {}
        statfree = {}

        def blocks(n):
            return list(range(max(0, n - 1), min(4, n + 2)))

        for u in range(len(units) + 2):
            if u < len(units):
                n, j, par = units[u]
                rows = slice(64 * par, 64 * par + 64)
                bl = blocks(n)
                nk = 128 * len(bl)
                w = self.wide[u % 2]
                q = QA[rows, j, n * 128:(n + 1) * 128]
                pe.mm(w[:, 512 - nk:512], q, KA[rows, bl[0] * 128:bl[0] * 128 + nk], True, True, sfree.get(u % 2))
                edge = []
                if n > 0:
                    edge.append((512 - nk, 0))
                if n < 3:
                    edge.append((384, 1))
                for i, (o, m) in enumerate(edge):
                    pe.mm(w[:, o:o + 128], IDB, ML[:, m * 128:(m + 1) * 128], False, True, share=True)
                pe.mm(w[:, 512:768], q, KA[rows, T:T + TC], True, True)
                ts_ = pe.tok()
                hs = 2 * j + par
                s = n % 2
                view = w[:, 512 - nk:768]
                tm = dve.maxr(MX[:, s, hs:hs + 1], view, ts_, statfree.get(n - 2))
                h = j + 4 * par
                tm = maxt[u] = dve.ts(NM[:, s, hs:hs + 1], MX[:, s, hs:hs + 1], -0.125, NSK[:, h:h + 1],
                                      ALU.mult, ALU.min, tm)
                expt[u] = sfree[u % 2] = act.fn(P[:, u % 2, 0:nk + 256], view, ACT.Exp, tm, pfree.get(u % 2),
                                                bias=NM[:, s, hs:hs + 1], scale=0.125, acc=DEN[:, s, hs:hs + 1])
            if 1 <= u <= len(units):
                v = u - 1
                n, j, par = units[v]
                nb = len(blocks(n)) + 2
                for i in range(nb):
                    pe.tr(self.banks[4 + i // 4][:, i % 4 * 128:i % 4 * 128 + 128], P[:, v % 2, i * 128:(i + 1) * 128],
                          self.ID, expt[v], ptpfree)
                pfree[v % 2] = pe.tok()
                t1 = act.fn(PT[:, v % 3, 0:512], self.banks[4], ACT.Copy, pfree[v % 2], ptfree.get(v % 3))
                evt[v] = [t1]
                if nb == 5:
                    evt[v].append(dve.cp(PT[:, v % 3, 512:640], self.banks[5][:, 0:128], pfree[v % 2], ptfree.get(v % 3)))
                ptpfree = evt[v]
            if u >= 2:
                v = u - 2
                n, j, par = units[v]
                hs = 2 * j + par
                bl = blocks(n) + [4, 5]
                for i, b in enumerate(bl):
                    pe.mm(self.banks[6][:, hs * 64:hs * 64 + 64], PT[:, v % 3, i * 128:(i + 1) * 128],
                          VA[:, b, par * 64:par * 64 + 64], i == 0, i == len(bl) - 1, evt[v],
                          ofree if hs == 0 and i == 0 else None)
                ptfree[v % 3] = pe.tok()
                if hs == 7:
                    s = n % 2
                    t = dve.do(lambda e, s=s: e.tensor_tensor(ES[:, s, 0:8:2], SK[:, 0:4], NM[:, s, 0:8:2], ALU.add),
                               maxt[v])
                    t2 = dve.do(lambda e, s=s: e.tensor_tensor(ES[:, s, 1:8:2], SK[:, 4:8], NM[:, s, 1:8:2], ALU.add),
                                maxt[v])
                    t = act.fn(ES[:, s, :], ES[:, s, :], ACT.Exp, t, t2)
                    t = dve.tt(DEN[:, s, :], DEN[:, s, :], ES[:, s, :], ALU.add, t, expt[v])
                    t = dve.recip(DEN[:, s, :], DEN[:, s, :], t)
                    o3 = self.banks[6].rearrange("p (h d) -> p h d", d=64)
                    rb = DEN[:, s, :].rearrange("p (h o) -> p h o", o=1).broadcast_to([128, 8, 64])
                    t = ofree = statfree[n] = dve.tt(ON[:, s, :].rearrange("p (h d) -> p h d", d=64), o3, rb,
                                                     ALU.mult, t, ptfree[v % 3], onfree.get(s))
                    yield
                    for c in range(4):
                        pe.tr(self.banks[4][:, c * 128:(c + 1) * 128], ON[:, s, c * 128:(c + 1) * 128], self.ID,
                              t, ptpfree)
                    onfree[s] = pe.tok()
                    ptpfree = act.fn(MIX[:, 0:4, n * 128:(n + 1) * 128],
                                    self.banks[4].rearrange("p (c t) -> p c t", t=128), ACT.Copy, onfree[s])
            yield
        self.window_on = False

    def gla(self, ctx, GQt, GKt, GRt, ZG, WA, VV, MIX, cc):
        pe, act, dve, pool = self.pe, self.act, self.dve, self.pool
        W = T + TC
        banks = self.banks
        sb = lambda n, s, dt=F32: self.sb(ctx, self.name(n), s, dt)
        GN = [sb(f"GN{d}", [128, 2, W]) for d in range(2)]
        KE = sb("KE", [128, 2, W])
        ST = self.over_ring("ST", [128, 2, 10, 256], F32, 0)
        QT = self.over_ring("QT", [128, 2, 2, T], F32, 20480)
        KT = self.over_ring("KT", [128, 2, 2, T], F32, 28672)
        KEN = [sb(f"KEN{d}", [128, 12, 2, 64]) for d in range(2)]
        DEC = sb("DEC", [128, 2, 2, 12])
        SM = sb("SM", [128, 2, W])
        AS = self.over_ring("AS", [128, 2, 256], F32, 36864)
        AB = self.over_ring("AB", [128, 2, 128], F32, 39936)
        MK = self.over_ring("MK", [128, 256], I32, 38912)
        ck = self.chan()
        pool.dma(MK[:, :], self.a["gla_mask"], ck)
        z = [pool.fill(SM[:, :, :], 1.0)]
        z = [pool.do(lambda e: e.memset(SM[:, 0, 0:W:64], 0.0), z), pool.do(lambda e: e.memset(SM[:, 1, 63:W:64], 0.0), z),
             pool.fill(AS[:, :, :], 0.0)]
        bfree = {}
        gt = {}
        nb = 0
        E = self.SQ[:, :, 0:T]
        efree = [None]
        for d in range(2):
            bias = self.vec("b_a_f" if d == 0 else "b_a_b", 0, 2)
            for p in range(2):
                for c0, c1 in ((0, T), (T, W)):
                    b = 7
                    nb += 1
                    out = banks[b][:, 0:c1 - c0]
                    pe.mm(out, WA[:, d, p * 128:(p + 1) * 128], ZG[:, c0:c1], True, True, bfree.get(b), cc.tok())
                    bp = bias[:, p:p + 1]
                    g = GN[d][:, p, c0:c1]
                    ab = KE[:, p, c0:c1]
                    t1 = act.fn(ab, out, ACT.Abs, pe.tok(), gt.get((d - 1, p)), bias=bp)
                    t2 = bfree[b] = dve.ts(g, out, bp, 0.0, ALU.add, ALU.min, t1)
                    t1 = act.fn(ab, ab, ACT.Exp, t1, scale=-1.0)
                    t1 = act.fn(ab, ab, ACT.Ln, t1, bias=1.0)
                    t = dve.stt(g, g, -1.0, ab, ALU.mult, ALU.add, t1, t2)
                    yield
                g, m = GN[d][:, p, :], SM[:, d, :]
                if d == 1:
                    g, m = g[:, ::-1], m[:, ::-1]
                gt[d, p] = dve.scan(g, m, g, 0.0, ALU.mult, ALU.add, t, z)
        ready = {}
        for d in range(2):
            G = GN[d]
            gs = [gt[d, 0], gt[d, 1]]
            ge = G[:, :, 63:W:64] if d == 0 else G[:, :, 0:W:64]
            dec = act.fn(DEC[:, d, :, :], ge, ACT.Exp, gs, scale=-0.0625)
            t = act.fn(E, G[:, :, 0:T], ACT.Exp, gs, efree[0], scale=-0.0625)
            yield
            tq = dve.stt(QT[:, d, :, :], GQt[:, :, :], 0.125, E, ALU.mult, ALU.mult, t)
            t = act.fn(E, G[:, :, 0:T], ACT.Exp, gs, tq, scale=0.0625)
            yield
            tk = efree[0] = dve.tt(KT[:, d, :, :], GKt[:, :, 0:T], E, ALU.mult, t)
            t = None
            for p in range(2):
                last = ge[:, p, :].rearrange("p (c o) -> p c o", o=1).broadcast_to([128, 12, 64])
                k3 = KE[:, p, :].rearrange("p (c t) -> p c t", t=64)
                t = dve.tt(k3, G[:, p, :].rearrange("p (c t) -> p c t", t=64), last, ALU.subtract, gs, gt[1, 1],
                           ready.get((d - 1, "ken")))
            yield
            t = act.fn(KE[:, :, :], KE[:, :, :], ACT.Exp, t, scale=0.0625)
            yield
            t = dve.tt(KE[:, :, :], KE[:, :, :], GKt[:, :, :], ALU.mult, t)
            kt = []
            for q in range(3):
                b = 7
                nb += 1
                for i in range(4):
                    cl = (4 * q + i) * 64
                    for p in range(2):
                        for par in range(2):
                            r = slice(64 * par, 64 * par + 64)
                            o = (i * 2 + p) * 64
                            pe.mm(banks[b][r, o:o + 64], KE[r, p, cl:cl + 64], self.ID[r, r], True, True, t, bfree.get(b))
                tt_ = pe.tok()
                bfree[b] = act.fn(KEN[d][:, 4 * q:4 * q + 4, :, :],
                                  banks[b].rearrange("p (c q f) -> p c q f", q=2, f=64), ACT.Copy, tt_)
                kt.append(bfree[b])
                yield
            ready[d] = (tq, tk, kt, dec)
            ready[d, "ken"] = tt_
        seq = [[8, 9, 10, 11] + list(range(8)), [11, 10, 9, 8] + list(range(7, -1, -1))]
        slot = lambda d, i: seq[d][i] if i >= 4 else 8 + i % 2
        stt_ = {}
        for i in range(11):
            for d in range(2):
                c = seq[d][i]
                for p in range(2):
                    for par in range(2):
                        r = slice(64 * par, 64 * par + 64)
                        pe.mm(banks[7][r, d * 256 + p * 128:d * 256 + (p + 1) * 128], KEN[d][r, c, p, :], VV[r, c, p, :],
                              True, True, ready[d][2], bfree[7])
            done = pe.tok()
            for d in range(2):
                c = seq[d][i]
                new = ST[:, d, slot(d, i + 1), :]
                if i == 0:
                    t = dve.cp(new, banks[7][:, d * 256:d * 256 + 256], done)
                else:
                    old = ST[:, d, slot(d, i), :]
                    for p in range(2):
                        ps = slice(p * 128, (p + 1) * 128)
                        t = dve.stt(new[:, ps], old[:, ps], DEC[:, d, p, c:c + 1],
                                    banks[7][:, d * 256 + p * 128:d * 256 + (p + 1) * 128], ALU.mult, ALU.add,
                                    done, stt_[d, i], ready[d][3])
                stt_[d, i + 1] = t
            bfree[7] = t
            yield
        while self.window_on:
            yield
        sdone = {d: stt_[d, 11] for d in range(2)}
        asfree = {}
        attm = {}

        def att(c):
            b = c % 2
            cl = slice(c * 64, c * 64 + 64)
            for d in range(2):
                for p in range(2):
                    for par in range(2):
                        r = slice(64 * par, 64 * par + 64)
                        o = (d * 2 + p) * 64
                        pe.mm(banks[b][r, o:o + 64], KT[r, d, p, cl], QT[r, d, p, cl], True, True,
                              ready[d][0], ready[d][1], bfree.get(b))
            t = bfree[b] = dve.do(
                lambda e: e.copy_predicated(AS[:, c % 2, :], MK[:, :], banks[b][:, 0:256]),
                pe.tok(), attm.get(c - 2), z, ck.tok())
            attm[c] = dve.tt(AB[:, c % 2, :], AS[:, c % 2, 0:128], AS[:, c % 2, 128:256], ALU.add, t, asfree.get(c % 2))

        for b in range(8):
            bfree[b] = [bfree.get(b), self.dve.tok(), self.act.tok()]
        att(0)
        for c in range(8):
            if c < 7:
                att(c + 1)
            cl = slice(c * 64, c * 64 + 64)
            for p in range(2):
                for par in range(2):
                    r = slice(64 * par, 64 * par + 64)
                    out = banks[4 + 2 * p + par][:, cl]
                    pe.mm(out, VV[r, c, p, :], AB[r, c % 2, p * 64:p * 64 + 64], True, False, attm[c],
                          bfree[7] if c == 0 else None, share=True)
                    for d in range(2):
                        pe.mm(out, ST[r, d, c, p * 128:(p + 1) * 128], QT[r, d, p, cl], False, d == 1, sdone[d],
                              share=True)
            asfree[c % 2] = pe.tok()
        done = pe.tok()
        fq = [efree[0], ready[1][1]]
        for h in range(4):
            t = act.fn(E[:, h % 2, :], banks[4 + h], ACT.Square, done, fq, asfree.get(("e", h % 2)))
            pe.mm(banks[0][0:4, :], self.Z11[:, 5 - h:9 - h], E[:, h % 2, :], h == 0, True, t, attm[6], attm[7],
                  bfree.get(0), share=h > 0)
            asfree["e", h % 2] = pe.tok()
        R4 = SM[0:4, 0, 0:T]
        t = self.rstd_into(R4, SM[0:4, 1, 0:T], banks[0][0:4, :], 128, pe.tok())[1]
        RS = KE[:, :, 0:T]
        mt = {}
        for h in range(4):
            b = 1 + h % 2
            pe.mm(banks[b], self.SEL6[0:4, h, :], R4, True, True, t, attm[6], attm[7], mt.get(h - 2))
            w = act.fn(RS[:, h % 2, :], banks[4 + h], ACT.Copy, mt.get(h - 2), scale=self.vec("gla_g"))
            w = dve.tt(RS[:, h % 2, :], RS[:, h % 2, :], GRt[:, h, :], ALU.mult, w)
            mt[h] = dve.tt(MIX[:, 4 + h, :], RS[:, h % 2, :], banks[b], ALU.mult, w, pe.tok())

    def mixer_hybrid(self, mi):
        pe, act, dve, pool, a = self.pe, self.act, self.dve, self.pool, self.a
        banks = self.banks
        with self.scope() as outer:
            self.barrier()
            sb = lambda n, s, dt=F32: self.sb(outer, self.name(n), s, dt)
            MIX = sb("MIX", [128, 8, T])
            MQt, MKt, MVt, MOt = sb("MQt", [128, 2, T]), sb("MKt", [128, 2, T]), sb("MVt", [128, 4, 512]), MIX[:, 0:4, :]
            DQt, DKt, DVt = MIX[:, 4:8, :], sb("DKt", [128, 4, T]), sb("DVt", [128, 4, 512])
            GT = sb("GT", [4, 4, T])
            cc = self.chan()
            with ExitStack() as ctx:
                RT = self.sb(ctx, self.name("RT"), [128, 2, T], F32)
                PR = self.sb(ctx, self.name("PR"), [128, 256], F32)
                GQ8 = self.sb(ctx, self.name("GQ8"), [128, 1], F32)
                pool.dma(RT[:, :, :], a["rope2"], cc)
                pool.dma(PR[:, :], a["perm2"], cc)
                gq8 = dve.ts(GQ8[:, :], self.vec("g_q_2"), 0.125, None, ALU.mult, None)
                self.norm_split(ctx, mi, [(0, T, 0)])
                CF = self.SQ[:, :, :].rearrange("p n t -> p (n t)")[:, T:T + 1024]
                cf = self.chan()
                pool.dma(CF[:, 0:128], a["cb"][:, 0:128], cf, list(self.sqfree))
                pool.dma(CF[:, 128:1024], a["cb"][:, 384:1280], cf)
                VB = self.SQ[:, 0, 0:T]
                TMP = self.sb(ctx, self.name("TMP"), [128, 3, T], F32)
                pfree = {5: None, 6: None, 7: None}
                free = {"vb": None, "tmp": None, "sq": None, "rs": None}
                nt = [0]

                def tbank():
                    nt[0] += 1
                    return 5 + nt[0] % 3

                def normed_rope(x, gain, t):
                    SQ, RS, TM = TMP[:, 0, :], TMP[:, 1, :], TMP[:, 2, :]
                    t1 = act.fn(SQ, x, ACT.Square, t, free["sq"])
                    yield
                    b = tbank()
                    pe.mm(banks[b], PR[:, 128:256], SQ, True, True, t1, pfree[b], cc.tok())
                    free["sq"] = pe.tok()
                    t1 = pfree[b] = act.fn(RS, banks[b], ACT.Sqrt, free["sq"], free["rs"], scale=1.0 / 64, bias=self.EPSC)
                    t1 = dve.recip(RS, RS, t1)
                    t1 = free["rs"] = dve.stt(x, x, gain, RS, ALU.mult, ALU.mult, t1, gq8)
                    yield
                    b = tbank()
                    pe.mm(banks[b], PR[:, 0:128], x, True, True, t1, pfree[b])
                    t2 = pfree[b] = dve.tt(TM, banks[b], RT[:, 1, :], ALU.mult, pe.tok(), free["tmp"], cc.tok())
                    t3 = dve.tt(x, x, RT[:, 0, :], ALU.mult, pe.tok())
                    free["tmp"] = dve.tt(x, x, TM, ALU.add, t2, t3)

                def token_major(V, h, out, done):
                    t = act.fn(VB, out, ACT.Copy, done, free["vb"])
                    vt.append(t)
                    yield
                    b = tbank()
                    for i in range(4):
                        pe.tr(banks[b][:, i * 128:(i + 1) * 128], VB[:, i * 128:(i + 1) * 128], self.ID, t, pfree[b])
                    free["vb"] = pe.tok()
                    pfree[b] = dve.cp(V[:, :, h * 128:(h + 1) * 128], banks[b].rearrange("p (n f) -> p n f", f=128), free["vb"])

                vt = []

                def evac(ch, c0, c1, out, done):
                    if ch < MK:
                        return act.fn(MQt[:, ch - MQ, :], out, ACT.Copy, done)
                    if ch < MV:
                        return act.fn(MKt[:, ch - MK, :], out, ACT.Copy, done, scale=0.125)
                    if ch < MO:
                        self.follow(token_major(MVt, ch - MV, out, done))
                        return vt[-1]
                    if ch < MG:
                        return act.fn(MOt[:, ch - MO, :], out, ACT.Sigmoid, done)
                    if ch == MG:
                        for g in range(4):
                            o = VOFF["gate_bias_2"] + g
                            t = act.fn(GT[:, g, :], out[32 * g:32 * g + 4, :], ACT.Identity, done, bias=self.VT[0:4, o:o + 1])
                        return t
                    if ch < DV:
                        X, i, gain = (DQt, ch - DQ, GQ8[:, :]) if ch < DK else (DKt, ch - DK, self.vec("g_k_2"))
                        t = act.fn(X[:, i, :], out, ACT.Copy, done)
                        self.follow(normed_rope(X[:, i, :], gain, t))
                        return t
                    self.follow(token_major(DVt, ch - DV, out, done))
                    return vt[-1]

                rest = list(range(DV, NIN2)) + list(range(MQ, MG))
                order = [MG]
                for i in range(8):
                    order += [DQ + i] + rest[2 * i:2 * i + 2]
                self.projection(a["w_in_2"], order, (0, 1, 2, 3),
                                lambda ch: [(0, T)], evac)
            with ExitStack() as both:
                self.barrier()
                self.side_by_side(self.mlstm(both, MQt, MKt, MVt, MOt, GT, MIX), self.dilated(both, DQt, DKt, DVt, MIX, CF, cf), extra=5)
            self.out_projection(mi, a["w_out_2"], MIX, [act.tok(), dve.tok()])

    def side_by_side(self, *parts, extra=0):
        parts, n = list(parts), 0
        while parts:
            n += 1
            parts = [g for g in parts if next(g, "end") != "end"]
            if extra and n % extra == 0 and len(parts) == 2:
                next(parts[0], None)

    def mlstm(self, ctx, Q, K, V, O, GT, MIX):
        pe, act, dve, pool = self.pe, self.act, self.dve, self.pool
        banks = self.banks
        sb = lambda n, s, dt=F32: self.sb(ctx, self.name(n), s, dt)
        U, EM = sb("U", [4, 2, T]), sb("EM", [4, 2, T])
        B, MG_, ON = sb("B", [4, T]), sb("MG", [4, 2, T]), sb("ON1", [4, T])
        R = U
        UT = sb("UT", [128, 8, 4])
        MB = self.over_ring("MB", [128, 8, T], F32, 0)
        NUM = self.over_ring("NUM", [128, 8, T], F32, 16384)
        MD = self.over_ring("MD", [128, 2, T], F32, 32768)
        A = sb("A", [128, 4, T])
        SEL, OH, MKD = sb("SEL", [4, 4, 128]), sb("OH", [128, 71]), sb("MKD", [128, 2, 128])
        ck = self.chan()
        pool.dma(SEL[:, :, :], self.a["sel"], ck)
        pool.dma(OH[:, :], self.a["onehot"], ck)
        pool.dma(MKD[:, :, :], self.a["tri"], ck)
        one = pool.fill(ON[:, :], 1.0)
        QK, DEN = 0, 3
        bfree = {}
        bt = {}
        emt = {}
        ut = []
        t = [act.fn(EM[:, d, :], GT[:, 2 * d + 1, :], ACT.Abs) for d in range(2)]
        t = [act.fn(EM[:, d, :], EM[:, d, :], ACT.Exp, t[d], scale=-1.0) for d in range(2)]
        t = [act.fn(EM[:, d, :], EM[:, d, :], ACT.Ln, t[d], bias=1.0) for d in range(2)]
        yield
        for d in range(2):
            li, z = GT[:, 2 * d, :], GT[:, 2 * d + 1, :]
            ab = EM[:, d, :]
            rv = (lambda x: x) if d == 0 else (lambda x: x[:, ::-1])
            w = dve.stt(z, z, 0.0, ab, ALU.min, ALU.subtract, t[d])
            w = dve.scan(rv(B[:, :]), ON[:, :], rv(z), 0.0, ALU.mult, ALU.add, w, one, bt.get(0))
            w = dve.tt(U[:, d, :], li, B[:, :], ALU.subtract, w)
            u = rv(U[:, d, :])
            w = dve.scan(rv(MG_[:, d, :]), u, u, -BIG, ALU.max, ALU.max, w)
            bt[d] = dve.tt(ab, B[:, :], MG_[:, d, :], ALU.add, w)
            yield
            emt[d] = act.fn(ab, ab, ACT.Exp, bt[d], scale=-1.0)
            for s in range(4):
                pe.tr(banks[QK][:, (d * 4 + s) * 4:(d * 4 + s) * 4 + 4], U[:, d, s * 128:(s + 1) * 128],
                      self.ID[0:4, 0:4], w)
            ut.append(pe.tok())
            yield
        ut = bfree[QK] = dve.cp(UT[:, :, :], banks[QK][:, 0:32].rearrange("p (s h) -> p s h", h=4), ut)
        mbt = {}
        for h in range(4):
            for d in range(2):
                b = 1 + d
                pe.mm(banks[b], SEL[:, h, :], MG_[:, d, :], True, True, bt[0], bt[1], bfree.get(b), ck.tok())
                mbt[d, h] = bfree[b] = act.fn(MB[:, d * 4 + h, :], banks[b], ACT.Copy, pe.tok())
            yield
        afree, mdfree, numt = {}, {}, {}
        nfree = {1: bfree[1], 2: bfree[2]}
        na = 0
        prev = []

        def sums(item):
            h, j, d, s, full, t = item
            b = 1 + d
            x = A[:, s, full]
            pe.mm(banks[b][:, full], V[:, j, h * 128:(h + 1) * 128], x, j == 0, True, t,
                  nfree[b] if j == 0 else None, share=j > 0)
            c = 32 * d + h
            pe.mm(banks[DEN][0:36, full], OH[:, 35 - c:71 - c], x, h + j + d == 0, True, ck.tok(), share=h + j + d > 0)
            afree[s] = pe.tok()
            if j == 3:
                numt[h, d] = nfree[b] = act.fn(NUM[:, d * 4 + h, :], banks[b], ACT.Copy, afree[s])

        for h in range(4):
            p, par = h // 2, h % 2
            r = slice(64 * par, 64 * par + 64)
            mdt = {}
            for d in range(2):
                m = MKD[:, d:d + 1, :].broadcast_to([128, 4, 128])
                mdt[d] = dve.tt(MD[:, d, :].rearrange("p (n t) -> p n t", t=128),
                                MB[:, d * 4 + h, :].rearrange("p (n t) -> p n t", t=128), m, ALU.add,
                                mbt[d, h], ck.tok(), mdfree.get(d))
            for j in range(4):
                js = slice(j * 128, j * 128 + 128)
                ex = []
                for d in range(2):
                    s = na % 4
                    na += 1
                    ub = UT[:, d * 4 + j, h:h + 1]
                    t1 = mdfree[d] = act.fn(A[:, s, js], MD[:, d, js], ACT.Exp, mdt[d], ut, afree.get(s), bias=ub, scale=-1.0)
                    off = slice((j + 1) * 128, T) if d == 0 else slice(0, j * 128)
                    if off.stop > off.start:
                        t1 = act.fn(A[:, s, off], MB[:, d * 4 + h, off], ACT.Exp, afree.get(s), bias=ub, scale=-1.0)
                    ex.append((s, t1))
                pe.mm(banks[QK], K[r, p, js], Q[r, p, :], True, True, bfree[QK])
                qt = pe.tok()
                yield
                for x in prev:
                    sums(x)
                prev = []
                bfree[QK] = []
                for d, (s, t1) in enumerate(ex):
                    full = slice(j * 128, T) if d == 0 else slice(0, (j + 1) * 128)
                    t = dve.tt(A[:, s, full], A[:, s, full], banks[QK][:, full], ALU.mult, t1, qt)
                    bfree[QK].append(t)
                    prev.append((h, j, d, s, full, t))
                yield
        for x in prev:
            sums(x)
        rt = {}
        last = pe.tok()
        for d in range(2):
            t = act.fn(R[:, d, :], banks[DEN][32 * d:32 * d + 4, :], ACT.Abs, last)
            t = dve.tt(R[:, d, :], R[:, d, :], EM[:, d, :], ALU.max, t, emt[d])
            rt[d] = dve.recip(R[:, d, :], R[:, d, :], t)
            yield
        for h in range(4):
            t = []
            for d in range(2):
                b = 1 + d
                pe.mm(banks[b], SEL[:, h, :], R[:, d, :], True, True, rt[d], bfree[b], nfree[b])
                x = NUM[:, d * 4 + h, :]
                bfree[b] = dve.tt(x, x, banks[b], ALU.mult, pe.tok(), numt[h, d])
                t.append(bfree[b])
            x = NUM[:, h, :]
            t = dve.tt(x, x, NUM[:, 4 + h, :], ALU.add, t)
            yield
            sq = act.fn(A[:, h, :], x, ACT.Square, t, afree[h])
            pe.mm(banks[QK][0:4, :], OH[:, 35 - h:39 - h], A[:, h, :], h == 0, True, sq, bfree[QK], share=h > 0)
        bfree[QK], rt = self.rstd_into(R[:, 0, :], MG_[:, 0, :], banks[QK][0:4, :], 128, pe.tok())
        for h in range(4):
            b = h % 3
            pe.mm(banks[b], SEL[:, h, :], R[:, 0, :], True, True, rt, bfree[b])
            x = NUM[:, h, :]
            t = bfree[b] = dve.stt(x, x, self.vec("g_mh_2", h), banks[b], ALU.mult, ALU.mult, pe.tok())
            dve.tt(MIX[:, h, :], x, O[:, h, :], ALU.mult, t)
            yield

    def dilated(self, ctx, Q, K, V, MIX, CF, cf):
        pe, act, dve, pool = self.pe, self.act, self.dve, self.pool
        banks = self.banks
        sb = lambda n, s, dt=F32: self.sb(ctx, self.name(n), s, dt)
        CB, CM = sb("CB", [128, 1024], BF16), sb("CM", [128, 896])
        PT, ON = sb("PT", [128, 3, 512]), sb("ON", [128, 2, 512])
        NM, DEN = sb("NM", [128, 2, 8]), sb("DEN", [128, 2, 8])
        ck = self.chan()
        P = self.SQ[:, :, :].rearrange("p n t -> p (n t)").rearrange("p (n t) -> p n t", t=512)
        pool.dma(CM[:, :], self.a["dil_count"], ck)
        cbt = act.fn(CB[:, :], CF, ACT.Copy, cf.tok())
        units = [(n, j, par) for n in range(4) for j in range(4) for par in range(2)]
        sfree, pfree, ptfree, pbfree, expt, pt_, evt, onfree, statfree = {}, {}, {}, None, {}, {}, {}, {}, {}
        ofree = None
        for u in range(len(units) + 3):
            if 1 <= u <= len(units):
                v = u - 1
                n, j, par = units[v]
                o = 384 - 128 * n
                hs, s = 2 * j + par, n % 2
                x = P[:, v % 3, :]
                pt_[v] = dve.stt(x, x, 1.0, CM[:, o:o + 512], ALU.mult, ALU.mult, expt[v], ck.tok(),
                                 statfree.get(n - 2), acc=DEN[:, s, hs:hs + 1])
            if u < len(units):
                n, j, par = units[u]
                r = slice(64 * par, 64 * par + 64)
                b = 4 + u % 2
                o = 384 - 128 * n
                hs, s = 2 * j + par, n % 2
                pe.mm(banks[b], Q[r, j, n * 128:(n + 1) * 128], K[r, j, :], True, True, sfree.get(b))
                pe.mm(banks[b], CB[:, 0:128], CB[:, 128 + o:128 + o + 512], False, True, cbt, share=True)
                t = dve.maxr(NM[:, s, hs:hs + 1], banks[b], pe.tok(), statfree.get(n - 2), negate=True)
                expt[u] = sfree[b] = act.fn(P[:, u % 3, :], banks[b], ACT.Exp, t, pfree.get(u % 3), cbt,
                                            bias=NM[:, s, hs:hs + 1])
            if 1 <= u <= len(units):
                v = u - 1
                for i in range(4):
                    pe.tr(banks[6][:, i * 128:(i + 1) * 128], P[:, v % 3, i * 128:(i + 1) * 128], self.ID,
                          pt_[v], pbfree)
                pfree[v % 3] = pe.tok()
                evt[v] = pbfree = act.fn(PT[:, v % 3, :], banks[6], ACT.Copy, pfree[v % 3], ptfree.get(v % 3))
            if 2 <= u <= len(units) + 1:
                v = u - 2
                n, j, par = units[v]
                hs, s = 2 * j + par, n % 2
                for i in range(4):
                    pe.mm(banks[7][:, hs * 64:hs * 64 + 64], PT[:, v % 3, i * 128:(i + 1) * 128],
                          V[:, i, hs * 64:hs * 64 + 64], i == 0, i == 3, evt[v], ofree if hs == 0 and i == 0 else None)
                ptfree[v % 3] = pe.tok()
                if hs == 7:
                    t = dve.recip(DEN[:, s, :], DEN[:, s, :], pt_[v])
                    rb = DEN[:, s, :].rearrange("p (h o) -> p h o", o=1).broadcast_to([128, 8, 64])
                    t = ofree = statfree[n] = dve.tt(ON[:, s, :].rearrange("p (h d) -> p h d", d=64),
                                                     banks[7].rearrange("p (h d) -> p h d", d=64), rb,
                                                     ALU.mult, t, ptfree[v % 3], onfree.get(s))
                    yield
                    for c in range(4):
                        pe.tr(banks[6][:, c * 128:(c + 1) * 128], ON[:, s, c * 128:(c + 1) * 128], self.ID, t, pbfree)
                    onfree[s] = pe.tok()
                    pbfree = act.fn(MIX[:, 4:8, n * 128:(n + 1) * 128], banks[6].rearrange("p (c t) -> p c t", t=128),
                                    ACT.Copy, onfree[s])
            yield

    def program(self):
        a = self.a
        st = self.stages
        self.setup()
        X = [(0, T, 0)]
        XC = [(0, T, 0), (T, T + TC, 1)]
        up = lambda w: [w[0], w[NF]]
        plan = {"f0": up(a["ffn1_wi"][0]), "m0": [a["w_in"][GZ], a["w_in"][AV]], "f1": up(a["ffn2_wi"][0]), "f2": up(a["ffn1_wi"][1]),
                "f3": up(a["ffn2_wi"][1]), "f4": up(a["w_gu1_2"]), "m2": [a["w_in_2"][MG], a["w_in_2"][DQ]], "f5": up(a["w_gu2_2"])}

        def on(s):
            if s not in st:
                return False
            nxt = [x for x in ALL[ALL.index(s) + 1:] if x in st and x not in ("n1", "n2")]
            self.next = list(plan.get(nxt[0], ())) if nxt else []
            return True

        if "f0" not in st:
            self.load_x()
            self.dve.wait(self.xt)
            for k in range(8):
                self.sums(k, T + TC if "m0" in st else T, self.xt)
        with self.scope() as sc:
            self.mod_ring(sc)
            if "f0" in st:
                self.mod_first()
                self.tiles0 = [self.split(self.load(s)) for s in plan["f0"]]
            else:
                self.barrier()
                for blk in range(3):
                    self.run_jobs(self.mod_jobs(blk, range(9)))
            more = (lambda b, *r: self.mod_jobs(b, r)) if "f0" in st else (lambda *bt: [])
            if on("f0"):
                self.ffn(0, XC, a["ffn1_wi"][0], a["ffn1_wo"][0], more(0, 3, 4, 5, 6, 7, 8), more(0, 2))
        if on("m0"):
            self.mixer_ab(1)
        if on("f1"):
            self.ffn(2, X, a["ffn2_wi"][0], a["ffn2_wo"][0], more(1, 0, 1, 2))
        if on("f2"):
            self.ffn(3, X, a["ffn1_wi"][1], a["ffn1_wo"][1], more(1, 3, 4, 5, 6, 7, 8))
        if on("m1"):
            self.mixer_pool(4)
        if on("f3"):
            self.ffn(5, X, a["ffn2_wi"][1], a["ffn2_wo"][1], more(2, 0, 1, 2))
        if on("n1"):
            self.final_norm("final_g")
        if on("f4"):
            self.ffn(6, X, a["w_gu1_2"], a["w_down1_2"], more(2, 3, 4, 5, 6, 7, 8))
        if on("m2"):
            self.mixer_hybrid(7)
        if on("f5"):
            self.ffn(8, X, a["w_gu2_2"], a["w_down2_2"], [])
        c = self.chan()
        if on("n2"):
            self.final_norm("g_final_2", c)
        else:
            self.barrier()
            self.sp.dma(a["out"], self.XT[:, :, 0:T], c, self.dve.tok())
        if "out_ctx" in a:
            self.sp.dma(a["out_ctx"], self.XT[:, :, T:T + TC], c)
        self.sp.wait(c.tok())

        block = self.ctx.enter_context(self.nc.Block())
        for name, q in (("sync", self.sp), ("tensor", self.pe), ("scalar", self.act), ("vector", self.dve),
                        ("gpsimd", self.pool)):
            if q.items:
                self.attach(block, name, q)

    def attach(self, block, name, q):
        on = {"sync": block.sync, "tensor": block.tensor, "scalar": block.scalar, "vector": block.vector,
              "gpsimd": block.gpsimd}[name]

        @on
        def _(eng):
            q.emit(eng)


ALL = ("f0", "m0", "f1", "f2", "m1", "f3", "n1", "f4", "m2", "f5", "n2")


def build(nc, a, stages=ALL):
    with ExitStack() as ctx:
        Program(nc, ctx, a, stages).program()



def cols(w):
    k, n = w.shape
    return np.ascontiguousarray(w.reshape(k // 128, 128, n // 128, 128).transpose(2, 1, 0, 3)).reshape(n // 128, 128, k)


def feat(v):
    return np.ascontiguousarray(v.reshape(-1, 128).T)


def constants():
    k = {}
    one = np.ones((128, 128), np.float32)
    idn = np.eye(128, dtype=np.float32)
    z = np.zeros((128, 12), np.float32)
    z[:, 5], z[:, 11] = 1.0, EPS
    k["sel6"] = np.ascontiguousarray(np.broadcast_to(np.eye(6, dtype=np.float32)[:, :, None], (6, 6, 128)))
    k["consts"] = np.concatenate([one, idn, z], axis=1)
    t = np.arange(T)
    cnt = []
    for w in (2, 4, 8, 16):
        lo, hi = np.maximum(t - w // 2, 0), np.minimum(t + (w - w // 2), T)
        cnt.append(1.0 / (hi - lo))
    k["pool_cnt"] = np.ascontiguousarray(np.broadcast_to(np.array(cnt, np.float32)[None], (128, 4, T)))
    i, j = np.arange(128)[:, None], np.arange(128)[None, :]
    left = np.where(j >= i, 0.0, -BIG)
    right = np.where(j <= i, 0.0, -BIG)
    y = np.arange(896)[None, :] - 384 - i
    near = [(np.abs(y) % d == 0) & (np.abs(y) // d <= 64) for d in (1, 4, 16)]
    count = near[0].astype(np.float32) + near[1] + near[2]
    add = np.where(count > 0, 0.0, -BIG)
    k["cb"] = np.concatenate([idn, left, right, add], axis=1).astype(np.float32)
    k["dil_count"] = np.ascontiguousarray(count.astype(np.float32))
    pos = np.arange(T)
    f = np.float32(10000.0) ** (-np.arange(16, dtype=np.float32) / np.float32(16))
    ang = [(pos // 64).astype(np.float32)[:, None] * f, (pos % 64).astype(np.float32)[:, None] * f]
    head = np.concatenate([np.concatenate([t_, t_], axis=1) for t_ in ang], axis=1).T
    ang = np.concatenate([head, head], axis=0)
    k["rope1"] = np.ascontiguousarray(np.stack([np.cos(ang), np.sin(ang)], axis=1).astype(np.float32))
    perm = np.zeros((128, 128), np.float32)
    for p in range(128):
        if p % 32 < 16:
            perm[p + 16, p] = -1.0
        else:
            perm[p - 16, p] = 1.0
    k["perm1"] = perm
    m = np.zeros((128, 2, 2, 64), np.int32)
    jj, ii = (np.arange(128) % 64)[:, None, None], np.arange(64)[None, None, :]
    m[:, 0] = jj <= ii
    m[:, 1] = jj >= ii
    k["gla_mask"] = m.reshape(128, 256)
    f = np.float32(500000.0) ** (-2.0 * np.arange(8, dtype=np.float32) / np.float32(16)).astype(np.float32)
    ang = pos.astype(np.float32)[:, None] * f
    c, s = np.ones((64, T), np.float32), np.zeros((64, T), np.float32)
    c[0:16], s[0:16] = np.tile(np.cos(ang).T, (2, 1)), np.tile(np.sin(ang).T, (2, 1))
    k["rope2"] = np.ascontiguousarray(np.stack([np.tile(c, (2, 1)), np.tile(s, (2, 1))], axis=1))
    perm = np.zeros((128, 256), np.float32)
    for p in range(128):
        if p % 64 < 8:
            perm[p + 8, p] = -1.0
        elif p % 64 < 16:
            perm[p - 8, p] = 1.0
        perm[64 * (p // 64):64 * (p // 64) + 64, 128 + p] = 1.0
    k["perm2"] = perm
    sel = np.zeros((4, 4, 128), np.float32)
    oh = np.zeros((128, 71), np.float32)
    oh[:, 35] = 1.0
    for h in range(4):
        sel[h, h] = 1.0
    k["sel"], k["onehot"] = sel, oh
    k["tri"] = np.ascontiguousarray(np.stack([np.where(i <= j, 0.0, BIG), np.where(i >= j, 0.0, BIG)], axis=1).astype(np.float32))
    return k


def arrange(i):
    f = {}
    vecs = []
    for name, n in VEC:
        v = np.asarray(i[name], np.float32)
        if name in ("g_q_2", "g_k_2"):
            v = np.tile(v.reshape(64, 1), (2, 1))
        elif name == "gate_bias_2":
            p = np.zeros((128, 4), np.float32)
            p[0:4] = v.reshape(4, 4).T
            v = p
        elif name == "sink":
            p = np.zeros((128, 1), np.float32)
            p[0:8, 0] = v.reshape(8)
            v = p
        else:
            v = feat(v.reshape(-1))
        assert v.shape == (128, n), name
        vecs.append(v)
    f["vecs"] = np.ascontiguousarray(np.concatenate(vecs, axis=1))
    tr = lambda x: np.ascontiguousarray(x[0].T.reshape(8, 128, -1).transpose(1, 0, 2))
    f["x_in"] = tr(i["x"])
    f["ctx_in"] = tr(i["ctx"])
    f["w_mod"] = i["w_mod"]
    f["w_ada_2"] = i["w_ada_2"][0]
    for n in ("ffn1_wi", "ffn2_wi"):
        f[n] = np.stack([cols(i[n][l]) for l in range(2)])
    for n in ("ffn1_wo", "ffn2_wo"):
        f[n] = i[n].reshape(2, NF, 128, D)
    f["w_gu1_2"] = cols(i["w_gu1_2"][0])
    f["w_gu2_2"] = cols(i["w_gu2_2"][0])
    f["w_down1_2"] = i["w_down1_2"].reshape(NF, 128, D)
    f["w_down2_2"] = i["w_down2_2"].reshape(NF, 128, D)
    f["pool_w"] = np.ascontiguousarray(i["w_pool"][0].reshape(4, 2, 128, 256).transpose(2, 0, 1, 3))
    w = i["w_in"][0]
    q = w[:, 0:512].reshape(D, 8, 64)
    q = np.stack([q[:, [j, j + 4]] for j in range(4)], axis=1).reshape(D, 512)
    f["w_in"] = cols(np.concatenate([q, w[:, 512:], np.zeros((D, 96), np.float32)], axis=1))
    wa = np.zeros((32, 2, 256), np.float32)
    wa[0:16, 0] = i["w_a2_f"][0]
    wa[16:32, 1] = i["w_a2_b"][0]
    f["wa2"] = wa
    w = i["w_out"][0]
    o = w[0:512].reshape(8, 64, D)
    o = np.stack([o[[j, j + 4]] for j in range(4)]).reshape(512, D)
    f["w_out"] = cols(np.concatenate([o, w[512:]]))
    w = i["w_in_2"][0]
    g = np.zeros((D, 4, 32), np.float32)
    g[:, :, 0:4] = w[:, 1536:1552].reshape(D, 4, 4)
    f["w_in_2"] = cols(np.concatenate([w[:, 0:1536], g.reshape(D, 128), w[:, 1552:]], axis=1))
    f["w_out_2"] = cols(i["w_out_2"][0])
    f.update(constants())
    return f


def kernel(**inputs):
    import concourse.bacc as bacc
    from concourse.bass_utils import run_bass_kernel_spmd

    inputs = {k: np.asarray(v) for k, v in inputs.items()}
    nc = bacc.Bacc("TRN2", target_bir_lowering=False, num_devices=1)
    arrays, a = {}, {}
    for name, v in arrange(inputs).items():
        arrays[f"in_{name}"] = v
        a[name] = nc.dram_tensor(f"in_{name}", v.shape, mybir.dt.from_np(v.dtype), kind="ExternalInput").ap()
    a["out"] = nc.dram_tensor("out_0", (128, 8, T), F32, kind="ExternalOutput").ap()
    build(nc, a)
    r = run_bass_kernel_spmd(nc, [arrays], core_ids=[0])
    o = np.asarray(r.results[0]["out_0"])
    return np.ascontiguousarray(o.transpose(2, 1, 0).reshape(1, T, D))
```
